# Optimizing a Trainium2 kernel written in Bass

```python
import jax, jax.numpy as jnp
from jax import lax
import numpy as np

D_MODEL = 1024
BATCH = 1
SEQ = 128
DEPTH = 1
DEC_BATCH = 1
DEC_SEQ = 1024
PAST_LEN = 128

GRID_W = 64
NH = 4
DK = 128
DV = 256
D_A = NH * DV
CHUNK = 64
POOL_WINDOWS = (2, 4, 8, 16)
POOL_GROUP = 128
D_POOL = POOL_GROUP * len(POOL_WINDOWS)
D_FF = 2816
CONV_W = 3
EPS = 1e-6
IN_SIZES = (NH * DK, NH * DK, D_A, D_A, 2 * NH, 2 * NH, D_POOL, D_MODEL, D_MODEL)
IN_COLS = int(sum(IN_SIZES))
IN_SPLIT_POINTS = [int(s) for s in np.cumsum(IN_SIZES)[:-1]]

kernel_name = 'bidir_mlstm_pool_hybrid_diffusion_step'

def _rmsnorm(x, g):
    xf = x.astype(jnp.float32)
    y = xf * lax.rsqrt(jnp.mean(xf * xf, axis=-1, keepdims=True) + EPS)
    return (y * g.astype(jnp.float32)).astype(x.dtype)

def _mlstm_chunked(q, k, v, log_i, log_f, C0, n0, m0):
    B, H, S, _ = q.shape
    nc = S // CHUNK
    qc = q.reshape(B, H, nc, CHUNK, DK)
    kc = k.reshape(B, H, nc, CHUNK, DK)
    vc = v.reshape(B, H, nc, CHUNK, DV)
    li = log_i.reshape(B, H, nc, CHUNK)
    b = jnp.cumsum(log_f.reshape(B, H, nc, CHUNK), axis=-1)
    b_last = b[..., -1]
    w = b_last[..., None] - b + li
    w_max = jnp.max(w, axis=-1)
    ew = jnp.exp(w - w_max[..., None])
    kv_chunk = jnp.einsum('bhcsk,bhcsv->bhckv', kc * ew[..., None], vc)
    n_chunk = jnp.einsum('bhcs,bhcsk->bhck', ew, kc)

    def step(carry, xs):
        C, n, m = carry
        kv_c, n_c, wmax_c, blast_c = xs
        m_new = jnp.maximum(m + blast_c, wmax_c)
        a = jnp.exp(m + blast_c - m_new)
        g = jnp.exp(wmax_c - m_new)
        C_new = a[..., None, None] * C + g[..., None, None] * kv_c
        n_new = a[..., None] * n + g[..., None] * n_c
        return (C_new, n_new, m_new), (C, n, m)

    xs = (jnp.moveaxis(kv_chunk, 2, 0), jnp.moveaxis(n_chunk, 2, 0),
          jnp.moveaxis(w_max, 2, 0), jnp.moveaxis(b_last, 2, 0))
    (Cf, nf, mf), (Cs, ns, ms) = lax.scan(step, (C0, n0, m0), xs)
    Cs = jnp.moveaxis(Cs, 0, 2)
    ns = jnp.moveaxis(ns, 0, 2)
    ms = jnp.moveaxis(ms, 0, 2)
    D = b[..., :, None] - b[..., None, :] + li[..., None, :]
    causal = np.tril(np.ones((CHUNK, CHUNK), dtype=bool))
    D = jnp.where(causal, D, -jnp.inf)
    inter = ms[..., None] + b
    m_t = jnp.maximum(inter, jnp.max(D, axis=-1))
    wts = jnp.exp(D - m_t[..., None])
    sc = jnp.exp(inter - m_t)
    qk = jnp.einsum('bhctk,bhcsk->bhcts', qc, kc) * wts
    num = jnp.einsum('bhcts,bhcsv->bhctv', qk, vc) + sc[..., None] * jnp.einsum('bhctk,bhckv->bhctv', qc, Cs)
    den = jnp.sum(qk, axis=-1) + sc * jnp.einsum('bhctk,bhck->bhct', qc, ns)
    h = num / jnp.maximum(jnp.abs(den), jnp.exp(-m_t))[..., None]
    return h.reshape(B, H, S, DV), (Cf, nf, mf)

def _pool_mixer(u, grid, w_pool, pool_scale):
    B, L, C = u.shape
    rows, cols = grid
    ur = u.astype(jnp.float32).reshape(B, rows, cols, C)
    cs = jnp.concatenate([jnp.zeros((B, rows, 1, C), jnp.float32), jnp.cumsum(ur, axis=2)], axis=2)
    t = np.arange(cols)
    outs = []
    for gi, win in enumerate(POOL_WINDOWS):
        lo = np.clip(t - win // 2, 0, cols)
        hi = np.clip(t + win // 2, 0, cols)
        cnt = (hi - lo).astype(np.float32)[:, None]
        sl = slice(gi * POOL_GROUP, (gi + 1) * POOL_GROUP)
        csg = cs[..., sl]
        mean = (jnp.take(csg, hi, axis=2) - jnp.take(csg, lo, axis=2)) / cnt
        d = mean - ur[..., sl]
        outs.append(jnp.einsum('brtc,cd->brtd', d, w_pool[gi].astype(jnp.float32)))
    y = jnp.concatenate(outs, axis=-1) * pool_scale.astype(jnp.float32)
    return y.reshape(B, L, C).astype(u.dtype)

def _dwconv_rows(h, w, bias, grid):
    B, L, C = h.shape
    rows, cols = grid
    hr = h.reshape(B, rows, cols, C)
    hp = jnp.pad(hr, ((0, 0), (0, 0), (1, 1), (0, 0)))
    out = hp[:, :, 0:cols] * w[0] + hp[:, :, 1:cols + 1] * w[1] + hp[:, :, 2:cols + 2] * w[2] + bias
    return out.reshape(B, L, C)

def _layer(x, cond, C0, n0, m0, grid, p):
    (w_ada, b_ada, g_pre_mix, g_post_mix, g_pre_ffn, g_post_ffn, w_in, b_gates, g_head,
     w_pool, pool_scale, w_br_a, w_br_b, w_out, w_up, conv_w, conv_b, w_down) = p
    B, L, _ = x.shape
    dt = x.dtype
    f32 = jnp.float32
    mod = jnp.dot(jax.nn.silu(cond), w_ada) + b_ada
    sh1, sc1, gt1, sh2, sc2, gt2 = [m[:, None, :] for m in jnp.split(mod, 6, axis=-1)]
    h = _rmsnorm(x, g_pre_mix) * (1 + sc1) + sh1
    z = jnp.einsum('bld,de->ble', h, w_in)
    q, k, v, o, ig, fg, u, ga, gb = jnp.split(z, IN_SPLIT_POINTS, axis=-1)
    qh = q.reshape(B, L, NH, DK).transpose(0, 2, 1, 3).astype(f32) * (DK ** -0.5)
    kh = k.reshape(B, L, NH, DK).transpose(0, 2, 1, 3).astype(f32)
    vh = v.reshape(B, L, NH, DV).transpose(0, 2, 1, 3).astype(f32)
    b_i, b_f = jnp.split(b_gates.astype(f32), 2)
    log_i = (ig.astype(f32) + b_i).reshape(B, L, 2, NH).transpose(2, 0, 3, 1)
    log_f = jax.nn.log_sigmoid(fg.astype(f32) + b_f).reshape(B, L, 2, NH).transpose(2, 0, 3, 1)
    h_f, (Cf, nf, mf) = _mlstm_chunked(qh, kh, vh, log_i[0], log_f[0], C0[:, 0], n0[:, 0], m0[:, 0])
    rev = lambda a: jnp.flip(a, axis=2)
    h_b, (Cb, nb, mb) = _mlstm_chunked(rev(qh), rev(kh), rev(vh), rev(log_i[1]), rev(log_f[1]),
                                       C0[:, 1], n0[:, 1], m0[:, 1])
    hm = h_f + rev(h_b)
    hm = hm * lax.rsqrt(jnp.mean(hm * hm, axis=-1, keepdims=True) + EPS) * g_head.astype(f32)[None, :, None, :]
    hm = hm.transpose(0, 2, 1, 3).reshape(B, L, D_A).astype(dt) * jax.nn.sigmoid(o)
    ya = jnp.einsum('blc,cd->bld', hm, w_br_a)
    yb = jnp.einsum('blc,cd->bld', _pool_mixer(u, grid, w_pool, pool_scale), w_br_b)
    y = jnp.einsum('bld,de->ble', jax.nn.sigmoid(ga) * ya + jax.nn.sigmoid(gb) * yb, w_out)
    x = x + gt1 * _rmsnorm(y, g_post_mix)
    h2 = _rmsnorm(x, g_pre_ffn) * (1 + sc2) + sh2
    up = _dwconv_rows(jnp.einsum('bld,df->blf', h2, w_up), conv_w, conv_b, grid)
    ug, uv = jnp.split(up, 2, axis=-1)
    f = jnp.einsum('blf,fd->bld', jax.nn.gelu(ug) * uv, w_down)
    x = x + gt2 * _rmsnorm(f, g_post_ffn)
    return x, (jnp.stack([Cf, Cb], axis=1), jnp.stack([nf, nb], axis=1), jnp.stack([mf, mb], axis=1))

def setup_inputs(seed: int = 0) -> dict:
    key = jax.random.key(seed)
    ks = jax.random.split(key, 32)
    nrm = lambda kk, shape, s: jax.random.normal(kk, shape, jnp.float32) * s
    gain = lambda kk, shape: 1.0 + 0.05 * jax.random.normal(kk, shape, jnp.float32)
    b_i = -1.0 + 0.1 * jax.random.normal(ks[10], (DEPTH, 2 * NH), jnp.float32)
    b_f = jnp.linspace(3.0, 6.0, 2 * NH, dtype=jnp.float32)[None, :] + 0.1 * jax.random.normal(ks[11], (DEPTH, 2 * NH), jnp.float32)
    return {
        'x_prompt': nrm(ks[0], (BATCH, SEQ, D_MODEL), 1.0),
        'x_sample': nrm(ks[1], (DEC_BATCH, DEC_SEQ, D_MODEL), 1.0),
        'state_C': nrm(ks[2], (DEC_BATCH, DEPTH, 2, NH, DK, DV), DK ** -0.5),
        'state_n': nrm(ks[3], (DEC_BATCH, DEPTH, 2, NH, DK), DK ** -0.5),
        'state_m': nrm(ks[4], (DEC_BATCH, DEPTH, 2, NH), 0.5),
        'c': nrm(ks[5], (DEC_BATCH, D_MODEL), 1.0),
        'c_ctx': nrm(ks[6], (D_MODEL,), 1.0),
        'w_ada': nrm(ks[7], (DEPTH, D_MODEL, 6 * D_MODEL), 0.5 * D_MODEL ** -0.5),
        'b_ada': nrm(ks[8], (DEPTH, 6 * D_MODEL), 0.02),
        'g_pre_mix': gain(ks[9], (DEPTH, D_MODEL)),
        'g_post_mix': gain(ks[12], (DEPTH, D_MODEL)),
        'g_pre_ffn': gain(ks[13], (DEPTH, D_MODEL)),
        'g_post_ffn': gain(ks[14], (DEPTH, D_MODEL)),
        'w_in': nrm(ks[15], (DEPTH, D_MODEL, IN_COLS), D_MODEL ** -0.5),
        'b_gates': jnp.concatenate([b_i, b_f], axis=-1),
        'g_head': gain(ks[16], (DEPTH, NH, DV)),
        'w_pool': nrm(ks[17], (DEPTH, len(POOL_WINDOWS), POOL_GROUP, POOL_GROUP), POOL_GROUP ** -0.5),
        'pool_scale': 1.0 + 0.1 * jax.random.normal(ks[18], (DEPTH, D_POOL), jnp.float32),
        'w_br_a': nrm(ks[19], (DEPTH, D_A, D_MODEL), D_A ** -0.5),
        'w_br_b': nrm(ks[20], (DEPTH, D_POOL, D_MODEL), D_POOL ** -0.5),
        'w_out': nrm(ks[21], (DEPTH, D_MODEL, D_MODEL), D_MODEL ** -0.5),
        'w_up': nrm(ks[22], (DEPTH, D_MODEL, 2 * D_FF), D_MODEL ** -0.5),
        'conv_w': nrm(ks[23], (DEPTH, CONV_W, 2 * D_FF), CONV_W ** -0.5),
        'conv_b': nrm(ks[24], (DEPTH, 2 * D_FF), 0.02),
        'w_down': nrm(ks[25], (DEPTH, D_FF, D_MODEL), D_FF ** -0.5),
    }

def reference(x_prompt, x_sample, state_C, state_n, state_m, c, c_ctx, w_ada, b_ada,
              g_pre_mix, g_post_mix, g_pre_ffn, g_post_ffn, w_in, b_gates, g_head,
              w_pool, pool_scale, w_br_a, w_br_b, w_out, w_up, conv_w, conv_b, w_down):
    Bp, Lp, _ = x_prompt.shape
    Bs, Ls, _ = x_sample.shape
    rows = Ls // GRID_W
    f32 = jnp.float32
    cond_ctx = jnp.broadcast_to(c_ctx[None, :], (Bp, D_MODEL))
    zC = jnp.zeros((Bp, 2, NH, DK, DV), f32)
    zn = jnp.zeros((Bp, 2, NH, DK), f32)
    zm = jnp.zeros((Bp, 2, NH), f32)
    y_p = x_prompt
    y_s = x_sample
    new_C, new_n, new_m = [], [], []
    for l in range(DEPTH):
        p = (w_ada[l], b_ada[l], g_pre_mix[l], g_post_mix[l], g_pre_ffn[l], g_post_ffn[l], w_in[l],
             b_gates[l], g_head[l], w_pool[l], pool_scale[l], w_br_a[l], w_br_b[l], w_out[l],
             w_up[l], conv_w[l], conv_b[l], w_down[l])
        y_p, (Cl, nl, ml) = _layer(y_p, cond_ctx, zC, zn, zm, (1, Lp), p)
        new_C.append(Cl)
        new_n.append(nl)
        new_m.append(ml)
        y_s, _ = _layer(y_s, c, state_C[:, l].astype(f32), state_n[:, l].astype(f32),
                        state_m[:, l].astype(f32), (rows, GRID_W), p)
    new_state_C = jnp.stack(new_C, axis=1).astype(state_C.dtype)
    new_state_n = jnp.stack(new_n, axis=1).astype(state_n.dtype)
    new_state_m = jnp.stack(new_m, axis=1).astype(state_m.dtype)
    return (y_p, y_s, new_state_C, new_state_n, new_state_m)


_drawn_inputs = setup_inputs


def setup_inputs(seed=0):
    import zlib

    import numpy as np

    out = dict(_drawn_inputs(seed))
    spreads = {}
    factors = {'state_C': 8.0,
     'state_n': 8.0,
     'state_m': 8.0,
     'g_post_mix': 3.6,
     'g_pre_ffn': 2.813,
     'g_post_ffn': 3.944,
     'g_head': 6.949,
     'conv_b': 7.567,
     'pool_scale': 2.842}
    for name, (base, spread) in spreads.items():
        noise = np.random.default_rng([zlib.crc32(name.encode()), seed]).standard_normal(out[name].shape)
        drawn = base * np.exp(spread * noise) if base else spread * noise
        out[name] = __import__('jax').numpy.asarray(drawn.astype(out[name].dtype))
    for name, factor in factors.items():
        out[name] = (out[name] * factor).astype(out[name].dtype)
    return out
```

```python
import numpy as np

import concourse.bass as bass
from concourse import mybir

F32 = mybir.dt.float32
F32R = mybir.dt.float32r
BF16 = mybir.dt.bfloat16
ALU = mybir.AluOpType
ACT = mybir.ActivationFunctionType

P = 128
DM = 1024
KD = DM // P
CTX = 128
LAT = 1024
T = CTX + LAT
NT = T // P
NB = 3
BW = T // NB
TB = BW // P
NH = 4
DK = 128
DV = 256
VW = DV + 1
DFF = 2816
NF = DFF // P
NC = NF // 2
ROW = 64
WINDOWS = (2, 4, 8, 16)
EPS = 1e-6
QSCALE = DK ** -0.5
NEG = -1e30

CQ, CK, CV, CO = 0, 512, 1024, 2048
CG, CU, CGA, CGB = 3072, 3088, 3600, 4624
GR = 36

V_BADA, V_GPM, V_GQM, V_GPF, V_GQF, V_GH, V_PS, V_C = 0, 48, 56, 64, 72, 80, 88, 92
V_W0, V_W1, V_W2, V_CB = 108, 152, 196, 240
NV = 284

H_ID, H_SEL, H_MASK, H_POOL = 0, 128, 128 + 8 * 128, 128 + 10 * 128
H_COLS = H_POOL + 8 * 128


def shape_constants():
    out = np.zeros((P, H_COLS), np.float32)
    out[:, H_ID:H_ID + P] = np.eye(P)
    for d in range(2):
        for h in range(NH):
            r = 32 * d + h
            for row in (r, 64 + r):
                out[row, H_SEL + (d * NH + h) * P:H_SEL + (d * NH + h + 1) * P] = 1.0
    s, t = np.arange(P)[:, None], np.arange(P)[None, :]
    out[:, H_MASK:H_MASK + P] = np.where(s <= t, 0.0, NEG)
    out[:, H_MASK + P:H_MASK + 2 * P] = np.where(s >= t, 0.0, NEG)
    for g, win in enumerate(WINDOWS):
        for kind, cols in enumerate((CTX, ROW)):
            m = np.zeros((P, P), np.float32)
            for tok in range(P):
                row, c = tok // cols, tok % cols
                lo, hi = max(c - win // 2, 0), min(c + win // 2, cols)
                m[row * cols + lo:row * cols + hi, tok] = np.float32(1.0) / np.float32(hi - lo)
                m[tok, tok] -= 1.0
            at = H_POOL + (2 * g + kind) * P
            out[:, at:at + P] = m
    return out


def plan():
    rest = [("o", j) for j in range(8)] + [("ga", j) for j in range(8)] + [("gb", j) for j in range(8)]
    mains = [("gates", 0)] + [("u", g) for g in range(4)]
    mains += [("v", 0), ("v", 1), ("q", 0), ("k", 0)]
    seg_start = len(mains)
    for h in range(NH):
        seg = []
        if h + 1 < NH:
            seg += [("v", 2 * h + 2), ("v", 2 * h + 3), ("q", h + 1), ("k", h + 1)]
            seg += rest[:5]
            rest = rest[5:]
        else:
            seg += rest
        mains += seg
    return mains, seg_start


def build(nc, x_prompt, x_sample, state_C, state_n, state_m, c, c_ctx, w_ada, b_ada, g_pre_mix, g_post_mix,
          g_pre_ffn, g_post_ffn, w_in, b_gates, g_head, w_pool, pool_scale, w_br_a, w_br_b, w_out, w_up,
          conv_w, conv_b, w_down, consts, y_prompt, y_sample, new_C, new_n, new_m):
    mains, SEG = plan()
    NM = len(mains)
    RS = 3
    ADA0 = 16

    S_BR = NM
    S_OUT = S_BR + 16
    S_FF = S_OUT + 8
    n_units = S_FF + 4 + 6 * (NC - 1) + 2
    raw_items = [("ada", a) for a in range(ADA0)]
    for s in range(1, NM):
        raw_items.append(("unit", s))
        if s <= 48 - ADA0:
            raw_items.append(("ada", ADA0 + s - 1))
    for s in range(S_BR, S_FF):
        raw_items.append(("unit", s))
    raw_of = {it: n for n, it in enumerate(raw_items)}
    N_FF = len(raw_items)

    def raw_n(s):
        return raw_of[("unit", s)] if s < S_FF else N_FF + s - S_FF

    uses = ["norm"] * 8
    use_of = {}
    for m, (kind, idx) in enumerate(mains):
        if m >= SEG and (m - SEG) % 9 == 1 and m - SEG > 9:
            h = (m - SEG) // 9 - 1
            for j in range(2):
                use_of[("hm", 2 * h + j)] = len(uses)
                uses.append("hm")
        use_of[("main", m)] = len(uses)
        uses.append(kind)
        if kind == "u":
            for st in range(2):
                use_of[("pool", idx, st)] = len(uses)
                uses.append("pool")
        if m and mains[m - 1][0] == "v":
            use_of[("turn", mains[m - 1][1])] = len(uses)
            uses.append("turn")
    for j in range(2):
        use_of[("hm", 2 * (NH - 1) + j)] = len(uses)
        uses.append("hm")
    Q_P1 = 3 * len(uses)
    U_YA = len(uses)
    U_OUT = U_YA + 8
    Q_N2 = 3 * (U_OUT + 8)
    Q_FF = Q_N2 + 24

    def unit_done_q(s):
        if s < NM:
            return 3 * use_of[("main", s)] + 3
        if s < S_OUT:
            return None
        return 3 * (U_OUT + s - S_OUT) + 3

    base = [(nc.sbuf_base + 63) // 64 * 64]

    def place(name, shape, dt=F32, at=None):
        size = int(np.prod(shape[1:])) * (2 if dt == BF16 else 4)
        off = base[0] if at is None else at
        if at is None:
            base[0] += (size + 31) // 32 * 32
        return nc.alloc_sbuf_tensor_at(name, shape, dt, offset=off)

    ident = place("ident", [P, P])
    vT = place("vT", [P, NV])
    modT = place("modT", [P, 48, 2])
    condT = place("condT", [P, 2, KD])
    coefA1 = place("coefA1", [P, KD, 2])
    coefA2 = place("coefA2", [P, KD, 2])
    coefG1 = place("coefG1", [P, KD, 2])
    coefG2 = place("coefG2", [P, KD, 2])
    stat = place("stat", [P, 4, NT])
    hstat = place("hstat", [P, 2, NT])
    taps = place("taps", [P, 2, 6])
    dsm = place("dsm", [P, 8])
    H_hi = place("H_hi", [P, KD, T], F32R)
    H_lo = place("H_lo", [P, KD, T], F32R)
    ring_hi = place("ring_hi", [P, RS, 1024], F32R)
    ring_lo = place("ring_lo", [P, RS, 1024], F32R)
    raw = place("raw", [P, RS, 1024])
    R = base[0]
    QKVW = T + T + NT * VW
    qT = [place(f"qT{i}", [P, T]) for i in range(2)]
    kT = [place(f"kT{i}", [P, T]) for i in range(2)]
    vaug = [place(f"vaug{i}", [P, NT, VW]) for i in range(2)]
    stage = [place(f"stage{i}", [P, T]) for i in range(2)]
    SC0 = base[0]
    sc = [place(f"sc{i}", [P, T]) for i in range(2)]
    HM0 = base[0]
    hm = [place(f"hm{i}", [P, NT, DV]) for i in range(2)]
    GS = place("GS", [P, T], F32R)
    YS = place("YS", [P, T], F32R)
    a_tok = place("a_tok", [P, NT, 2, NH])
    en_tok = place("en_tok", [P, NT, 2, NH])
    Cst = place("Cst", [P, 2, VW])
    Cctx = place("Cctx", [P, 2, VW])
    AT0 = base[0]
    Wt = place("Wt", [P, 2, P])
    Et = place("Et", [P, 2, P])
    Pt = place("Pt", [P, 2, P])
    kw = place("kw", [P, 2, P])
    qs = place("qs", [P, 2, P])
    sel = place("sel", [P, 8, P], F32R)
    idbf = place("idbf", [P, P], BF16)
    maskbf = place("maskbf", [P, 2, P], BF16)
    assert base[0] <= nc.sbuf_usable_end, (base[0], nc.sbuf_usable_end)
    X0 = place("X0", [P, NT, DM], at=R)
    Gt = place("Gt", [P, 8, T], at=R)
    vecs = place("vecs", [P, 3, P], at=AT0)
    tsc = place("tsc", [P, 2, BW], at=SC0)
    reset = place("reset", [P, T], at=HM0)
    wgate = place("wgate", [P, KD, 16], at=HM0 + 4 * T)
    gbias = place("gbias", [P, 2], at=HM0 + 4 * T + 512)
    m0t = place("m0t", [P, 1], at=HM0 + 4 * T + 544)
    mprev = place("mprev", [P, NT], at=HM0 + 4 * T + 576)
    poolM = place("poolM", [P, 8, P], at=HM0 + 9216)
    wpool = place("wpool", [P, 4, P], at=HM0 + 9216 + 4096)
    pT_hi = place("pT_hi", [P, 4, T], F32R, at=R)
    pT_lo = place("pT_lo", [P, 4, T], F32R, at=R + 16 * T)
    mixF = place("mixF", [P, KD, T], at=R + 32 * T)
    ld = place("ld", [P, 4, T], at=R + 64 * T)
    yT = place("yT", [P, KD, T], at=R)
    X1 = place("X1", [P, NT, DM], at=R + 32 * T)
    gtb1 = place("gtb1", [P, 2, DM], at=R + 64 * T)
    xld = place("xld", [P, 2, DM], at=R + 64 * T + 8192)
    tsc2 = place("tsc2", [P, 2, BW], at=R + 80 * T)
    acc = place("acc", [P, NT, DM], at=R)
    fT_hi = place("fT_hi", [P, 2, 2, T], F32R, at=R + 32 * T)
    fT_lo = place("fT_lo", [P, 2, 2, T], F32R, at=R + 48 * T)
    cg = place("cg", [P, T], at=R + 64 * T)
    cv = place("cv", [P, T], at=R + 68 * T)
    x1ld = place("x1ld", [P, 2, DM], at=R + 64 * T)
    gtb2 = place("gtb2", [P, 2, DM], at=R + 72 * T)
    assert R + 72 * T + 8192 <= nc.sbuf_usable_end

    ps = nc.alloc_psum_tensor("ps", [P, 8, 512], F32)

    Z = {k: nc.dram_tensor("z_" + k, (n, P, T), F32, kind="Internal").ap()
         for k, n in (("o", 8), ("ga", 8), ("gb", 8), ("hm", 8), ("pool", 4))}
    x1_dram = nc.dram_tensor("z_x1", (NT, P, DM), F32, kind="Internal").ap()

    S = lambda name: nc.alloc_semaphore(name)
    s_cst, s_vec, s_x, s_wg, s_st0 = S("s_cst"), S("s_vec"), S("s_x"), S("s_wg"), S("s_st0")
    landed = [S(f"landed{i}") for i in range(RS)]
    hi_ready, lo_ready, ada_used = S("hi_ready"), S("lo_ready"), S("ada_used")
    done0, evac0 = S("done0"), S("evac0")
    done1, evac1 = S("done1"), S("evac1")
    done2, evac2 = S("done2"), S("evac2")
    act_seq, dve_seq, pool_seq = S("act_seq"), S("dve_seq"), S("pool_seq")
    vec_done, cond_done, ada0_done, coef1 = S("vec_done"), S("cond_done"), S("ada0_done"), S("coef1")
    ss_done, rt_done, x_scaled = S("ss_done"), S("rt_done"), S("x_scaled")
    t_done, tl_done = S("t_done"), S("tl_done")
    g_lf, g_ready, g_pe, g_tok = S("g_lf"), S("g_ready"), S("g_pe"), S("g_tok")
    ones_done = S("ones_done")
    attB = S("attB")
    attA, attX, attP, attN, attC = S("attA"), S("attX"), S("attP"), S("attN"), S("attC")
    c_in, c_out = S("c_in"), S("c_out")
    hss, hrt, hscaled = S("hss"), S("hrt"), S("hscaled")
    stored = [S("stored0"), S("stored1")]
    ld_in = [S(f"ld_in{i}") for i in range(4)]
    ld_used = S("ld_used")
    sgm, hmx, hmhi = S("sgm"), S("hmx"), S("hmhi")
    mixed, mixhi, mix_ready = S("mixed"), S("mixhi"), S("mix_ready")
    coef2, gtb_pe, gtb_done = S("coef2"), S("gtb_pe"), S("gtb_done")
    x_in = [S("x_in0"), S("x_in1")]
    x1_ready, x1_stored = S("x1_ready"), [S("x1s0"), S("x1s1")]
    ss2, rt2, vv2 = S("ss2"), S("rt2"), S("vv2")
    acc_zero = S("acc_zero")
    conv_a, conv_g, gel, conv_v, fhi, f_ready = S("conv_a"), S("conv_g"), S("gel"), S("conv_v"), S("fhi"), S("f_ready")
    dve_ff, fin_ss, fin_rt, fin_o = S("dve_ff"), S("fin_ss"), S("fin_rt"), S("fin_o")
    x1_in = [S("x1_in0"), S("x1_in1")]
    s_out = S("s_out")
    taps_done = S("taps_done")
    s_outn = [S("s_outA"), S("s_outB")]

    def tile_cols(w, kt, c0):
        return w.rearrange("(k p) c -> p k c", p=P)[:, 0:kt, c0:c0 + P]

    cols_of = {"q": CQ, "k": CK, "v": CV, "o": CO, "u": CU, "ga": CGA, "gb": CGB}

    def unit_source(s):
        if s < NM:
            kind, idx = mains[s]
            return tile_cols(w_in[0], KD, cols_of[kind] + idx * P), KD
        if s < S_OUT:
            d = (s - S_BR) // 2
            return (tile_cols(w_br_b[0], 4, d * P), 4) if (s - S_BR) % 2 == 0 else (tile_cols(w_br_a[0], KD, d * P), KD)
        return tile_cols(w_out[0], KD, (s - S_OUT) * P), KD

    def unit_width(s):
        return 512 if S_BR <= s < S_OUT and (s - S_BR) % 2 == 0 else 1024

    w_up_t = w_up[0].rearrange("(k p) f -> p k f", p=P)

    def lin(at, step, i):
        return at if i is None else i * step + at

    def row_parts(b):
        return [(0, 1, CTX), (CTX, (BW - CTX) // ROW, ROW)] if b == 0 else [(0, BW // ROW, ROW)]

    def put_out(eng, t):
        eng.wait_ge(fin_o, t + 1)
        dst = y_prompt[0] if t == 0 else y_sample[0, (t - 1) * P:t * P, :]
        eng.dma_start(dst, acc[:, t, :]).then_inc(s_outn[t % 2], 16)

    def stage_order():
        out = []
        for m, (kind, idx) in enumerate(mains):
            if m >= SEG and (m - SEG) % 9 == 1 and m - SEG > 9:
                h = (m - SEG) // 9 - 1
                out += [("hm", 2 * h), ("hm", 2 * h + 1)]
            if kind in ("o", "ga", "gb"):
                out.append((kind, idx))
            if kind == "u":
                out.append(("pool", idx))
        return out + [("hm", 2 * NH - 2), ("hm", 2 * NH - 1)]

    stage_no = {it: w for w, it in enumerate(stage_order())}

    def n_stage():
        return len(stage_no)

    NORM_AFTER = (4, 7, 8)

    def gate_rows(pe, coef, g0):
        pe.wait_ge(coef2, 1)
        for cond in range(2):
            if g0 + cond:
                pe.wait_ge(gtb_done, g0 + cond)
            for k in range(KD):
                mm = pe.matmul(ps[:, 6 + k // 4, (k % 4) * P:(k % 4 + 1) * P],
                               coef[:, k, cond:cond + 1].to_broadcast([P, P]), ident[:, :], start=True, stop=True)
            mm.then_inc(gtb_pe, 1)

    def vcol(col, i):
        return vT[:, col:col + 1] if i is None else vT[:, bass.ds(i * 4 + col, 1)]

    def evac_q(act, q0, dst, scale, exps, done, evac, ps_):
        for b in range(NB):
            act.wait_ge(done, q0 + b + 1)
            kw_ = {} if scale is None else {"scale": scale}
            act.activation(dst[:, b * BW:(b + 1) * BW], ps_[:, b, 0:BW], ACT.Copy, **kw_).then_inc(evac, 1)
            if b == 0:
                exps()

    def free_slot(eng, s):
        p = s - RS
        if p < 0:
            return
        if p < S_BR or p >= S_OUT:
            eng.wait_ge(done0, unit_done_q(p))
        elif (p - S_BR) % 2 == 0:
            eng.wait_ge(done1, 3 * ((p - S_BR) // 2 + 1))
        else:
            eng.wait_ge(done0, 3 * (U_YA + (p - S_BR) // 2 + 1))

    with nc.Block() as block:
        @block.sync
        def _(sp):
            sp.dma_start(ident[:, :], consts[:, H_ID:H_ID + P]).then_inc(s_cst, 16)
            sp.dma_start(stage[1][:, 0:8 * P], consts[:, H_SEL:H_SEL + 8 * P]).then_inc(s_cst, 16)
            sp.dma_start(sc[1][:, 0:2 * P], consts[:, H_MASK:H_MASK + 2 * P]).then_inc(s_cst, 16)
            vecA = [b_ada[0], g_pre_mix[0], g_post_mix[0], g_pre_ffn[0], g_post_ffn[0],
                    g_head[0].rearrange("h v -> (h v)"), pool_scale[0], c_ctx, c[0]]
            at = 0
            for v in vecA:
                n = v.shape[0] // P
                sp.dma_start(vecs[at:at + n, 0, :], v.rearrange("(r p) -> r p", p=P)).then_inc(s_vec, 16)
                at += n
            for j, o, v in ((1, 0, conv_w[0, 0]), (1, 44, conv_w[0, 1]), (2, 0, conv_w[0, 2]), (2, 44, conv_b[0])):
                sp.dma_start(vecs[o:o + 44, j, :], v.rearrange("(r p) -> r p", p=P)).then_inc(s_vec, 16)
            sp.dma_start(X0[:, 0, :], x_prompt[0]).then_inc(s_x, 16)
            sp.dma_start(X0[:, 1:NT, :], x_sample[0].rearrange("(t p) d -> p t d", p=P)).then_inc(s_x, 16)

            for n, it in enumerate(raw_items):
                if n >= RS:
                    prev = raw_items[n - RS]
                    if prev[0] == "ada":
                        sp.wait_ge(ada_used, prev[1] + 1)
                    else:
                        sp.wait_ge(lo_ready, prev[1] + 1)
                if it[0] == "ada":
                    src, kt = tile_cols(w_ada[0], KD, it[1] * P), KD
                else:
                    src, kt = unit_source(it[1])
                sp.dma_start(raw[:, n % RS, 0:kt * P].rearrange("p (k c) -> p k c", c=P), src)\
                  .then_inc(landed[n % RS], 16)

            def ff_load(j, i, src, by_tile):
                n0 = N_FF + j
                sp.wait_ge(lo_ready, lin(S_FF + j - RS + 1, 12, i))
                dst = raw[:, n0 % RS, :]
                if by_tile:
                    dst = dst.rearrange("p (k c) -> p k c", c=P)
                sp.dma_start(dst, src).then_inc(landed[n0 % RS], 16)

            def up_src(f, i, half):
                if i is None:
                    return w_up_t[:, :, f * P + half * DFF:(f + 1) * P + half * DFF]
                return w_up_t[:, :, bass.ds(i * (4 * P) + (f * P + half * DFF), P)]

            def down_src(f, i):
                if i is None:
                    return w_down[0][f * P:(f + 1) * P, :]
                return w_down[0][bass.ds(i * (4 * P) + f * P, P), :]

            for j in range(4):
                ff_load(j, None, up_src(j // 2, None, j % 2), True)
            with sp.Fori(0, (NC - 1) // 2) as i:
                for cc in range(2):
                    for j in range(4):
                        ff_load(4 + 6 * cc + j, i, up_src(2 + 2 * cc + j // 2, i, j % 2), True)
                    for j in range(2):
                        ff_load(8 + 6 * cc + j, i, down_src(2 * cc + j, i), False)
            for j in range(2):
                ff_load(4 + 6 * (NC - 1) + j, None, down_src(NF - 2 + j, None), False)
            for d in range(2):
                sp.wait_ge(s_outn[d], 16 * ((NT + 1 - d) // 2))
            sp.wait_ge(c_out, 16 * 4 * NH)
            sp.wait_ge(s_out, 32)

        @block.gpsimd
        def _(pool):
            rr = reset[:, :].rearrange("p (t s) -> p t s", s=P)
            fills = ((reset[:, :], 1.0), (rr[0:4, :, 0:1], 0.0), (rr[32:36, :, P - 1:P], 0.0), (gbias[:, :], 0.0),
                     (m0t[:, :], 0.0), (mprev[:, :], 0.0))
            for n, (out, value) in enumerate(fills):
                pool.memset(out, value).then_inc(pool_seq, 1)
                pool.wait_ge(pool_seq, n + 1)
            bg = b_gates[0].rearrange("(r c) -> r c", c=1)
            for d in range(2):
                pool.dma_start(gbias[32 * d:32 * d + 4, 0:1], bg[4 * d:4 * d + 4, :]).then_inc(s_wg, 16)
                pool.dma_start(gbias[32 * d:32 * d + 4, 1:2], bg[8 + 4 * d:12 + 4 * d, :]).then_inc(s_wg, 16)
                pool.dma_start(m0t[32 * d:32 * d + 4, :], state_m[0, 0, d].rearrange("(r c) -> r c", c=1)).then_inc(s_wg, 16)
            pool.dma_start(wgate[:, :, :], w_in[0].rearrange("(k p) c -> p k c", p=P)[:, :, CG:CG + 16]).then_inc(s_wg, 16)
            pool.dma_start(poolM[:, :, :], consts[:, H_POOL:H_POOL + 8 * P].rearrange("p (m c) -> p m c", c=P)).then_inc(s_wg, 16)
            pool.dma_start(wpool[:, :, :], w_pool[0].rearrange("g c d -> c g d")).then_inc(s_wg, 16)
            pool.wait_ge(g_ready, 1)
            nm = new_m[0, 0]
            pool.dma_start(nm[0].rearrange("(r c) -> r c", c=1), Gt[0:4, 4, CTX - 1:CTX]).then_inc(s_out, 16)
            pool.dma_start(nm[1].rearrange("(r c) -> r c", c=1), Gt[32:36, 4, 0:1]).then_inc(s_out, 16)
            for h in range(NH):
                if h:
                    pool.wait_ge(attN, 18 * h)
                for d in range(2):
                    pool.dma_start(Cst[:, d, 0:DV], state_C[0, 0, d, h]).then_inc(c_in, 16)
                    pool.dma_start(Cst[:, d, DV:VW], state_n[0, 0, d, h].rearrange("(r c) -> r c", c=1)).then_inc(c_in, 16)
                pool.wait_ge(attC, 18 * h + 2)
                for d in range(2):
                    pool.dma_start(new_C[0, 0, d, h], Cctx[:, d, 0:DV]).then_inc(c_out, 16)
                    pool.dma_start(new_n[0, 0, d, h].rearrange("(r c) -> r c", c=1), Cctx[:, d, DV:VW]).then_inc(c_out, 16)

            pool.wait_ge(evac0, Q_P1)
            pool.wait_ge(c_out, 16 * 4 * NH)
            pool.wait_ge(s_out, 32)
            n_st = n_stage()
            for i in range(2):
                pool.wait_ge(stored[i], 16 * ((n_st + 1 - i) // 2))
            loads = [Z["pool"][g] for g in range(4)]
            for k in range(KD):
                loads += [Z["hm"][k], Z["o"][k]]
            for d in range(KD):
                loads += [Z["gb"][d], Z["ga"][d]]
            for w, src in enumerate(loads):
                if w >= 4:
                    pool.wait_ge(ld_used, w - 3)
                pool.dma_start(ld[:, w % 4, :], src).then_inc(ld_in[w % 4], 16)
            pool.wait_ge(ld_used, 36)
            for t in range(NT):
                if t >= 2:
                    pool.wait_ge(ss2, 2 * (t - 2) + 2)
                src = x_prompt[0] if t == 0 else x_sample[0, (t - 1) * P:t * P, :]
                pool.dma_start(xld[:, t % 2, :], src).then_inc(x_in[t % 2], 16)
                if t >= 1:
                    pool.wait_ge(x1_ready, t)
                    pool.dma_start(x1_dram[t - 1], X1[:, t - 1, :]).then_inc(x1_stored[(t - 1) % 2], 16)
            pool.wait_ge(x1_ready, NT)
            pool.dma_start(x1_dram[NT - 1], X1[:, NT - 1, :]).then_inc(x1_stored[(NT - 1) % 2], 16)
            pool.wait_ge(done2, NT)
            pool.memset(acc[:, :, :], 0.0).then_inc(acc_zero, 1)
            pool.wait_ge(f_ready, 3 * NF)
            for t in range(NT):
                if t >= 2:
                    pool.wait_ge(fin_o, t - 1)
                pool.dma_start(x1ld[:, t % 2, :], x1_dram[t]).then_inc(x1_in[t % 2], 16)
                if t >= 1:
                    put_out(pool, t - 1)
            put_out(pool, NT - 1)

        @block.tensor
        def _(pe):
            def take0(q):
                if q >= 3:
                    pe.wait_ge(evac0, q - 2)

            def mm3(out, whi, wlo, xhi, xlo, first, last):
                pe.matmul(out, whi, xhi, start=first, stop=False)
                pe.matmul(out, whi, xlo, start=False, stop=False)
                return pe.matmul(out, wlo, xhi, start=False, stop=last)

            def block_product(out, s, b, kt, xhi, xlo, pieces=None):
                r = s % RS
                for k in range(kt):
                    w = slice(k * P, (k + 1) * P)
                    tok = slice(b * BW, (b + 1) * BW)
                    mm = mm3(out, ring_hi[:, r, w], ring_lo[:, r, w], xhi[:, k, tok], xlo[:, k, tok], k == 0, k == kt - 1)
                return mm

            pe.wait_ge(s_cst, 48)
            pe.wait_ge(s_vec, 16 * 13)
            pe.transpose(ps[:, 3, 0:108], vecs[0:108, 0, :], ident[0:108, 0:108])
            pe.transpose(ps[:, 3, 108:196], vecs[0:88, 1, :], ident[0:88, 0:88])
            pe.transpose(ps[:, 3, 196:284], vecs[0:88, 2, :], ident[0:88, 0:88]).then_inc(vec_done, 1)

            def ada_tile(a, bank, col):
                n = raw_of[("ada", a)]
                pe.wait_ge(landed[n % RS], 16 * (n // RS + 1))
                for k in range(KD):
                    mm = pe.matmul(ps[:, bank, col:col + 2], raw[:, n % RS, k * P:(k + 1) * P], condT[:, :, k],
                                   start=(k == 0), stop=(k == KD - 1))
                mm.then_inc(ada_used, 1)

            def norm_block(Xt, q0, b, ready):
                if True:
                    pe.wait_ge(x_scaled, ready)
                    for k in range(KD):
                        q = q0 + b * KD + k
                        take0(q)
                        for j in range(TB):
                            mm = pe.transpose(ps[:, q % 3, j * P:(j + 1) * P],
                                              Xt[:, b * TB + j, k * P:(k + 1) * P], ident[:, :])
                        mm.then_inc(done0, 1)

            pe.wait_ge(cond_done, 1)
            for a in range(ADA0):
                ada_tile(a, 7, 2 * a)
            for b in range(NB):
                norm_block(X0, 0, b, TB * (b + 1))

            def attention_scores(h, i):
                e = h * 9 + i
                cf, cb = (0, 0) if i == 0 else (i, NT - i)
                v = h % 2
                if i == 0:
                    mk = mains.index(("k", h))
                    pe.wait_ge(evac0, 3 * use_of[("main", mk)] + 3)
                    if h == 0:
                        pe.wait_ge(g_tok, 1)
                if e:
                    pe.wait_ge(attP, e)
                for d, cx in ((0, cf), (1, cb)):
                    tok = slice(cx * P, (cx + 1) * P)
                    j = d * NH + h
                    o = d * P
                    pe.matmul(ps[:, 3, o:o + P], idbf[:, :], maskbf[:, d, :], start=True, stop=False)
                    pe.matmul(ps[:, 3, o:o + P], sel[:, j, :], GS[:, tok], start=False, stop=True)
                    pe.matmul(ps[:, 3, 256 + o:256 + o + P], sel[:, j, :], YS[:, tok], start=True, stop=True)
                    pe.matmul(ps[:, 4, o:o + P], kT[v][:, tok], qT[v][:, tok], start=True, stop=True)
                    mm = pe.transpose(ps[:, 4, 256 + o:256 + o + P], kT[v][:, tok], ident[:, :])
                mm.then_inc(attA, 1)

            def attention_values(h, i, d):
                e = h * 9 + i
                cx = 0 if i == 0 else (i, NT - i)[d]
                v = h % 2
                pe.wait_ge(attP, e + 1)
                if i == 0 and d == 0:
                    pe.wait_ge(evac0, 3 * use_of[("turn", 2 * h + 1)] + 3)
                    if h == 0:
                        pe.wait_ge(ones_done, 1)
                if i == 1 and d == 0:
                    pe.wait_ge(c_in, 64 * (h + 1))
                if e or d:
                    pe.wait_ge(attN, 2 * e + d)
                    pe.wait_ge(attC, 2 * e + d)
                pe.matmul(ps[:, 5 + d, 0:VW], Pt[:, d, :], vaug[v][:, cx, :], start=True, stop=(i == 0))
                if i:
                    pe.matmul(ps[:, 5 + d, 0:VW], qs[:, d, :], Cst[:, d, :], start=False, stop=True)
                pe.matmul(ps[:, 7, 0:VW], kw[:, d, :], vaug[v][:, cx, :], start=True, stop=True).then_inc(attB, 1)

            def turn(src, n_src, q0):
                for b in range(NB):
                    take0(q0 + b)
                    for j in range(TB):
                        mm = n_src(ps[:, b, j * P:(j + 1) * P], b * TB + j)
                    mm.then_inc(done0, 1)

            def hm_turn(h):
                pe.wait_ge(hscaled, h + 1)
                for j in range(2):
                    turn(None, lambda o, t, j=j: pe.transpose(o, hm[h % 2][:, t, j * P:(j + 1) * P], ident[:, :]),
                         3 * use_of[("hm", 2 * h + j)])

            for m, (kind, idx) in enumerate(mains):
                seg = m - SEG
                if seg > 9 and seg % 9 == 1:
                    hm_turn(seg // 9 - 1)
                q0 = 3 * use_of[("main", m)]
                take0(q0)
                if 1 <= m <= 48 - ADA0:
                    ada_tile(ADA0 + m - 1, 0, 400)
                pe.wait_ge(lo_ready, m + 1)
                if m == 0:
                    pe.wait_ge(tl_done, 24)
                for b in range(NB):
                    take0(q0 + b)
                    block_product(ps[:, b, 0:BW], m, b, KD, H_hi, H_lo).then_inc(done0, 1)
                    if seg >= 0:
                        if b == 0:
                            attention_scores(seg // 9, seg % 9)
                        else:
                            attention_values(seg // 9, seg % 9, b - 1)
                if kind == "gates":
                    pass
                if kind == "u":
                    if idx == 0:
                        pe.wait_ge(s_wg, 16 * 9)
                    u_in = 3 * use_of[("main", m)]
                    pe.wait_ge(evac0, u_in + 3)
                    turn(None, lambda o, t: pe.matmul(o, sc[0][:, t * P:(t + 1) * P], wpool[:, idx, :], start=True, stop=True),
                         3 * use_of[("pool", idx, 0)])
                    pe.wait_ge(evac0, 3 * use_of[("pool", idx, 0)] + 3)
                    turn(None, lambda o, t: pe.matmul(o, sc[1][:, t * P:(t + 1) * P], poolM[:, 2 * idx + (t > 0), :],
                                                      start=True, stop=True),
                         3 * use_of[("pool", idx, 1)])
                if m and mains[m - 1][0] == "v":
                    vi = mains[m - 1][1]
                    pe.wait_ge(evac0, 3 * use_of[("main", m - 1)] + 3)
                    turn(None, lambda o, t: pe.transpose(o, sc[vi % 2][:, t * P:(t + 1) * P], ident[:, :]),
                         3 * use_of[("turn", vi)])
                if m == 2:
                    pe.wait_ge(g_ready, 1)
                    for t in range(NT):
                        pe.transpose(ps[:, 3, t * GR:(t + 1) * GR], Gt[0:GR, 6, t * P:(t + 1) * P], ident[0:GR, 0:GR])
                    for t in range(NT):
                        mm = pe.transpose(ps[:, 4, t * GR:(t + 1) * GR], Gt[0:GR, 4, t * P:(t + 1) * P], ident[0:GR, 0:GR])
                    mm.then_inc(g_pe, 1)
            hm_turn(NH - 1)

            for d in range(KD):
                s = S_BR + 2 * d
                if d == 0:
                    pe.wait_ge(ld_used, 4)
                pe.wait_ge(lo_ready, s + 1)
                for b in range(NB):
                    if d:
                        pe.wait_ge(evac1, 3 * (d - 1) + b + 1)
                    block_product(ps[:, 3 + b, 0:BW], s, b, 4, pT_hi, pT_lo).then_inc(done1, 1)
                pe.wait_ge(lo_ready, s + 2)
                for b in range(NB):
                    q = 3 * (U_YA + d) + b
                    take0(q)
                    r = (s + 1) % RS
                    for k in range(KD):
                        if d == 0 and b == 0:
                            pe.wait_ge(ld_used, 4 + 2 * (k + 1))
                        w = slice(k * P, (k + 1) * P)
                        tok = slice(b * BW, (b + 1) * BW)
                        mm = mm3(ps[:, b, 0:BW], ring_hi[:, r, w], ring_lo[:, r, w], H_hi[:, k, tok], H_lo[:, k, tok],
                                 k == 0, k == KD - 1)
                    mm.then_inc(done0, 1)
            for d in range(KD):
                s = S_OUT + d
                pe.wait_ge(lo_ready, s + 1)
                for b in range(NB):
                    q = 3 * (U_OUT + d) + b
                    take0(q)
                    r = s % RS
                    for k in range(KD):
                        if d == 0:
                            pe.wait_ge(mix_ready, b * KD + k + 1)
                        w = slice(k * P, (k + 1) * P)
                        tok = slice(b * BW, (b + 1) * BW)
                        mm = mm3(ps[:, b, 0:BW], ring_hi[:, r, w], ring_lo[:, r, w], H_hi[:, k, tok], H_lo[:, k, tok],
                                 k == 0, k == KD - 1)
                    mm.then_inc(done0, 1)
                if d == 0:
                    gate_rows(pe, coefG1, 0)

            def tok_turn(t):
                p = 4 + 2 * (t % 2)
                if t >= 2:
                    pe.wait_ge(evac2, t - 1)
                for k in range(KD):
                    mm = pe.transpose(ps[:, p + k // 4, (k % 4) * P:(k % 4 + 1) * P], yT[:, k, t * P:(t + 1) * P], ident[:, :])
                mm.then_inc(done2, 1)

            pe.wait_ge(evac0, Q_N2)
            pe.wait_ge(gtb_done, 2)
            for t in range(NT):
                tok_turn(t)
                if t in NORM_AFTER:
                    b = NORM_AFTER.index(t)
                    norm_block(X1, Q_N2, b, NT + TB * (b + 1))
            gate_rows(pe, coefG2, 2)

            def up_unit(r, bank, done, freed, f, i):
                for b in range(NB):
                    if f >= 1:
                        pe.wait_ge(freed, lin(3 * f + b - 2, 12, i))
                    for k in range(KD):
                        w = slice(k * P, (k + 1) * P)
                        tok = slice(b * BW, (b + 1) * BW)
                        mm = mm3(ps[:, bank + b, 0:BW], ring_hi[:, r, w], ring_lo[:, r, w], H_hi[:, k, tok],
                                 H_lo[:, k, tok], k == 0, k == KD - 1)
                    mm.then_inc(done, 1)

            def up_chunk(j0, f0, i):
                for e in range(2):
                    j = j0 + 2 * e
                    pe.wait_ge(lo_ready, lin(S_FF + j + 1, 12, i))
                    up_unit((S_FF + j) % RS, 0, done0, conv_g, f0 + e, i)
                    pe.wait_ge(lo_ready, lin(S_FF + j + 2, 12, i))
                    up_unit((S_FF + j + 1) % RS, 3, done1, conv_v, f0 + e, i)

            def down_chunk(j0, ch, i):
                pe.wait_ge(lo_ready, lin(S_FF + j0 + 2, 12, i))
                pe.wait_ge(f_ready, lin(6 * (ch + 1), 12, i))
                slot = ch % 2
                for t in range(NT):
                    tok = slice(t * P, (t + 1) * P)
                    for hb in range(2):
                        pe.wait_ge(evac2, lin(NT + 18 * ch + 2 * t + hb - 1, 36, i))
                        cols = slice(hb * 512, (hb + 1) * 512)
                        out = ps[:, 6 + hb, :]
                        for k in range(2):
                            r = (S_FF + j0 + k) % RS
                            pe.matmul(out, fT_hi[:, slot, k, tok], ring_hi[:, r, cols], start=(k == 0), stop=False)
                            pe.matmul(out, fT_hi[:, slot, k, tok], ring_lo[:, r, cols], start=False, stop=False)
                            mm = pe.matmul(out, fT_lo[:, slot, k, tok], ring_hi[:, r, cols], start=False, stop=(k == 1))
                        mm.then_inc(done2, 1)

            pe.wait_ge(tl_done, 48)
            pe.wait_ge(gtb_done, 4)
            up_chunk(0, 0, None)
            with pe.Fori(0, (NC - 1) // 2) as i:
                for cc in range(2):
                    up_chunk(4 + 6 * cc, 2 + 2 * cc, i)
                    down_chunk(8 + 6 * cc, cc, i)
            down_chunk(4 + 6 * (NC - 1), NC - 1, None)

        @block.scalar
        def _(act):
            seq = [0]

            def link(ins):
                seq[0] += 1
                ins.then_inc(act_seq, 1)
                act.wait_ge(act_seq, seq[0])

            def hi_split(s):
                if s >= S_FF:
                    return ff_hi(s - S_FF, None)
                n = raw_n(s)
                w = unit_width(s)
                act.wait_ge(landed[n % RS], 16 * (n // RS + 1))
                free_slot(act, s)
                act.activation(ring_hi[:, s % RS, 0:w], raw[:, n % RS, 0:w], ACT.Copy).then_inc(hi_ready, 1)

            def ff_hi(j, i):
                n0 = N_FF + j
                r = (S_FF + j) % RS
                act.wait_ge(landed[n0 % RS], lin(16 * (n0 // RS + 1), 16 * (12 // RS), i))
                if j < RS:
                    free_slot(act, S_FF + j)
                else:
                    p = j - RS
                    if p < 4:
                        if p % 2:
                            act.wait_ge(done1, lin(3 * KD + 3 * (p // 2 + 1), 12, i))
                        else:
                            act.wait_ge(done0, lin(Q_FF + 3 * (p // 2 + 1), 12, i))
                        if p >= 2 and i is not None:
                            act.wait_ge(done2, lin(NT, 36, i))
                    else:
                        ch, at = 1 + (p - 4) // 6, (p - 4) % 6
                        if at < 4:
                            f = 2 * ch + at // 2
                            act.wait_ge(done1 if at % 2 else done0, lin((3 * KD if at % 2 else Q_FF) + 3 * (f + 1), 12, i))
                        else:
                            act.wait_ge(done2, lin(NT + 18 * ch, 36, i))
                act.activation(ring_hi[:, r, :], raw[:, n0 % RS, :], ACT.Copy).then_inc(hi_ready, 1)

            act.wait_ge(vec_done, 2)
            act.activation(condT[:, :, :], vT[:, V_C:V_C + 16].rearrange("p (c k) -> p c k", c=2), ACT.Silu).then_inc(cond_done, 1)
            act.wait_ge(s_x, 32)
            for t in range(NT):
                if t:
                    act.wait_ge(ss_done, t)
                act.activation(stage[0][:, 0:DM], X0[:, t, :], ACT.Square, accum_out=stat[:, 0, t:t + 1]).then_inc(ss_done, 1)
            act.wait_ge(rt_done, 1)
            act.activation(stat[:, 2, :], stat[:, 1, :], ACT.Sqrt).then_inc(rt_done, 1)

            def norm_evac(q0, coefA, sh, n0, tile, b):
                if True:
                    for k in range(KD):
                        q = q0 + b * KD + k
                        w = n0 + b * KD + k
                        act.wait_ge(done0, q + 1)
                        if w - n0 >= 2:
                            act.wait_ge(tl_done, w - 1)
                        parts = [(0, 0, P), (1, P, BW)] if b == 0 else [(1, 0, BW)]
                        for cond, lo, hi in parts:
                            act.activation(tile[:, w % 2, lo:hi], ps[:, q % 3, lo:hi], ACT.Identity,
                                           scale=coefA[:, k, cond:cond + 1], bias=modT[:, sh + k, cond:cond + 1])
                            ins = act.activation(H_hi[:, k, b * BW + lo:b * BW + hi], ps[:, q % 3, lo:hi], ACT.Identity,
                                                 scale=coefA[:, k, cond:cond + 1], bias=modT[:, sh + k, cond:cond + 1])
                        ins.then_inc(evac0, 1)

            act.wait_ge(coef1, 1)
            for b in range(NB):
                norm_evac(0, coefA1, 0, 0, tsc, b)

            store_no = [0]

            def stage_slot(item):
                w = stage_no[item]
                if w >= 2:
                    act.wait_ge(stored[w % 2], 16 * (w // 2))
                return w % 2

            def put(item, q_end):
                w = stage_no[item]
                act.wait_ge(evac0, q_end)
                act.dma_start(Z[item[0]][item[1]], stage[w % 2][:, :]).then_inc(stored[w % 2], 16)

            def evac_copy(q0, dst, scale=None, func=ACT.Copy):
                for b in range(NB):
                    act.wait_ge(done0, q0 + b + 1)
                    out = dst(b)
                    src = ps[:, b, 0:BW]
                    if len(out.shape) == 3:
                        src = src.rearrange("p (t s) -> p t s", s=P)
                    kw_ = {} if scale is None else {"scale": scale}
                    act.activation(out, src, func, **kw_).then_inc(evac0, 1)

            def hm_evac(h):
                for j in range(2):
                    item = ("hm", 2 * h + j)
                    st = stage_slot(item)
                    q0 = 3 * use_of[item]
                    evac_copy(q0, lambda b: stage[st][:, b * BW:(b + 1) * BW])
                    put(item, q0 + 3)

            def hm_norm(h):
                act.wait_ge(attN, 18 * (h + 1))
                for t in range(NT):
                    if t:
                        act.wait_ge(hss, NT * h + t)
                    act.activation(Wt[:, :, :].rearrange("p a b -> p (a b)"), hm[h % 2][:, t, :], ACT.Square,
                                   accum_out=hstat[:, 0, t:t + 1]).then_inc(hss, 1)
                act.wait_ge(hrt, 2 * h + 1)
                act.activation(hstat[:, 1, :], hstat[:, 0, :], ACT.Sqrt).then_inc(hrt, 1)

            hi_split(1)
            for m, (kind, idx) in enumerate(mains):
                seg = m - SEG
                if seg > 9 and seg % 9 == 1:
                    hm_evac(seg // 9 - 1)
                hi_split(m + 2)
                q0 = 3 * use_of[("main", m)]
                if 1 <= m <= 48 - ADA0:
                    j = ADA0 + m - 1
                    act.wait_ge(ada_used, j + 1)
                    act.wait_ge(done0, q0 + 1)
                    act.activation(modT[:, j, :], ps[:, 0, 400:402], ACT.Identity, bias=vT[:, V_BADA + j:V_BADA + j + 1])
                if kind == "gates":
                    act.wait_ge(s_wg, 16 * 9)
                    for b in range(NB):
                        tok = slice(b * BW, (b + 1) * BW)
                        act.wait_ge(done0, q0 + b + 1)
                        act.activation(Gt[0:GR, 0, tok], ps[0:GR, b, 0:BW], ACT.Identity, bias=gbias[0:GR, 0:1])
                        act.activation(Gt[0:GR, 1, tok], ps[64:64 + GR, b, 0:BW], ACT.Identity, bias=gbias[0:GR, 1:2]).then_inc(evac0, 1)
                    act.wait_ge(evac0, q0 + 3)
                    link(act.activation(Gt[0:GR, 2, :], Gt[0:GR, 1, :], ACT.Abs))
                    link(act.activation(Gt[0:GR, 2, :], Gt[0:GR, 2, :], ACT.Exp, scale=-1.0))
                    act.activation(Gt[0:GR, 2, :], Gt[0:GR, 2, :], ACT.Ln, bias=1.0).then_inc(g_lf, 1)
                    continue
                first = [True]
                if seg >= 0:
                    def exps():
                        h, i = seg // 9, seg % 9
                        e = h * 9 + i
                        cf, cb = (0, 0) if i == 0 else (i, NT - i)
                        act.wait_ge(attA, e + 1)
                        if e:
                            act.wait_ge(attC, 2 * e)
                        for d, cx in ((0, cf), (1, cb)):
                            act.activation(Wt[:, d, :], ps[:, 3, d * P:(d + 1) * P], ACT.Exp, bias=a_tok[:, cx, d, h:h + 1])
                        act.activation(Et[:, :, :], ps[:, 3, 256:512].rearrange("p (a b) -> p a b", b=P), ACT.Exp).then_inc(attX, 1)
                else:
                    exps = lambda: None
                if kind == "q":
                    evac_q(act, q0, qT[idx % 2], QSCALE, exps, done0, evac0, ps)
                elif kind == "k":
                    evac_q(act, q0, kT[idx % 2], None, exps, done0, evac0, ps)
                elif kind in ("v", "u"):
                    evac_q(act, q0, sc[idx % 2 if kind == "v" else 0], None, exps, done0, evac0, ps)
                else:
                    st = stage_slot((kind, idx))
                    evac_q(act, q0, stage[st], None, exps, done0, evac0, ps)
                    put((kind, idx), q0 + 3)
                if kind == "u":
                    q1 = 3 * use_of[("pool", idx, 0)]
                    evac_copy(q1, lambda b: sc[1][:, b * BW:(b + 1) * BW])
                    st = stage_slot(("pool", idx))
                    q1 += 3
                    evac_copy(q1, lambda b: stage[st][:, b * BW:(b + 1) * BW], scale=vT[:, V_PS + idx:V_PS + idx + 1],
                              func=ACT.Identity)
                    put(("pool", idx), q1 + 3)
                if m and mains[m - 1][0] == "v":
                    vi = mains[m - 1][1]
                    q1 = 3 * use_of[("turn", vi)]
                    if vi == 0:
                        act.wait_ge(s_out, 32)
                    evac_copy(q1, lambda b: vaug[(vi // 2) % 2][:, b * TB:(b + 1) * TB, (vi % 2) * P:(vi % 2 + 1) * P])
                if m == 2:
                    act.wait_ge(g_pe, 1)
                    for src, dst, f, sc_ in ((3, a_tok, ACT.Copy, 1.0), (4, en_tok, ACT.Exp, -1.0)):
                        for d in range(2):
                            ins = act.activation(dst[:, :, d, :], ps[:, src, 0:NT * GR].rearrange("p (t r) -> p t r", r=GR)
                                                 [:, :, 32 * d:32 * d + NH], f, scale=sc_)
                    ins.then_inc(g_tok, 1)
                if seg >= 0 and seg % 9 == 8:
                    hm_norm(seg // 9)
            hm_evac(NH - 1)

            def landed_ld(eng, w):
                eng.wait_ge(ld_in[w % 4], 16 * (w // 4 + 1))

            for g in range(4):
                landed_ld(act, g)
                act.activation(pT_hi[:, g, :], ld[:, g, :], ACT.Copy).then_inc(hmhi, 1)

            def sig(w):
                landed_ld(act, w)
                act.activation(ld[:, w % 4, :], ld[:, w % 4, :], ACT.Sigmoid).then_inc(sgm, 1)

            sig(5)
            for k in range(KD):
                if k + 1 < KD:
                    sig(5 + 2 * (k + 1))
                act.wait_ge(hmx, k + 1)
                act.activation(H_hi[:, k, :], ld[:, (4 + 2 * k) % 4, :], ACT.Copy).then_inc(hmhi, 1)
            for d in range(KD):
                s = S_BR + 2 * d
                hi_split(s + 2)
                sig(20 + 2 * d)
                sig(21 + 2 * d)
                hi_split(s + 3)
            for b in range(NB):
                tok = slice(b * BW, (b + 1) * BW)
                for k in range(KD):
                    if b == 0 and k == 0:
                        act.wait_ge(ld_used, 36)
                    act.activation(H_hi[:, k, tok], mixF[:, k, tok], ACT.Copy).then_inc(mixhi, 1)
            for d in range(KD):
                hi_split(S_OUT + d + 2)
                evac_copy(3 * (U_OUT + d), lambda b: yT[:, d, b * BW:(b + 1) * BW])
                if d == 0:
                    for cond in range(2):
                        act.wait_ge(gtb_pe, cond + 1)
                        act.activation(gtb1[:, cond, :], ps[:, 6:8, :].rearrange("p a b -> p (a b)"), ACT.Copy).then_inc(gtb_done, 1)
            for t in range(NT):
                p = 4 + 2 * (t % 2)
                pair = ps[:, p:p + 2, :].rearrange("p a b -> p (a b)")
                act.wait_ge(done2, t + 1)
                if t == 0:
                    act.wait_ge(mix_ready, NB * KD)
                act.activation(X1[:, t, :], pair, ACT.Square, accum_out=stat[:, 0, t:t + 1]).then_inc(ss2, 1)
                act.wait_ge(vv2, 2 * t + 1)
                act.activation(stat[:, 2, t:t + 1], stat[:, 1, t:t + 1], ACT.Sqrt).then_inc(rt2, 1)
                act.wait_ge(x1_ready, t + 1)
                act.activation(xld[:, t % 2, :], X1[:, t, :], ACT.Square, accum_out=stat[:, 3, t:t + 1]).then_inc(ss2, 1)
                act.wait_ge(vv2, 2 * t + 2)
                act.activation(hstat[:, 1, t:t + 1], hstat[:, 0, t:t + 1], ACT.Sqrt).then_inc(rt2, 1)
                if t in NORM_AFTER:
                    norm_evac(Q_N2, coefA2, 24, 24, tsc2, NORM_AFTER.index(t))
            for cond in range(2):
                act.wait_ge(gtb_pe, 3 + cond)
                act.activation(gtb2[:, cond, :], ps[:, 6:8, :].rearrange("p a b -> p (a b)"), ACT.Copy).then_inc(gtb_done, 1)

            def ff_up_act(f, e, slot, splits, i):
                first = V_W1 + f
                cols = slice(first, first + 5 * NF + 1, NF) if i is None else bass.ds(i * 4 + first, 6, NF)
                act.activation(taps[:, e, :], vT[:, cols], ACT.Copy).then_inc(taps_done, 1)
                act.wait_ge(taps_done, lin(f + 1, 4, i))
                for half in range(2):
                    for j in splits[half]:
                        ff_hi(j, i)
                    tile = cv if half else cg
                    for b in range(NB):
                        tok = slice(b * BW, (b + 1) * BW)
                        if half:
                            act.wait_ge(done1, lin(3 * KD + 3 * f + b + 1, 12, i))
                        else:
                            act.wait_ge(done0, lin(Q_FF + 3 * f + b + 1, 12, i))
                        if f:
                            act.wait_ge(f_ready, lin(3 * f + b - 2, 12, i))
                        act.activation(tile[:, tok], ps[:, b + 3 * half, 0:BW], ACT.Identity,
                                       scale=taps[:, e, half:half + 1], bias=taps[:, e, 4 + half:5 + half]).then_inc(conv_a, 1)
                        if half:
                            act.wait_ge(conv_v, lin(3 * f + b + 1, 12, i))
                            act.activation(fT_hi[:, slot, e, tok], cv[:, tok], ACT.Copy).then_inc(fhi, 1)
                        else:
                            act.wait_ge(conv_g, lin(3 * f + b + 1, 12, i))
                            act.activation(cg[:, tok], cg[:, tok], ACT.Gelu_apprx_tanh).then_inc(gel, 1)

            ff_up_act(0, 0, 0, [[2], [3]], None)
            ff_up_act(1, 1, 0, [[4], []], None)
            with act.Fori(0, (NC - 1) // 2) as i:
                for cc in range(2):
                    j = 4 + 6 * cc
                    ff_up_act(2 + 2 * cc, 0, 1 - cc, [[j + 1, j + 2], [j + 3]], i)
                    ff_up_act(3 + 2 * cc, 1, 1 - cc, [[j + 4], [j + 5]], i)
                    ff_hi(j + 6, i)
            ff_hi(5 + 6 * (NC - 1), None)
            for t in range(NT):
                act.wait_ge(evac2, NT + 18 * (NC - 1) + 2 * (t + 1))
                act.activation(ps[:, 0:2, :], acc[:, t, :].rearrange("p (a b) -> p a b", b=512), ACT.Square,
                               accum_out=stat[:, 0, t:t + 1]).then_inc(fin_rt, 1)
                act.wait_ge(fin_ss, t + 1)
                act.activation(stat[:, 2, t:t + 1], stat[:, 1, t:t + 1], ACT.Sqrt).then_inc(fin_rt, 1)

        @block.vector
        def _(dve):
            seq = [0]

            def link(ins):
                seq[0] += 1
                ins.then_inc(dve_seq, 1)
                dve.wait_ge(dve_seq, seq[0])

            def sub_hi(out, full, hi):
                return dve.tensor_tensor(out, full, hi.bitcast(F32), ALU.subtract)

            def lo_split(s):
                if s >= S_FF:
                    return ff_lo(s - S_FF, None)
                n, w = raw_n(s), unit_width(s)
                dve.wait_ge(hi_ready, s)
                sub_hi(ring_lo[:, s % RS, 0:w], raw[:, n % RS, 0:w], ring_hi[:, s % RS, 0:w]).then_inc(lo_ready, 1)

            def ff_lo(j, i):
                n0, r = N_FF + j, (S_FF + j) % RS
                dve.wait_ge(hi_ready, lin(S_FF + j, 12, i))
                sub_hi(ring_lo[:, r, :], raw[:, n0 % RS, :], ring_hi[:, r, :]).then_inc(lo_ready, 1)

            def rows(col, n):
                return vT[:, col:col + n].unsqueeze(2).to_broadcast([P, n, 2])

            dve.wait_ge(s_cst, 48)
            dve.tensor_copy(idbf[:, :], ident[:, :])
            dve.tensor_copy(maskbf[:, :, :], sc[1][:, 0:2 * P].rearrange("p (a b) -> p a b", b=P))
            dve.tensor_copy(sel[:, :, :], stage[1][:, 0:8 * P].rearrange("p (a b) -> p a b", b=P))
            dve.wait_ge(vec_done, 1)
            dve.tensor_copy(vT[:, :], ps[:, 3, 0:NV]).then_inc(vec_done, 1)
            dve.wait_ge(s_wg, 16 * 9)
            dve.memset(ring_hi[:, 0, :].bitcast(F32), 0.0)
            link(dve.memset(ring_lo[:, 0, :].bitcast(F32), 0.0))
            spread = lambda ap: ap.rearrange("p (k g c) -> p k g c", k=KD, g=4)[:, :, :, 0:4]
            wg4 = wgate[:, :, :].rearrange("p k (g c) -> p k g c", c=4)
            link(dve.tensor_copy(spread(ring_hi[:, 0, :]), wg4))
            sub_hi(spread(ring_lo[:, 0, :]), wg4, spread(ring_hi[:, 0, :])).then_inc(lo_ready, 1)

            dve.wait_ge(ss_done, NT)
            dve.tensor_scalar(stat[:, 1, :], stat[:, 0, :], 1.0 / DM, EPS, ALU.mult, ALU.add).then_inc(rt_done, 1)
            dve.wait_ge(rt_done, 2)
            link(dve.reciprocal(stat[:, 3, :], stat[:, 2, :]))
            for t in range(NT):
                dve.tensor_scalar(X0[:, t, :], X0[:, t, :], stat[:, 3, t:t + 1], None, ALU.mult).then_inc(x_scaled, 1)
            dve.wait_ge(ada_used, ADA0)
            link(dve.tensor_tensor(modT[:, 0:ADA0, :], ps[:, 7, 0:2 * ADA0].rearrange("p (a b) -> p a b", b=2),
                                   rows(V_BADA, ADA0), ALU.add))
            dve.scalar_tensor_tensor(out=coefA1[:, :, :], in0=modT[:, 8:16, :], scalar=1.0, in1=rows(V_GPM, KD),
                                     op0=ALU.add, op1=ALU.mult).then_inc(coef1, 1)

            def norm_lo(q0, n0, tile, b):
                for k in range(KD):
                    w = n0 + b * KD + k
                    dve.wait_ge(evac0, q0 + b * KD + k + 1)
                    tok = slice(b * BW, (b + 1) * BW)
                    sub_hi(H_lo[:, k, tok], tile[:, w % 2, :], H_hi[:, k, tok]).then_inc(tl_done, 1)

            for b in range(NB):
                norm_lo(0, 0, tsc, b)

            def gates():
                link(dve.memset(Gt[0:GR, 3:5, :], 0.0))
                dve.memset(GS[:, :].bitcast(F32), 0.0)
                dve.memset(YS[:, :].bitcast(F32), 0.0)
                dve.wait_ge(g_lf, 1)
                li, lf, bb, mm_, gg, aa, yy = (Gt[0:GR, r, :] for r in (0, 1, 3, 4, 5, 6, 7))
                link(dve.scalar_tensor_tensor(out=lf, in0=lf, scalar=0.0, in1=Gt[0:GR, 2, :], op0=ALU.min, op1=ALU.subtract))
                fwd, bwd = slice(0, 4), slice(32, 36)
                dve.tensor_tensor_scan(Gt[fwd, 3, :], reset[fwd, :], Gt[fwd, 1, :], 0.0, ALU.mult, ALU.add)
                dve.tensor_tensor_scan(Gt[bwd, 3, :][:, ::-1], reset[bwd, :][:, ::-1], Gt[bwd, 1, :][:, ::-1], 0.0,
                                       ALU.mult, ALU.add)
                for rw, dr in ((fwd, 1), (bwd, -1)):
                    for lo, hi, init in ((0, CTX, 0.0), (CTX, T, m0t[rw, :])):
                        a = [Gt[rw, r, lo:hi] if dr == 1 else Gt[rw, r, lo:hi][:, ::-1] for r in (4, 1, 0)]
                        ins = dve.tensor_tensor_scan(a[0], a[1], a[2], init, ALU.add, ALU.max)
                link(ins)
                m3 = Gt[0:GR, 4, :].rearrange("p (t s) -> p t s", s=P)
                dve.tensor_copy(mprev[fwd, 1:2], m0t[fwd, :])
                dve.tensor_copy(mprev[bwd, NT - 1:NT], m0t[bwd, :])
                dve.tensor_copy(mprev[fwd, 2:NT], m3[fwd, 1:NT - 1, P - 1])
                dve.tensor_copy(mprev[bwd, 1:NT - 1], m3[bwd, 2:NT, 0])
                dve.tensor_tensor(aa, li, bb, ALU.subtract)
                link(dve.tensor_tensor(gg, bb, mm_, ALU.subtract))
                link(dve.tensor_tensor(yy.rearrange("p (t s) -> p t s", s=P), gg.rearrange("p (t s) -> p t s", s=P),
                                       mprev[0:GR, :].unsqueeze(2).to_broadcast([GR, NT, P]), ALU.add))
                dve.tensor_copy(GS[0:GR, :], gg)
                link(dve.tensor_copy(YS[0:GR, :], yy))
                sub_hi(GS[64:64 + GR, :], gg, GS[0:GR, :])
                sub_hi(YS[64:64 + GR, :], yy, YS[0:GR, :]).then_inc(g_ready, 1)

            def attention_weights(h, i):
                e = h * 9 + i
                tiles = (0, 0) if i == 0 else (i, NT - i)
                v = h % 2
                dve.wait_ge(attX, e + 1)
                dve.tensor_tensor(Pt[:, :, :].rearrange("p a b -> p (a b)"), ps[:, 4, 0:256],
                                  Wt[:, :, :].rearrange("p a b -> p (a b)"), ALU.mult)
                if i:
                    for d, cx in enumerate(tiles):
                        dve.tensor_tensor(qs[:, d, :], qT[v][:, cx * P:(cx + 1) * P], Et[:, d, :], ALU.mult)
                for d in range(2):
                    last = (1 - d) * (P - 1)
                    ins = dve.tensor_scalar(kw[:, d, :], ps[:, 4, 256 + d * P:256 + (d + 1) * P], Wt[:, d, last:last + 1], None,
                                            ALU.mult)
                ins.then_inc(attP, 1)

            def attention_outputs(h, i, d):
                e = h * 9 + i
                cx = 0 if i == 0 else (i, NT - i)[d]
                hd = hm[h % 2]
                last = (1 - d) * (P - 1)
                dve.wait_ge(attB, 2 * e + d + 1)
                if i == 0:
                    if h:
                        dve.wait_ge(c_out, 64 * h)
                    dve.tensor_copy(Cctx[:, d, :], ps[:, 7, 0:VW]).then_inc(attC, 1)
                else:
                    dve.scalar_tensor_tensor(out=Cst[:, d, :], in0=Cst[:, d, :], scalar=Et[:, d, last:last + 1],
                                             in1=ps[:, 7, 0:VW], op0=ALU.mult, op1=ALU.add).then_inc(attC, 1)
                den, rec = dsm[:, 2 * d:2 * d + 1], dsm[:, 2 * d + 1:2 * d + 2]
                link(dve.scalar_tensor_tensor(out=den, in0=ps[:, 5 + d, DV:VW], scalar=-1.0, in1=en_tok[:, cx, d, h:h + 1],
                                              op0=ALU.mult, op1=ALU.max))
                link(dve.tensor_tensor(den, ps[:, 5 + d, DV:VW], den, ALU.max))
                link(dve.reciprocal(rec, den))
                if (i == 0 and d == 0) or 1 <= i <= 4:
                    dve.tensor_scalar(hd[:, cx, :], ps[:, 5 + d, 0:DV], rec, None, ALU.mult).then_inc(attN, 1)
                else:
                    dve.scalar_tensor_tensor(out=hd[:, cx, :], in0=ps[:, 5 + d, 0:DV], scalar=rec, in1=hd[:, cx, :],
                                             op0=ALU.mult, op1=ALU.add).then_inc(attN, 1)

            lo_split(1)
            for m, (kind, idx) in enumerate(mains):
                seg = m - SEG
                lo_split(m + 2)
                if m == 0:
                    gates()
                if m == SEG - 4:
                    dve.wait_ge(g_tok, 1)
                    dve.wait_ge(s_out, 32)
                    dve.memset(vaug[0][:, :, DV:VW], 1.0)
                    dve.memset(vaug[1][:, :, DV:VW], 1.0).then_inc(ones_done, 1)
                if seg >= 0:
                    h, i = seg // 9, seg % 9
                    attention_weights(h, i)
                    attention_outputs(h, i, 0)
                    attention_outputs(h, i, 1)
                    if i == 8:
                        dve.wait_ge(hss, NT * (h + 1))
                        dve.tensor_scalar(hstat[:, 0, :], hstat[:, 0, :], 1.0 / DV, EPS, ALU.mult, ALU.add).then_inc(hrt, 1)
                        dve.wait_ge(hrt, 2 * h + 2)
                        link(dve.reciprocal(hstat[:, 0, :], hstat[:, 1, :]))
                        for t in range(NT):
                            ins = dve.tensor_scalar(hm[h % 2][:, t, :], hm[h % 2][:, t, :], hstat[:, 0, t:t + 1], None, ALU.mult)
                        ins.then_inc(hscaled, 1)

            dve.wait_ge(evac0, Q_P1)
            dve.scalar_tensor_tensor(out=coefA2[:, :, :], in0=modT[:, 32:40, :], scalar=1.0, in1=rows(V_GPF, KD),
                                     op0=ALU.add, op1=ALU.mult)
            dve.tensor_tensor(coefG1[:, :, :], modT[:, 16:24, :], rows(V_GQM, KD), ALU.mult)
            dve.tensor_tensor(coefG2[:, :, :], modT[:, 40:48, :], rows(V_GQF, KD), ALU.mult).then_inc(coef2, 1)
            for g in range(4):
                dve.wait_ge(hmhi, g + 1)
                sub_hi(pT_lo[:, g, :], ld[:, g, :], pT_hi[:, g, :]).then_inc(ld_used, 1)
            for k in range(KD):
                w = 4 + 2 * k
                dve.wait_ge(ld_in[w % 4], 16 * (w // 4 + 1))
                dve.wait_ge(sgm, k + 1)
                dve.scalar_tensor_tensor(out=ld[:, w % 4, :], in0=ld[:, w % 4, :], scalar=vT[:, V_GH + k:V_GH + k + 1],
                                         in1=ld[:, (w + 1) % 4, :], op0=ALU.mult, op1=ALU.mult).then_inc(hmx, 1)
                dve.wait_ge(hmhi, 4 + k + 1)
                sub_hi(H_lo[:, k, :], ld[:, w % 4, :], H_hi[:, k, :]).then_inc(ld_used, 2)
            for d in range(KD):
                s = S_BR + 2 * d
                lo_split(s + 2)
                wb, wa = (20 + 2 * d) % 4, (21 + 2 * d) % 4
                dve.wait_ge(sgm, KD + 2 * d + 1)
                for b in range(NB):
                    tok = slice(b * BW, (b + 1) * BW)
                    dve.wait_ge(done1, 3 * d + b + 1)
                    dve.tensor_tensor(ld[:, wb, tok], ps[:, 3 + b, 0:BW], ld[:, wb, tok], ALU.mult).then_inc(evac1, 1)
                lo_split(s + 3)
                dve.wait_ge(sgm, KD + 2 * d + 2)
                for b in range(NB):
                    tok = slice(b * BW, (b + 1) * BW)
                    q = 3 * (U_YA + d) + b + 1
                    dve.wait_ge(done0, q)
                    dve.tensor_tensor(ld[:, wa, tok], ps[:, b, 0:BW], ld[:, wa, tok], ALU.mult).then_inc(evac0, 1)
                    dve.wait_ge(evac0, q)
                    ins = dve.tensor_tensor(mixF[:, d, tok], ld[:, wa, tok], ld[:, wb, tok], ALU.add)
                ins.then_inc(ld_used, 2)
            for b in range(NB):
                for k in range(KD):
                    tok = slice(b * BW, (b + 1) * BW)
                    dve.wait_ge(mixhi, b * KD + k + 1)
                    sub_hi(H_lo[:, k, tok], mixF[:, k, tok], H_hi[:, k, tok]).then_inc(mix_ready, 1)
            for d in range(KD):
                lo_split(S_OUT + d + 2)

            def scale_tile(t):
                dve.wait_ge(x1_stored[t % 2], 16 * (t // 2 + 1))
                dve.tensor_scalar(X1[:, t, :], X1[:, t, :], stat[:, 3, t:t + 1], None, ALU.mult).then_inc(x_scaled, 1)

            dve.wait_ge(gtb_done, 2)
            for t in range(NT):
                p = 4 + 2 * (t % 2)
                cond = 0 if t == 0 else 1
                dve.wait_ge(ss2, 2 * t + 1)
                dve.tensor_scalar(stat[:, 1, t:t + 1], stat[:, 0, t:t + 1], 1.0 / DM, EPS, ALU.mult, ALU.add).then_inc(vv2, 1)
                dve.wait_ge(rt2, 2 * t + 1)
                link(dve.reciprocal(stat[:, 0, t:t + 1], stat[:, 2, t:t + 1]))
                dve.scalar_tensor_tensor(out=X1[:, t, :], in0=ps[:, p:p + 2, :].rearrange("p a b -> p (a b)"),
                                         scalar=stat[:, 0, t:t + 1], in1=gtb1[:, cond, :], op0=ALU.mult,
                                         op1=ALU.mult).then_inc(evac2, 1)
                dve.wait_ge(evac2, t + 1)
                dve.wait_ge(x_in[t % 2], 16 * (t // 2 + 1))
                dve.tensor_tensor(X1[:, t, :], X1[:, t, :], xld[:, t % 2, :], ALU.add).then_inc(x1_ready, 1)
                dve.wait_ge(ss2, 2 * t + 2)
                dve.tensor_scalar(hstat[:, 0, t:t + 1], stat[:, 3, t:t + 1], 1.0 / DM, EPS, ALU.mult, ALU.add).then_inc(vv2, 1)
                dve.wait_ge(rt2, 2 * t + 2)
                link(dve.reciprocal(stat[:, 3, t:t + 1], hstat[:, 1, t:t + 1]))
                if t >= 2:
                    scale_tile(t - 2)
                if t == NT - 1:
                    scale_tile(t - 1)
                    scale_tile(t)
                if t in NORM_AFTER:
                    norm_lo(Q_N2, 3 * KD, tsc2, NORM_AFTER.index(t))

            def ff_up_dve(f, e, slot, splits, i):
                n = [12 * f]

                def step(ins):
                    n[0] += 1
                    ins.then_inc(dve_ff, 1)

                def settle():
                    dve.wait_ge(dve_ff, lin(n[0], 48, i))

                for half in range(2):
                    for j in splits[half]:
                        ff_lo(j, i)
                    tile = cv if half else cg
                    for b in range(NB):
                        dve.wait_ge(conv_a, lin(6 * f + 3 * half + b + 1, 24, i))

                        def tap(lo, nr, ln, shift):
                            out = tile[:, b * BW + lo:b * BW + lo + nr * ln].rearrange("p (r c) -> p r c", c=ln)
                            src = ps[:, b + 3 * half, lo:lo + nr * ln].rearrange("p (r c) -> p r c", c=ln)
                            if shift < 0:
                                out, src, w = out[:, :, 1:ln], src[:, :, 0:ln - 1], V_W0
                            else:
                                out, src, w = out[:, :, 0:ln - 1], src[:, :, 1:ln], V_W2
                            return dve.scalar_tensor_tensor(out=out, in0=src, scalar=vcol(w + NF * half + f, i), in1=out,
                                                            op0=ALU.mult, op1=ALU.add)

                        parts = row_parts(b)
                        for pt in parts:
                            step(tap(*pt, -1))
                        settle()
                        tok = slice(b * BW, (b + 1) * BW)
                        if half == 0:
                            for pt in parts:
                                ins = tap(*pt, 1)
                            ins.then_inc(conv_g, 1)
                        else:
                            for pt in parts:
                                step(tap(*pt, 1))
                            settle()
                            dve.wait_ge(gel, lin(3 * f + b + 1, 12, i))
                            dve.tensor_tensor(cv[:, tok], cg[:, tok], cv[:, tok], ALU.mult).then_inc(conv_v, 1)
                            dve.wait_ge(fhi, lin(3 * f + b + 1, 12, i))
                            sub_hi(fT_lo[:, slot, e, tok], cv[:, tok], fT_hi[:, slot, e, tok]).then_inc(f_ready, 1)
                assert n[0] == 12 * (f + 1)

            def add_halves(ch, t, i):
                for hb in range(2):
                    dve.wait_ge(done2, lin(NT + 18 * ch + 2 * t + hb + 1, 36, i))
                    cols = slice(hb * 512, (hb + 1) * 512)
                    dve.tensor_tensor(acc[:, t, cols], ps[:, 6 + hb, :], acc[:, t, cols], ALU.add).then_inc(evac2, 1)

            ff_up_dve(0, 0, 0, [[2], [3]], None)
            ff_up_dve(1, 1, 0, [[4], []], None)
            dve.wait_ge(acc_zero, 1)
            with dve.Fori(0, (NC - 1) // 2) as i:
                for cc in range(2):
                    j = 4 + 6 * cc
                    ff_up_dve(2 + 2 * cc, 0, 1 - cc, [[j + 1, j + 2], [j + 3]], i)
                    ff_up_dve(3 + 2 * cc, 1, 1 - cc, [[j + 4], [j + 5]], i)
                    ff_lo(j + 6, i)
                    for t in range(NT):
                        add_halves(cc, t, i)
            ff_lo(5 + 6 * (NC - 1), None)

            def finish(t):
                dve.wait_ge(fin_rt, 2 * t + 1)
                dve.tensor_scalar(stat[:, 1, t:t + 1], stat[:, 0, t:t + 1], 1.0 / DM, EPS, ALU.mult, ALU.add).then_inc(fin_ss, 1)
                dve.wait_ge(fin_rt, 2 * t + 2)
                link(dve.reciprocal(stat[:, 3, t:t + 1], stat[:, 2, t:t + 1]))
                link(dve.scalar_tensor_tensor(out=acc[:, t, :], in0=acc[:, t, :], scalar=stat[:, 3, t:t + 1],
                                              in1=gtb2[:, 0 if t == 0 else 1, :], op0=ALU.mult, op1=ALU.mult))
                dve.wait_ge(x1_in[t % 2], 16 * (t // 2 + 1))
                dve.tensor_tensor(acc[:, t, :], acc[:, t, :], x1ld[:, t % 2, :], ALU.add).then_inc(fin_o, 1)

            dve.wait_ge(gtb_done, 4)
            for t in range(NT):
                add_halves(NC - 1, t, None)
                if t:
                    finish(t - 1)
            finish(NT - 1)


_INS = ['x_prompt', 'x_sample', 'state_C', 'state_n', 'state_m', 'c', 'c_ctx', 'w_ada', 'b_ada', 'g_pre_mix',
        'g_post_mix', 'g_pre_ffn', 'g_post_ffn', 'w_in', 'b_gates', 'g_head', 'w_pool', 'pool_scale', 'w_br_a',
        'w_br_b', 'w_out', 'w_up', 'conv_w', 'conv_b', 'w_down']
_OUTS = [(1, 128, 1024), (1, 1024, 1024), (1, 1, 2, 4, 128, 256), (1, 1, 2, 4, 128), (1, 1, 2, 4)]


def kernel(**inputs):
    import concourse.bacc as _bacc
    from concourse.bass_utils import run_bass_kernel_spmd as _run

    nc = _bacc.Bacc("TRN2", target_bir_lowering=False, num_devices=1)
    arrays, args = {}, []
    for name in _INS:
        a = np.ascontiguousarray(inputs[name])
        arrays[f"in_{name}_dram"] = a
        args.append(nc.dram_tensor(f"in_{name}_dram", a.shape, mybir.dt.from_np(a.dtype), kind="ExternalInput").ap())
    arrays["in_consts_dram"] = shape_constants()
    args.append(nc.dram_tensor("in_consts_dram", (P, H_COLS), F32, kind="ExternalInput").ap())
    for i, shape in enumerate(_OUTS):
        args.append(nc.dram_tensor(f"out_{i}_dram", shape, F32, kind="ExternalOutput").ap())
    build(nc, *args)
    r = _run(nc, [arrays], core_ids=[0])
    return tuple(r.results[0][f"out_{i}_dram"] for i in range(len(_OUTS)))
```

```python
import numpy as np

import concourse.bass as bass
from concourse import mybir

F32 = mybir.dt.float32
F32R = mybir.dt.float32r
BF16 = mybir.dt.bfloat16
ALU = mybir.AluOpType
ACT = mybir.ActivationFunctionType

P = 128
DM = 1024
KD = DM // P
CTX = 128
LAT = 1024
T = CTX + LAT
NT = T // P
NB = 3
BW = T // NB
TB = BW // P
NH = 4
DK = 128
DV = 256
VW = DV + 1
DFF = 2816
NF = DFF // P
NC = NF // 2
ROW = 64
WINDOWS = (2, 4, 8, 16)
EPS = 1e-6
QSCALE = DK ** -0.5
NEG = -1e30

CQ, CK, CV, CO = 0, 512, 1024, 2048
CG, CU, CGA, CGB = 3072, 3088, 3600, 4624
GR = 36

V_BADA, V_GPM, V_GQM, V_GPF, V_GQF, V_GH, V_PS, V_C = 0, 48, 56, 64, 72, 80, 88, 92
V_W0, V_W1, V_W2, V_CB = 108, 152, 196, 240
NV = 284

H_ID, H_SEL, H_MASK, H_POOL = 0, 128, 128 + 8 * 128, 128 + 10 * 128
H_COLS = H_POOL + 8 * 128


def shape_constants():
    out = np.zeros((P, H_COLS), np.float32)
    out[:, H_ID:H_ID + P] = np.eye(P)
    for d in range(2):
        for h in range(NH):
            r = 32 * d + h
            for row in (r, 64 + r):
                out[row, H_SEL + (d * NH + h) * P:H_SEL + (d * NH + h + 1) * P] = 1.0
    s, t = np.arange(P)[:, None], np.arange(P)[None, :]
    out[:, H_MASK:H_MASK + P] = np.where(s <= t, 0.0, NEG)
    out[:, H_MASK + P:H_MASK + 2 * P] = np.where(s >= t, 0.0, NEG)
    for g, win in enumerate(WINDOWS):
        for kind, cols in enumerate((CTX, ROW)):
            m = np.zeros((P, P), np.float32)
            for tok in range(P):
                row, c = tok // cols, tok % cols
                lo, hi = max(c - win // 2, 0), min(c + win // 2, cols)
                m[row * cols + lo:row * cols + hi, tok] = np.float32(1.0) / np.float32(hi - lo)
                m[tok, tok] -= 1.0
            at = H_POOL + (2 * g + kind) * P
            out[:, at:at + P] = m
    return out


def plan():
    rest = [("o", j) for j in range(8)] + [("ga", j) for j in range(8)] + [("gb", j) for j in range(8)]
    mains = [("gates", 0)] + [("u", g) for g in range(4)]
    mains += [("v", 0), ("v", 1), ("q", 0), ("k", 0)]
    seg_start = len(mains)
    for h in range(NH):
        seg = []
        if h + 1 < NH:
            seg += [("v", 2 * h + 2), ("v", 2 * h + 3), ("q", h + 1), ("k", h + 1)]
            seg += rest[:5]
            rest = rest[5:]
        else:
            seg += rest
        mains += seg
    return mains, seg_start


def build(nc, x_prompt, x_sample, state_C, state_n, state_m, c, c_ctx, w_ada, b_ada, g_pre_mix, g_post_mix,
          g_pre_ffn, g_post_ffn, w_in, b_gates, g_head, w_pool, pool_scale, w_br_a, w_br_b, w_out, w_up,
          conv_w, conv_b, w_down, consts, y_prompt, y_sample, new_C, new_n, new_m):
    mains, SEG = plan()
    NM = len(mains)
    SEG_P = SEG + NT * (NH - 1) + 3
    RS = 3
    LS = 5
    ADA0 = 16

    S_BR = NM
    S_YA = S_BR + 8
    S_OUT = S_YA + 8
    S_FF = S_OUT + 8
    n_units = S_FF + 4 + 6 * (NC - 1) + 2
    raw_items = []
    for s in range(1, NM):
        raw_items.append(("unit", s))
        if s <= 48 - ADA0:
            raw_items.append(("ada", ADA0 + s - 1))
    for s in range(S_BR, S_FF):
        raw_items.append(("unit", s))
    raw_of = {it: n for n, it in enumerate(raw_items)}
    N_FF = len(raw_items)

    def raw_n(s):
        return raw_of[("unit", s)] if s < S_FF else N_FF + s - S_FF

    uses = []
    use_of = {}
    for m, (kind, idx) in enumerate(mains):
        if m >= SEG and (m - SEG) % 9 == 1 and m - SEG > 9:
            h = (m - SEG) // 9 - 1
            for j in range(2):
                use_of[("hm", 2 * h + j)] = len(uses)
                uses.append("hm")
        use_of[("main", m)] = len(uses)
        uses.append(kind)
        if kind == "u":
            for st in range(2):
                use_of[("pool", idx, st)] = len(uses)
                uses.append("pool")
        if m and mains[m - 1][0] == "v":
            use_of[("turn", mains[m - 1][1])] = len(uses)
            uses.append("turn")
    for j in range(2):
        use_of[("hm", 2 * (NH - 1) + j)] = len(uses)
        uses.append("hm")
    Q_P1 = 3 * len(uses)
    U_YA = len(uses)
    U_OUT = U_YA + 8
    Q_N2 = 3 * (U_OUT + 8)
    Q_FF = Q_N2 + 24

    def unit_done_q(s):
        if s < NM:
            return 3 * use_of[("main", s)] + 3
        if s < S_OUT:
            return None
        return 3 * (U_OUT + s - S_OUT) + 3

    base = [(nc.sbuf_base + 63) // 64 * 64]

    def place(name, shape, dt=F32, at=None):
        size = int(np.prod(shape[1:])) * (2 if dt == BF16 else 4)
        off = base[0] if at is None else at
        if at is None:
            base[0] += (size + 31) // 32 * 32
        return nc.alloc_sbuf_tensor_at(name, shape, dt, offset=off)

    ident = place("ident", [P, P])
    vT = place("vT", [P, NV])
    modT = place("modT", [P, 48, 2])
    condT = place("condT", [P, 2, KD])
    coefA1 = place("coefA1", [P, KD, 2])
    coefA2 = place("coefA2", [P, KD, 2])
    coefG1 = place("coefG1", [P, KD, 2])
    coefG2 = place("coefG2", [P, KD, 2])
    stat = place("stat", [P, 4, NT])
    hstat = place("hstat", [P, 2, NT])
    taps = place("taps", [P, 2, 6])
    dsm = place("dsm", [P, 8])
    HH0 = base[0]
    H_hi = place("H_hi", [P, KD, T], F32R)
    H_lo = place("H_lo", [P, KD, T], F32R)
    ring_hi = place("ring_hi", [P, RS, 1024], F32R)
    ring_lo = place("ring_lo", [P, RS, 1024], F32R)
    raw = place("raw", [P, RS, 1024])
    R = base[0]
    qT, kT, vaug, hm = [None, None], [None, None], [None, None], [None, None]
    for i in range(2):
        base_of_head1 = base[0]
        qT[i] = place(f"qT{i}", [P, T])
        kT[i] = place(f"kT{i}", [P, T])
        vaug[i] = place(f"vaug{i}", [P, NT, VW])
        if i == 0:
            SC0 = base[0]
            sc = [place(f"sc{j}", [P, T]) for j in range(2)]
        HM1 = base[0]
        hm[i] = place(f"hm{i}", [P, NT, DV])
    stage = [place(f"stage{i}", [P, T]) for i in range(2)]
    base_of_gates = base[0]
    GS = place("GS", [P, T], F32R)
    YS = place("YS", [P, T], F32R)
    a_tok = place("a_tok", [P, NT, 2, NH])
    en_tok = place("en_tok", [P, NT, 2, NH])
    ST0 = base[0]
    Cst = place("Cst", [P, 2, VW])
    Cctx = place("Cctx", [P, 2, VW])
    AT0 = base[0]
    Wt = place("Wt", [P, 2, P])
    Et = place("Et", [P, 2, P])
    Pt = place("Pt", [P, 2, P])
    kw = place("kw", [P, 2, P])
    qs = place("qs", [P, 2, P])
    sel = place("sel", [P, 8, P], F32R)
    idbf = place("idbf", [P, P], BF16)
    maskbf = place("maskbf", [P, 2, P], BF16)
    assert base[0] <= nc.sbuf_usable_end, (base[0], nc.sbuf_usable_end)
    adaw = place("adaw", [P, ADA0 // 2, KD, 2 * P], at=HH0)
    X0 = place("X0", [P, NT, DM], at=R)
    Gt = [place(f"Gt{r}", [P, T], at=(R if r < 4 else base_of_head1) + (r % 4) * 4 * T) for r in range(8)]
    vecs = place("vecs", [P, 3, P], at=AT0 + 2048)
    tsc = place("tsc", [P, 4, BW], at=base_of_head1)
    reset = place("reset", [P, T], at=ST0)
    wgate = place("wgate", [P, KD, 16], at=ST0 + 4 * T)
    gbias = place("gbias", [P, 2], at=ST0 + 4 * T + 512)
    m0t = place("m0t", [P, 1], at=ST0 + 4 * T + 544)
    mprev = place("mprev", [P, NT], at=ST0 + 4 * T + 576)
    poolM = place("poolM", [P, 8, P], at=HM1)
    mask32 = place("mask32", [P, 2 * P], at=HM1 + 6144)
    wpool = place("wpool", [P, 4, P], at=HM1 + 4096)
    pT_hi = place("pT_hi", [P, 4, T], F32R, at=R)
    pF = place("pF", [P, 4, T], at=SC0)
    pT_lo = place("pT_lo", [P, 4, T], F32R, at=SC0)
    mixF = place("mixF", [P, KD, T], at=SC0 + 16 * T)
    LD0 = base_of_gates
    ld = place("ld", [P, LS, T], at=LD0)
    assert SC0 + 16 * T == base_of_head1 and SC0 + 48 * T <= LD0 and LD0 + 4 * LS * T <= nc.sbuf_usable_end
    yT = place("yT", [P, KD, T], at=R)
    X1 = place("X1", [P, NT, DM], at=SC0 + 16 * T)
    gtb1 = place("gtb1", [P, 2, DM], at=LD0)
    xld = place("xld", [P, 2, DM], at=LD0 + 8192)
    tsc2 = place("tsc2", [P, 4, BW], at=LD0 + 16 * T)
    acc = place("acc", [P, NT, DM], at=R)
    FF0 = R + 4 * NT * DM
    fT_hi = place("fT_hi", [P, 2, 2, T], F32R, at=FF0)
    fT_lo = place("fT_lo", [P, 2, 2, T], F32R, at=FF0 + 16 * T)
    cg = place("cg", [P, T], at=FF0 + 32 * T)
    cv = place("cv", [P, T], at=FF0 + 36 * T)
    x1ld = place("x1ld", [P, 2, DM], at=FF0 + 32 * T)
    gtb2 = place("gtb2", [P, 2, DM], at=FF0 + 40 * T)
    assert FF0 + 40 * T + 8192 <= nc.sbuf_usable_end

    ps = nc.alloc_psum_tensor("ps", [P, 8, 512], F32)

    Z = {k: nc.dram_tensor("z_" + k, (n, P, T), F32, kind="Internal").ap()
         for k, n in (("o", 8), ("ga", 8), ("gb", 8), ("hm", 8), ("pool", 4))}
    x1_dram = nc.dram_tensor("z_x1", (NT, P, DM), F32, kind="Internal").ap()

    S = lambda name: nc.alloc_semaphore(name)
    s_id, s_cst, s_vec, s_wg = S("s_id"), S("s_cst"), S("s_vec"), S("s_wg")
    s_x = [S(f"s_x{b}") for b in range(NB)]
    ada_in = [S(f"ada_in{j}") for j in range(ADA0 // 2)]
    xt_done, xt_free = S("xt_done"), S("xt_free")
    landed = [S(f"landed{i}") for i in range(RS)]
    hi_ready, lo_ready, ada_used = S("hi_ready"), S("lo_ready"), S("ada_used")
    done0, evac0 = S("done0"), S("evac0")
    done1, evac1 = S("done1"), S("evac1")
    done2, evac2 = S("done2"), S("evac2")
    act_seq, dve_seq, pool_seq = S("act_seq"), S("dve_seq"), S("pool_seq")
    vec_done, cond_done, ada0_done, coef1 = S("vec_done"), S("cond_done"), S("ada0_done"), S("coef1")
    ss_done, rt_done, x_scaled = S("ss_done"), S("rt_done"), S("x_scaled")
    t_done, tl_done = S("t_done"), S("tl_done")
    g_lf, g_ready, g_pe, g_tok = S("g_lf"), S("g_ready"), S("g_pe"), S("g_tok")
    ones_done = S("ones_done")
    attB = S("attB")
    attA, attX, attP, attN, attC = S("attA"), S("attX"), S("attP"), S("attN"), S("attC")
    c_in, c_out = S("c_in"), S("c_out")
    hss, hrt, hscaled = S("hss"), S("hrt"), S("hscaled")
    stored = [S("stored0"), S("stored1")]
    ld_in = [S(f"ld_in{i}") for i in range(LS)]
    pf_in, p_hi, p_lo = S("pf_in"), S("p_hi"), S("p_lo")
    ld_used = S("ld_used")
    sgm, hmx, hmhi = S("sgm"), S("hmx"), S("hmhi")
    mixed, mixhi, mix_ready = S("mixed"), S("mixhi"), S("mix_ready")
    coef2, gtb_pe, gtb_done = S("coef2"), S("gtb_pe"), S("gtb_done")
    x_in = [S("x_in0"), S("x_in1")]
    x1_ready, x1_stored = S("x1_ready"), [S("x1s0"), S("x1s1")]
    ss2, rt2, vv2 = S("ss2"), S("rt2"), S("vv2")
    acc_zero = S("acc_zero")
    conv_a, conv_g, gel, conv_v, fhi, f_ready = S("conv_a"), S("conv_g"), S("gel"), S("conv_v"), S("fhi"), S("f_ready")
    dve_ff, fin_ss, fin_rt, fin_m, fin_o = S("dve_ff"), S("fin_ss"), S("fin_rt"), S("fin_m"), S("fin_o")
    x1_in = [S("x1_in0"), S("x1_in1")]
    s_out = S("s_out")
    taps_done = S("taps_done")
    s_outn = [S("s_outA"), S("s_outB")]

    def tile_cols(w, kt, c0):
        return w.rearrange("(k p) c -> p k c", p=P)[:, 0:kt, c0:c0 + P]

    cols_of = {"q": CQ, "k": CK, "v": CV, "o": CO, "u": CU, "ga": CGA, "gb": CGB}

    def unit_source(s):
        if s < NM:
            kind, idx = mains[s]
            return tile_cols(w_in[0], KD, cols_of[kind] + idx * P), KD
        if s < S_YA:
            return tile_cols(w_br_b[0], 4, (s - S_BR) * P), 4
        if s < S_OUT:
            return tile_cols(w_br_a[0], KD, (s - S_YA) * P), KD
        return tile_cols(w_out[0], KD, (s - S_OUT) * P), KD

    def unit_width(s):
        return 512 if S_BR <= s < S_YA else 1024

    w_up_t = w_up[0].rearrange("(k p) f -> p k f", p=P)

    def lin(at, step, i):
        return at if i is None else i * step + at

    def row_parts(b):
        return [(0, 1, CTX), (CTX, (BW - CTX) // ROW, ROW)] if b == 0 else [(0, BW // ROW, ROW)]

    def put_out(eng, t):
        eng.wait_ge(fin_o, t + 1)
        dst = y_prompt[0] if t == 0 else y_sample[0, (t - 1) * P:t * P, :]
        eng.dma_start(dst, acc[:, t, :]).then_inc(s_outn[t % 2], 16)

    def stage_order():
        out = []
        for m, (kind, idx) in enumerate(mains):
            if m >= SEG and (m - SEG) % 9 == 1 and m - SEG > 9:
                h = (m - SEG) // 9 - 1
                out += [("hm", 2 * h), ("hm", 2 * h + 1)]
            if kind in ("o", "ga", "gb"):
                out.append((kind, idx))
            if kind == "u":
                out.append(("pool", idx))
        return out + [("hm", 2 * NH - 2), ("hm", 2 * NH - 1)]

    stage_no = {it: w for w, it in enumerate(stage_order())}

    def n_stage():
        return len(stage_no)

    NORM_AFTER = (4, 7, 8)

    def gate_rows(pe, coef, g0):
        pe.wait_ge(coef2, 1)
        for cond in range(2):
            if g0 + cond:
                pe.wait_ge(gtb_done, g0 + cond)
            for k in range(KD):
                mm = pe.matmul(ps[:, 6 + k // 4, (k % 4) * P:(k % 4 + 1) * P],
                               coef[:, k, cond:cond + 1].to_broadcast([P, P]), ident[:, :], start=True, stop=True)
            mm.then_inc(gtb_pe, 1)

    def vcol(col, i):
        return vT[:, col:col + 1] if i is None else vT[:, bass.ds(i * 4 + col, 1)]

    def evac_q(act, q0, dst, scale, exps, done, evac, ps_):
        for b in range(NB):
            act.wait_ge(done, q0 + b + 1)
            kw_ = {} if scale is None else {"scale": scale}
            act.activation(dst[:, b * BW:(b + 1) * BW], ps_[:, b, 0:BW], ACT.Copy, **kw_).then_inc(evac, 1)
            if b == 0:
                exps()

    def free_slot(eng, s):
        p = s - RS
        if p < 0:
            return
        if p < S_BR or p >= S_OUT:
            eng.wait_ge(done0, unit_done_q(p))
        elif p < S_YA:
            eng.wait_ge(done1, 3 * (p - S_BR + 1))
        else:
            eng.wait_ge(done0, 3 * (U_YA + p - S_YA + 1))

    with nc.Block() as block:
        @block.sync
        def _(sp):
            sp.dma_start(ident[:, :], consts[:, H_ID:H_ID + P]).then_inc(s_id, 16)
            vecA = [b_ada[0], g_pre_mix[0], g_post_mix[0], g_pre_ffn[0], g_post_ffn[0],
                    g_head[0].rearrange("h v -> (h v)"), pool_scale[0], c_ctx, c[0]]
            at = 0
            for v in vecA:
                n = v.shape[0] // P
                sp.dma_start(vecs[at:at + n, 0, :], v.rearrange("(r p) -> r p", p=P)).then_inc(s_vec, 16)
                at += n
            for j, o, v in ((1, 0, conv_w[0, 0]), (1, 44, conv_w[0, 1]), (2, 0, conv_w[0, 2]), (2, 44, conv_b[0])):
                sp.dma_start(vecs[o:o + 44, j, :], v.rearrange("(r p) -> r p", p=P)).then_inc(s_vec, 16)

            def x_load(b):
                if b == 0:
                    sp.dma_start(X0[:, 0, :], x_prompt[0]).then_inc(s_x[0], 16)
                t0 = max(b * TB, 1)
                rows = x_sample[0, (t0 - 1) * P:((b + 1) * TB - 1) * P, :]
                sp.dma_start(X0[:, t0:(b + 1) * TB, :], rows.rearrange("(t p) d -> p t d", p=P)).then_inc(s_x[b], 16)

            x_load(0)
            x_load(1)
            for j in range(ADA0 // 2):
                src = w_ada[0].rearrange("(k p) c -> p k c", p=P)[:, :, j * 2 * P:(j + 1) * 2 * P]
                sp.dma_start(adaw[:, j, :, :], src).then_inc(ada_in[j], 16)
            x_load(2)
            sp.dma_start(stage[1][:, 0:8 * P], consts[:, H_SEL:H_SEL + 8 * P]).then_inc(s_cst, 16)
            sp.dma_start(mask32[:, :], consts[:, H_MASK:H_MASK + 2 * P]).then_inc(s_cst, 16)

            for n, it in enumerate(raw_items):
                if n >= RS:
                    prev = raw_items[n - RS]
                    if prev[0] == "ada":
                        sp.wait_ge(ada_used, prev[1] + 1)
                    else:
                        sp.wait_ge(lo_ready, prev[1] + 1)
                if it[0] == "ada":
                    src, kt = tile_cols(w_ada[0], KD, it[1] * P), KD
                else:
                    src, kt = unit_source(it[1])
                sp.dma_start(raw[:, n % RS, 0:kt * P].rearrange("p (k c) -> p k c", c=P), src)\
                  .then_inc(landed[n % RS], 16)

            def ff_load(j, i, src, by_tile):
                n0 = N_FF + j
                sp.wait_ge(lo_ready, lin(S_FF + j - RS + 1, 12, i))
                dst = raw[:, n0 % RS, :]
                if by_tile:
                    dst = dst.rearrange("p (k c) -> p k c", c=P)
                sp.dma_start(dst, src).then_inc(landed[n0 % RS], 16)

            def up_src(f, i, half):
                if i is None:
                    return w_up_t[:, :, f * P + half * DFF:(f + 1) * P + half * DFF]
                return w_up_t[:, :, bass.ds(i * (4 * P) + (f * P + half * DFF), P)]

            def down_src(f, i):
                if i is None:
                    return w_down[0][f * P:(f + 1) * P, :]
                return w_down[0][bass.ds(i * (4 * P) + f * P, P), :]

            for j in range(4):
                ff_load(j, None, up_src(j // 2, None, j % 2), True)
            with sp.Fori(0, (NC - 1) // 2) as i:
                for cc in range(2):
                    for j in range(4):
                        ff_load(4 + 6 * cc + j, i, up_src(2 + 2 * cc + j // 2, i, j % 2), True)
                    for j in range(2):
                        ff_load(8 + 6 * cc + j, i, down_src(2 * cc + j, i), False)
            for j in range(2):
                ff_load(4 + 6 * (NC - 1) + j, None, down_src(NF - 2 + j, None), False)
            for d in range(2):
                sp.wait_ge(s_outn[d], 16 * ((NT + 1 - d) // 2))
            sp.wait_ge(c_out, 16 * 4 * NH)
            sp.wait_ge(s_out, 32)

        @block.gpsimd
        def _(pool):
            rr = reset[:, :].rearrange("p (t s) -> p t s", s=P)
            fills = ((reset[:, :], 1.0), (rr[0:4, :, 0:1], 0.0), (rr[32:36, :, P - 1:P], 0.0), (gbias[:, :], 0.0),
                     (m0t[:, :], 0.0), (mprev[:, :], 0.0))
            for n, (out, value) in enumerate(fills):
                pool.memset(out, value).then_inc(pool_seq, 1)
                pool.wait_ge(pool_seq, n + 1)
            bg = b_gates[0].rearrange("(r c) -> r c", c=1)
            for d in range(2):
                pool.dma_start(gbias[32 * d:32 * d + 4, 0:1], bg[4 * d:4 * d + 4, :]).then_inc(s_wg, 16)
                pool.dma_start(gbias[32 * d:32 * d + 4, 1:2], bg[8 + 4 * d:12 + 4 * d, :]).then_inc(s_wg, 16)
                pool.dma_start(m0t[32 * d:32 * d + 4, :], state_m[0, 0, d].rearrange("(r c) -> r c", c=1)).then_inc(s_wg, 16)
            pool.dma_start(wgate[:, :, :], w_in[0].rearrange("(k p) c -> p k c", p=P)[:, :, CG:CG + 16]).then_inc(s_wg, 16)
            pool.dma_start(poolM[:, :, :], consts[:, H_POOL:H_POOL + 8 * P].rearrange("p (m c) -> p m c", c=P)).then_inc(s_wg, 16)
            pool.dma_start(wpool[:, :, :], w_pool[0].rearrange("g c d -> c g d")).then_inc(s_wg, 16)
            pool.wait_ge(g_ready, 1)
            nm = new_m[0, 0]
            pool.dma_start(nm[0].rearrange("(r c) -> r c", c=1), Gt[4][0:4, CTX - 1:CTX]).then_inc(s_out, 16)
            pool.dma_start(nm[1].rearrange("(r c) -> r c", c=1), Gt[4][32:36, 0:1]).then_inc(s_out, 16)
            for h in range(NH):
                if h:
                    pool.wait_ge(attN, 18 * h)
                for d in range(2):
                    pool.dma_start(Cst[:, d, 0:DV], state_C[0, 0, d, h]).then_inc(c_in, 16)
                    pool.dma_start(Cst[:, d, DV:VW], state_n[0, 0, d, h].rearrange("(r c) -> r c", c=1)).then_inc(c_in, 16)
                pool.wait_ge(attC, 18 * h + 2)
                for d in range(2):
                    pool.dma_start(new_C[0, 0, d, h], Cctx[:, d, 0:DV]).then_inc(c_out, 16)
                    pool.dma_start(new_n[0, 0, d, h].rearrange("(r c) -> r c", c=1), Cctx[:, d, DV:VW]).then_inc(c_out, 16)

                if h == NH - 1:
                    pool.wait_ge(evac0, 3 * use_of[("hm", 2 * (NH - 2) + 1)] + 3)
                    for g in range(4):
                        w = stage_no[("pool", g)]
                        pool.wait_ge(stored[w % 2], 16 * (w // 2 + 1))
                        pool.dma_start(pF[:, g, :], Z["pool"][g]).then_inc(pf_in, 16)

            pool.wait_ge(attN, 2 * NT * NH)
            pool.wait_ge(attC, 2 * NT * NH)
            pool.wait_ge(c_out, 16 * 4 * NH)
            pool.wait_ge(s_out, 32)
            loads = []
            for d in range(KD):
                loads += [("gb", d), ("o", d), ("hm", d)]
            loads += [("ga", d) for d in range(KD)]
            for w, (what, d) in enumerate(loads):
                n = stage_no[(what, d)]
                pool.wait_ge(stored[n % 2], 16 * (n // 2 + 1))
                if w >= LS:
                    last, e = loads[w - LS]
                    if last == "gb":
                        pool.wait_ge(evac1, NB * (e + 1))
                    elif last == "o":
                        pool.wait_ge(hmx, e + 1)
                    elif last == "hm":
                        pool.wait_ge(ld_used, e + 1)
                    else:
                        pool.wait_ge(ld_used, KD + e + 1)
                pool.dma_start(ld[:, w % LS, :], Z[what][d]).then_inc(ld_in[w % LS], 16)
            pool.wait_ge(ld_used, 2 * KD)
            for t in range(NT):
                if t >= 2:
                    pool.wait_ge(ss2, 2 * (t - 2) + 2)
                src = x_prompt[0] if t == 0 else x_sample[0, (t - 1) * P:t * P, :]
                pool.dma_start(xld[:, t % 2, :], src).then_inc(x_in[t % 2], 16)
                if t >= 1:
                    pool.wait_ge(x1_ready, t)
                    pool.dma_start(x1_dram[t - 1], X1[:, t - 1, :]).then_inc(x1_stored[(t - 1) % 2], 16)
            pool.wait_ge(x1_ready, NT)
            pool.dma_start(x1_dram[NT - 1], X1[:, NT - 1, :]).then_inc(x1_stored[(NT - 1) % 2], 16)
            pool.wait_ge(done2, NT)
            pool.memset(acc[:, :, :], 0.0).then_inc(acc_zero, 1)
            pool.wait_ge(f_ready, 3 * NF)
            def x1_load(t):
                pool.dma_start(x1ld[:, t % 2, :], x1_dram[t]).then_inc(x1_in[t % 2], 16)

            x1_load(0)
            x1_load(1)
            for t in range(NT):
                pool.wait_ge(fin_m, t + 1)
                pool.wait_ge(x1_in[t % 2], 16 * (t // 2 + 1))
                pool.tensor_tensor(acc[:, t, :], acc[:, t, :], x1ld[:, t % 2, :], ALU.add).then_inc(fin_o, 1)
                put_out(pool, t)
                if t + 2 < NT:
                    x1_load(t + 2)

        @block.tensor
        def _(pe):
            def take0(q):
                if q >= 3:
                    pe.wait_ge(evac0, q - 2)

            def mm3(out, whi, wlo, xhi, xlo, first, last):
                pe.matmul(out, whi, xhi, start=first, stop=False)
                pe.matmul(out, whi, xlo, start=False, stop=False)
                return pe.matmul(out, wlo, xhi, start=False, stop=last)

            def block_product(out, s, b, kt, xhi, xlo, pieces=None):
                r = s % RS
                for k in range(kt):
                    w = slice(k * P, (k + 1) * P)
                    tok = slice(b * BW, (b + 1) * BW)
                    mm = mm3(out, ring_hi[:, r, w], ring_lo[:, r, w], xhi[:, k, tok], xlo[:, k, tok], k == 0, k == kt - 1)
                return mm

            pe.wait_ge(s_id, 16)
            pe.wait_ge(s_vec, 16 * 13)
            pe.transpose(ps[:, 3, 0:108], vecs[0:108, 0, :], ident[0:108, 0:108])
            pe.transpose(ps[:, 3, 108:196], vecs[0:88, 1, :], ident[0:88, 0:88])
            pe.transpose(ps[:, 3, 196:284], vecs[0:88, 2, :], ident[0:88, 0:88]).then_inc(vec_done, 1)

            def ada_tile(a, bank, col):
                if a < ADA0:
                    pe.wait_ge(ada_in[a // 2], 16)
                    w = lambda k: adaw[:, a // 2, k, (a % 2) * P:(a % 2 + 1) * P]
                else:
                    n = raw_of[("ada", a)]
                    pe.wait_ge(landed[n % RS], 16 * (n // RS + 1))
                    w = lambda k: raw[:, n % RS, k * P:(k + 1) * P]
                for k in range(KD):
                    mm = pe.matmul(ps[:, bank, col:col + 2], w(k), condT[:, :, k], start=(k == 0), stop=(k == KD - 1))
                mm.then_inc(ada_used, 1)

            def norm_turn(Xt, out, b, k):
                for j in range(TB):
                    mm = pe.transpose(out[:, j * P:(j + 1) * P], Xt[:, b * TB + j, k * P:(k + 1) * P], ident[:, :])
                return mm

            def norm_block(Xt, q0, b, ready):
                pe.wait_ge(x_scaled, ready)
                for k in range(KD):
                    q = q0 + b * KD + k
                    take0(q)
                    norm_turn(Xt, ps[:, q % 3, :], b, k).then_inc(done0, 1)

            def first_norm(b, k):
                w = b * KD + k
                if w >= 4:
                    pe.wait_ge(xt_free, w - 3)
                norm_turn(X0, ps[:, 3 + w % 4, :], b, k).then_inc(xt_done, 1)

            pe.wait_ge(cond_done, 1)
            for a in range(ADA0):
                ada_tile(a, 7, 2 * a)
            pe.wait_ge(x_scaled, TB)
            for k in range(KD):
                first_norm(0, k)
            pe.wait_ge(lo_ready, 1)
            for b in range(NB):
                if b + 1 < NB:
                    pe.wait_ge(x_scaled, TB * (b + 2))
                for k in range(KD):
                    if b + 1 < NB:
                        first_norm(b + 1, k)
                    pe.wait_ge(tl_done, b * KD + k + 1)
                    w = slice(k * P, (k + 1) * P)
                    tok = slice(b * BW, (b + 1) * BW)
                    mm = mm3(ps[:, b, 0:BW], ring_hi[:, 0, w], ring_lo[:, 0, w], H_hi[:, k, tok], H_lo[:, k, tok],
                             k == 0, k == KD - 1)
                mm.then_inc(done0, 1)

            def attention_scores(h, i):
                e = h * 9 + i
                cf, cb = (0, 0) if i == 0 else (i, NT - i)
                v = h % 2
                if i == 0:
                    mk = mains.index(("k", h))
                    pe.wait_ge(evac0, 3 * use_of[("main", mk)] + 3)
                    if h == 0:
                        pe.wait_ge(g_tok, 1)
                if e:
                    pe.wait_ge(attP, e)
                for d, cx in ((0, cf), (1, cb)):
                    tok = slice(cx * P, (cx + 1) * P)
                    j = d * NH + h
                    o = d * P
                    pe.matmul(ps[:, 3, o:o + P], idbf[:, :], maskbf[:, d, :], start=True, stop=False)
                    pe.matmul(ps[:, 3, o:o + P], sel[:, j, :], GS[:, tok], start=False, stop=True)
                    pe.matmul(ps[:, 3, 256 + o:256 + o + P], sel[:, j, :], YS[:, tok], start=True, stop=True)
                    pe.matmul(ps[:, 4, o:o + P], kT[v][:, tok], qT[v][:, tok], start=True, stop=True)
                    mm = pe.transpose(ps[:, 4, 256 + o:256 + o + P], kT[v][:, tok], ident[:, :])
                mm.then_inc(attA, 1)

            def attention_values(h, i, d):
                e = h * 9 + i
                cx = 0 if i == 0 else (i, NT - i)[d]
                v = h % 2
                pe.wait_ge(attP, e + 1)
                if i == 0 and d == 0:
                    pe.wait_ge(evac0, 3 * use_of[("turn", 2 * h + 1)] + 3)
                    if h == 0:
                        pe.wait_ge(ones_done, 1)
                if i == 1 and d == 0:
                    pe.wait_ge(c_in, 64 * (h + 1))
                if e or d:
                    pe.wait_ge(attN, 2 * e + d)
                    pe.wait_ge(attC, 2 * e + d)
                pe.matmul(ps[:, 5 + d, 0:VW], Pt[:, d, :], vaug[v][:, cx, :], start=True, stop=(i == 0))
                if i:
                    pe.matmul(ps[:, 5 + d, 0:VW], qs[:, d, :], Cst[:, d, :], start=False, stop=True)
                pe.matmul(ps[:, 7, 0:VW], kw[:, d, :], vaug[v][:, cx, :], start=True, stop=True).then_inc(attB, 1)

            def turn(src, n_src, q0):
                for b in range(NB):
                    take0(q0 + b)
                    for j in range(TB):
                        mm = n_src(ps[:, b, j * P:(j + 1) * P], b * TB + j)
                    mm.then_inc(done0, 1)

            def hm_turn(h):
                pe.wait_ge(hscaled, h + 1)
                for j in range(2):
                    turn(None, lambda o, t, j=j: pe.transpose(o, hm[h % 2][:, t, j * P:(j + 1) * P], ident[:, :]),
                         3 * use_of[("hm", 2 * h + j)])

            for m, (kind, idx) in enumerate(mains):
                seg = m - SEG
                if seg > 9 and seg % 9 == 1:
                    hm_turn(seg // 9 - 1)
                q0 = 3 * use_of[("main", m)]
                if m == 0:
                    continue
                take0(q0)
                if 1 <= m <= 48 - ADA0:
                    ada_tile(ADA0 + m - 1, 0, 400)
                pe.wait_ge(lo_ready, m + 1)
                for b in range(NB):
                    take0(q0 + b)
                    block_product(ps[:, b, 0:BW], m, b, KD, H_hi, H_lo).then_inc(done0, 1)
                    if seg >= 0:
                        if b == 0:
                            attention_scores(seg // 9, seg % 9)
                        else:
                            attention_values(seg // 9, seg % 9, b - 1)
                if kind == "u":
                    if idx == 0:
                        pe.wait_ge(s_wg, 16 * 9)
                    u_in = 3 * use_of[("main", m)]
                    pe.wait_ge(evac0, u_in + 3)
                    turn(None, lambda o, t: pe.matmul(o, sc[0][:, t * P:(t + 1) * P], wpool[:, idx, :], start=True, stop=True),
                         3 * use_of[("pool", idx, 0)])
                    pe.wait_ge(evac0, 3 * use_of[("pool", idx, 0)] + 3)
                    turn(None, lambda o, t: pe.matmul(o, sc[1][:, t * P:(t + 1) * P], poolM[:, 2 * idx + (t > 0), :],
                                                      start=True, stop=True),
                         3 * use_of[("pool", idx, 1)])
                if m and mains[m - 1][0] == "v":
                    vi = mains[m - 1][1]
                    pe.wait_ge(evac0, 3 * use_of[("main", m - 1)] + 3)
                    turn(None, lambda o, t: pe.transpose(o, sc[vi % 2][:, t * P:(t + 1) * P], ident[:, :]),
                         3 * use_of[("turn", vi)])
                if m == 2:
                    pe.wait_ge(g_ready, 1)
                    for t in range(NT):
                        pe.transpose(ps[:, 3, t * GR:(t + 1) * GR], Gt[6][0:GR, t * P:(t + 1) * P], ident[0:GR, 0:GR])
                    for t in range(NT):
                        mm = pe.transpose(ps[:, 4, t * GR:(t + 1) * GR], Gt[4][0:GR, t * P:(t + 1) * P], ident[0:GR, 0:GR])
                    mm.then_inc(g_pe, 1)
            for d in range(KD):
                s = S_BR + d
                if d == 0:
                    pe.wait_ge(p_lo, 4)
                    pe.wait_ge(attN, 2 * NT * NH)
                pe.wait_ge(lo_ready, s + 1)
                for b in range(NB):
                    if d:
                        pe.wait_ge(evac1, 3 * (d - 1) + b + 1)
                    block_product(ps[:, 3 + b, 0:BW], s, b, 4, pT_hi, pT_lo).then_inc(done1, 1)
                if d == 1:
                    hm_turn(NH - 1)
            for d in range(KD):
                s = S_YA + d
                pe.wait_ge(lo_ready, s + 1)
                for b in range(NB):
                    take0(3 * (U_YA + d) + b)
                    r = s % RS
                    for k in range(KD):
                        if d == 0 and b == 0:
                            pe.wait_ge(ld_used, k + 1)
                        w = slice(k * P, (k + 1) * P)
                        tok = slice(b * BW, (b + 1) * BW)
                        mm = mm3(ps[:, b, 0:BW], ring_hi[:, r, w], ring_lo[:, r, w], H_hi[:, k, tok], H_lo[:, k, tok],
                                 k == 0, k == KD - 1)
                    mm.then_inc(done0, 1)
            for d in range(KD):
                s = S_OUT + d
                pe.wait_ge(lo_ready, s + 1)
                for b in range(NB):
                    q = 3 * (U_OUT + d) + b
                    take0(q)
                    r = s % RS
                    for k in range(KD):
                        if d == 0:
                            pe.wait_ge(mix_ready, b * KD + k + 1)
                        w = slice(k * P, (k + 1) * P)
                        tok = slice(b * BW, (b + 1) * BW)
                        mm = mm3(ps[:, b, 0:BW], ring_hi[:, r, w], ring_lo[:, r, w], H_hi[:, k, tok], H_lo[:, k, tok],
                                 k == 0, k == KD - 1)
                    mm.then_inc(done0, 1)
                if d == 0:
                    gate_rows(pe, coefG1, 0)

            def tok_turn(t):
                p = 4 + 2 * (t % 2)
                if t >= 2:
                    pe.wait_ge(evac2, t - 1)
                for k in range(KD):
                    mm = pe.transpose(ps[:, p + k // 4, (k % 4) * P:(k % 4 + 1) * P], yT[:, k, t * P:(t + 1) * P], ident[:, :])
                mm.then_inc(done2, 1)

            pe.wait_ge(evac0, Q_N2)
            pe.wait_ge(gtb_done, 2)
            for t in range(NT):
                tok_turn(t)
                if t in NORM_AFTER:
                    b = NORM_AFTER.index(t)
                    norm_block(X1, Q_N2, b, NT + TB * (b + 1))
            gate_rows(pe, coefG2, 2)

            def up_unit(r, bank, done, freed, f, i):
                for b in range(NB):
                    if f >= 1:
                        pe.wait_ge(freed, lin(3 * f + b - 2, 12, i))
                    for k in range(KD):
                        w = slice(k * P, (k + 1) * P)
                        tok = slice(b * BW, (b + 1) * BW)
                        mm = mm3(ps[:, bank + b, 0:BW], ring_hi[:, r, w], ring_lo[:, r, w], H_hi[:, k, tok],
                                 H_lo[:, k, tok], k == 0, k == KD - 1)
                    mm.then_inc(done, 1)

            def up_chunk(j0, f0, i):
                for e in range(2):
                    j = j0 + 2 * e
                    pe.wait_ge(lo_ready, lin(S_FF + j + 1, 12, i))
                    up_unit((S_FF + j) % RS, 0, done0, conv_g, f0 + e, i)
                    pe.wait_ge(lo_ready, lin(S_FF + j + 2, 12, i))
                    up_unit((S_FF + j + 1) % RS, 3, done1, conv_v, f0 + e, i)

            def down_chunk(j0, ch, i):
                pe.wait_ge(lo_ready, lin(S_FF + j0 + 2, 12, i))
                pe.wait_ge(f_ready, lin(6 * (ch + 1), 12, i))
                slot = ch % 2
                for t in range(NT):
                    tok = slice(t * P, (t + 1) * P)
                    for hb in range(2):
                        pe.wait_ge(evac2, lin(NT + 18 * ch + 2 * t + hb - 1, 36, i))
                        cols = slice(hb * 512, (hb + 1) * 512)
                        out = ps[:, 6 + hb, :]
                        for k in range(2):
                            r = (S_FF + j0 + k) % RS
                            pe.matmul(out, fT_hi[:, slot, k, tok], ring_hi[:, r, cols], start=(k == 0), stop=False)
                            pe.matmul(out, fT_hi[:, slot, k, tok], ring_lo[:, r, cols], start=False, stop=False)
                            mm = pe.matmul(out, fT_lo[:, slot, k, tok], ring_hi[:, r, cols], start=False, stop=(k == 1))
                        mm.then_inc(done2, 1)

            pe.wait_ge(tl_done, 48)
            pe.wait_ge(gtb_done, 4)
            up_chunk(0, 0, None)
            with pe.Fori(0, (NC - 1) // 2) as i:
                for cc in range(2):
                    up_chunk(4 + 6 * cc, 2 + 2 * cc, i)
                    down_chunk(8 + 6 * cc, cc, i)
            down_chunk(4 + 6 * (NC - 1), NC - 1, None)

        @block.scalar
        def _(act):
            seq = [0]

            def link(ins):
                seq[0] += 1
                ins.then_inc(act_seq, 1)
                act.wait_ge(act_seq, seq[0])

            def hi_split(s):
                if s >= S_FF:
                    return ff_hi(s - S_FF, None)
                n = raw_n(s)
                w = unit_width(s)
                act.wait_ge(landed[n % RS], 16 * (n // RS + 1))
                free_slot(act, s)
                act.activation(ring_hi[:, s % RS, 0:w], raw[:, n % RS, 0:w], ACT.Copy).then_inc(hi_ready, 1)

            def ff_hi(j, i):
                n0 = N_FF + j
                r = (S_FF + j) % RS
                act.wait_ge(landed[n0 % RS], lin(16 * (n0 // RS + 1), 16 * (12 // RS), i))
                if j < RS:
                    free_slot(act, S_FF + j)
                else:
                    p = j - RS
                    if p < 4:
                        if p % 2:
                            act.wait_ge(done1, lin(3 * KD + 3 * (p // 2 + 1), 12, i))
                        else:
                            act.wait_ge(done0, lin(Q_FF + 3 * (p // 2 + 1), 12, i))
                        if p >= 2 and i is not None:
                            act.wait_ge(done2, lin(NT, 36, i))
                    else:
                        ch, at = 1 + (p - 4) // 6, (p - 4) % 6
                        if at < 4:
                            f = 2 * ch + at // 2
                            act.wait_ge(done1 if at % 2 else done0, lin((3 * KD if at % 2 else Q_FF) + 3 * (f + 1), 12, i))
                        else:
                            act.wait_ge(done2, lin(NT + 18 * ch, 36, i))
                act.activation(ring_hi[:, r, :], raw[:, n0 % RS, :], ACT.Copy).then_inc(hi_ready, 1)

            act.wait_ge(vec_done, 2)
            act.activation(condT[:, :, :], vT[:, V_C:V_C + 16].rearrange("p (c k) -> p c k", c=2), ACT.Silu).then_inc(cond_done, 1)
            for b in range(NB):
                act.wait_ge(s_x[b], 32 if b == 0 else 16)
                tiles = slice(b * TB, (b + 1) * TB)
                for t in range(b * TB, (b + 1) * TB):
                    if t:
                        act.wait_ge(ss_done, t)
                    act.activation(stage[0][:, 0:DM], X0[:, t, :], ACT.Square, accum_out=stat[:, 0, t:t + 1]).then_inc(ss_done, 1)
                act.wait_ge(rt_done, 2 * b + 1)
                act.activation(stat[:, 2, tiles], stat[:, 1, tiles], ACT.Sqrt).then_inc(rt_done, 1)

            def norm_evac(src_of, ready, freed, coefA, sh, n0, tile, b):
                for k in range(KD):
                    w = n0 + b * KD + k
                    ready(b * KD + k)
                    if w - n0 >= 4:
                        act.wait_ge(tl_done, w - 3)
                    parts = [(0, 0, P), (1, P, BW)] if b == 0 else [(1, 0, BW)]
                    for cond, lo, hi in parts:
                        ins = act.activation(tile[:, w % 4, lo:hi], src_of(b * KD + k)[:, lo:hi], ACT.Identity,
                                             scale=coefA[:, k, cond:cond + 1], bias=modT[:, sh + k, cond:cond + 1])
                    ins.then_inc(freed, 1)

            act.wait_ge(coef1, 1)
            for b in range(NB):
                norm_evac(lambda w: ps[:, 3 + w % 4, :], lambda w: act.wait_ge(xt_done, w + 1), xt_free, coefA1, 0, 0, tsc, b)


            def stage_slot(item):
                w = stage_no[item]
                if w >= 2:
                    act.wait_ge(stored[w % 2], 16 * (w // 2))
                return w % 2

            def put(item, q_end):
                w = stage_no[item]
                act.wait_ge(evac0, q_end)
                act.dma_start(Z[item[0]][item[1]], stage[w % 2][:, :]).then_inc(stored[w % 2], 16)

            def evac_copy(q0, dst, scale=None, func=ACT.Copy):
                for b in range(NB):
                    act.wait_ge(done0, q0 + b + 1)
                    out = dst(b)
                    src = ps[:, b, 0:BW]
                    if len(out.shape) == 3:
                        src = src.rearrange("p (t s) -> p t s", s=P)
                    kw_ = {} if scale is None else {"scale": scale}
                    act.activation(out, src, func, **kw_).then_inc(evac0, 1)

            def hm_evac(h):
                for j in range(2):
                    item = ("hm", 2 * h + j)
                    st = stage_slot(item)
                    q0 = 3 * use_of[item]
                    evac_copy(q0, lambda b: stage[st][:, b * BW:(b + 1) * BW])
                    put(item, q0 + 3)

            def hm_norm(h):
                act.wait_ge(attN, 18 * (h + 1))
                for t in range(NT):
                    if t:
                        act.wait_ge(hss, NT * h + t)
                    out = ps[:, 7, 0:DV] if h == NH - 1 else Wt[:, :, :].rearrange("p a b -> p (a b)")
                    act.activation(out, hm[h % 2][:, t, :], ACT.Square,
                                   accum_out=hstat[:, 0, t:t + 1]).then_inc(hss, 1)
                act.wait_ge(hrt, 2 * h + 1)
                act.activation(hstat[:, 1, :], hstat[:, 0, :], ACT.Sqrt).then_inc(hrt, 1)

            hi_split(1)
            for m, (kind, idx) in enumerate(mains):
                seg = m - SEG
                if seg > 9 and seg % 9 == 1:
                    hm_evac(seg // 9 - 1)
                hi_split(m + 2)
                q0 = 3 * use_of[("main", m)]
                if 1 <= m <= 48 - ADA0:
                    j = ADA0 + m - 1
                    act.wait_ge(ada_used, j + 1)
                    act.wait_ge(done0, q0 + 1)
                    act.activation(modT[:, j, :], ps[:, 0, 400:402], ACT.Identity, bias=vT[:, V_BADA + j:V_BADA + j + 1])
                if kind == "gates":
                    act.wait_ge(s_wg, 16 * 9)
                    for b in range(NB):
                        tok = slice(b * BW, (b + 1) * BW)
                        act.wait_ge(done0, q0 + b + 1)
                        act.activation(Gt[0][0:GR, tok], ps[0:GR, b, 0:BW], ACT.Identity, bias=gbias[0:GR, 0:1])
                        act.activation(Gt[1][0:GR, tok], ps[64:64 + GR, b, 0:BW], ACT.Identity, bias=gbias[0:GR, 1:2]).then_inc(evac0, 1)
                    act.wait_ge(evac0, q0 + 3)
                    link(act.activation(Gt[2][0:GR, :], Gt[1][0:GR, :], ACT.Abs))
                    link(act.activation(Gt[2][0:GR, :], Gt[2][0:GR, :], ACT.Exp, scale=-1.0))
                    act.activation(Gt[2][0:GR, :], Gt[2][0:GR, :], ACT.Ln, bias=1.0).then_inc(g_lf, 1)
                    continue
                first = [True]
                if seg >= 0:
                    def exps():
                        h, i = seg // 9, seg % 9
                        e = h * 9 + i
                        cf, cb = (0, 0) if i == 0 else (i, NT - i)
                        act.wait_ge(attA, e + 1)
                        if e:
                            act.wait_ge(attC, 2 * e)
                        for d, cx in ((0, cf), (1, cb)):
                            act.activation(Wt[:, d, :], ps[:, 3, d * P:(d + 1) * P], ACT.Exp, bias=a_tok[:, cx, d, h:h + 1])
                        act.activation(Et[:, :, :], ps[:, 3, 256:512].rearrange("p (a b) -> p a b", b=P), ACT.Exp).then_inc(attX, 1)
                else:
                    exps = lambda: None
                if kind == "q":
                    evac_q(act, q0, qT[idx % 2], QSCALE, exps, done0, evac0, ps)
                elif kind == "k":
                    evac_q(act, q0, kT[idx % 2], None, exps, done0, evac0, ps)
                elif kind in ("v", "u"):
                    evac_q(act, q0, sc[idx % 2 if kind == "v" else 0], None, exps, done0, evac0, ps)
                else:
                    st = stage_slot((kind, idx))
                    evac_q(act, q0, stage[st], None, exps, done0, evac0, ps)
                    put((kind, idx), q0 + 3)
                if kind == "u":
                    q1 = 3 * use_of[("pool", idx, 0)]
                    evac_copy(q1, lambda b: sc[1][:, b * BW:(b + 1) * BW])
                    st = stage_slot(("pool", idx))
                    q1 += 3
                    evac_copy(q1, lambda b: stage[st][:, b * BW:(b + 1) * BW], scale=vT[:, V_PS + idx:V_PS + idx + 1],
                              func=ACT.Identity)
                    put(("pool", idx), q1 + 3)
                if m and mains[m - 1][0] == "v":
                    vi = mains[m - 1][1]
                    q1 = 3 * use_of[("turn", vi)]
                    if vi == 0:
                        act.wait_ge(s_out, 32)
                    evac_copy(q1, lambda b: vaug[(vi // 2) % 2][:, b * TB:(b + 1) * TB, (vi % 2) * P:(vi % 2 + 1) * P])
                if m == 2:
                    act.wait_ge(g_pe, 1)
                    for src, dst, f, sc_ in ((3, a_tok, ACT.Copy, 1.0), (4, en_tok, ACT.Exp, -1.0)):
                        for d in range(2):
                            ins = act.activation(dst[:, :, d, :], ps[:, src, 0:NT * GR].rearrange("p (t r) -> p t r", r=GR)
                                                 [:, :, 32 * d:32 * d + NH], f, scale=sc_)
                    ins.then_inc(g_tok, 1)
                if SEG_P <= m < SEG_P + 4:
                    act.wait_ge(pf_in, 64)
                    act.activation(pT_hi[:, m - SEG_P, :], pF[:, m - SEG_P, :], ACT.Copy).then_inc(p_hi, 1)
                if seg >= 0 and seg % 9 == 8:
                    hm_norm(seg // 9)

            def sig(w):
                act.wait_ge(ld_in[w % LS], 16 * (w // LS + 1))
                act.activation(ld[:, w % LS, :], ld[:, w % LS, :], ACT.Sigmoid).then_inc(sgm, 1)

            sig(0)
            sig(1)
            for d in range(KD):
                hi_split(S_BR + d + 2)
                act.wait_ge(hmx, d + 1)
                act.activation(H_hi[:, d, :], ld[:, (3 * d + 2) % LS, :], ACT.Copy).then_inc(hmhi, 1)
                if d + 1 < KD:
                    sig(3 * (d + 1))
                    sig(3 * (d + 1) + 1)
                if d == 1:
                    hm_evac(NH - 1)
            for d in range(KD):
                hi_split(S_YA + d + 2)
                sig(3 * KD + d)
            for b in range(NB):
                tok = slice(b * BW, (b + 1) * BW)
                for k in range(KD):
                    if b == 0 and k == 0:
                        act.wait_ge(ld_used, 2 * KD)
                    act.activation(H_hi[:, k, tok], mixF[:, k, tok], ACT.Copy).then_inc(mixhi, 1)
            for d in range(KD):
                hi_split(S_OUT + d + 2)
                evac_copy(3 * (U_OUT + d), lambda b: yT[:, d, b * BW:(b + 1) * BW])
                if d == 0:
                    for cond in range(2):
                        act.wait_ge(gtb_pe, cond + 1)
                        act.activation(gtb1[:, cond, :], ps[:, 6:8, :].rearrange("p a b -> p (a b)"), ACT.Copy).then_inc(gtb_done, 1)
            for t in range(NT):
                p = 4 + 2 * (t % 2)
                pair = ps[:, p:p + 2, :].rearrange("p a b -> p (a b)")
                act.wait_ge(done2, t + 1)
                if t == 0:
                    act.wait_ge(mix_ready, NB * KD)
                act.activation(X1[:, t, :], pair, ACT.Square, accum_out=stat[:, 0, t:t + 1]).then_inc(ss2, 1)
                act.wait_ge(vv2, 2 * t + 1)
                act.activation(stat[:, 2, t:t + 1], stat[:, 1, t:t + 1], ACT.Sqrt).then_inc(rt2, 1)
                act.wait_ge(x1_ready, t + 1)
                act.activation(xld[:, t % 2, :], X1[:, t, :], ACT.Square, accum_out=stat[:, 3, t:t + 1]).then_inc(ss2, 1)
                act.wait_ge(vv2, 2 * t + 2)
                act.activation(hstat[:, 1, t:t + 1], hstat[:, 0, t:t + 1], ACT.Sqrt).then_inc(rt2, 1)
                if t in NORM_AFTER:
                    norm_evac(lambda w: ps[:, (Q_N2 + w) % 3, :], lambda w: act.wait_ge(done0, Q_N2 + w + 1), evac0,
                              coefA2, 24, 24, tsc2, NORM_AFTER.index(t))
            for cond in range(2):
                act.wait_ge(gtb_pe, 3 + cond)
                act.activation(gtb2[:, cond, :], ps[:, 6:8, :].rearrange("p a b -> p (a b)"), ACT.Copy).then_inc(gtb_done, 1)

            def ff_up_act(f, e, slot, splits, i):
                first = V_W1 + f
                cols = slice(first, first + 5 * NF + 1, NF) if i is None else bass.ds(i * 4 + first, 6, NF)
                act.activation(taps[:, e, :], vT[:, cols], ACT.Copy).then_inc(taps_done, 1)
                act.wait_ge(taps_done, lin(f + 1, 4, i))
                for half in range(2):
                    for j in splits[half]:
                        ff_hi(j, i)
                    tile = cv if half else cg
                    for b in range(NB):
                        tok = slice(b * BW, (b + 1) * BW)
                        if half:
                            act.wait_ge(done1, lin(3 * KD + 3 * f + b + 1, 12, i))
                        else:
                            act.wait_ge(done0, lin(Q_FF + 3 * f + b + 1, 12, i))
                        if f:
                            act.wait_ge(f_ready, lin(3 * f + b - 2, 12, i))
                        act.activation(tile[:, tok], ps[:, b + 3 * half, 0:BW], ACT.Identity,
                                       scale=taps[:, e, half:half + 1], bias=taps[:, e, 4 + half:5 + half]).then_inc(conv_a, 1)
                        if half:
                            act.wait_ge(conv_v, lin(3 * f + b + 1, 12, i))
                            act.activation(fT_hi[:, slot, e, tok], cv[:, tok], ACT.Copy).then_inc(fhi, 1)
                        else:
                            act.wait_ge(conv_g, lin(3 * f + b + 1, 12, i))
                            act.activation(cg[:, tok], cg[:, tok], ACT.Gelu_apprx_tanh).then_inc(gel, 1)

            ff_up_act(0, 0, 0, [[2], [3]], None)
            ff_up_act(1, 1, 0, [[4], []], None)
            with act.Fori(0, (NC - 1) // 2) as i:
                for cc in range(2):
                    j = 4 + 6 * cc
                    ff_up_act(2 + 2 * cc, 0, 1 - cc, [[j + 1, j + 2], [j + 3]], i)
                    ff_up_act(3 + 2 * cc, 1, 1 - cc, [[j + 4], [j + 5]], i)
                    ff_hi(j + 6, i)
            ff_hi(5 + 6 * (NC - 1), None)
            for t in range(NT):
                act.wait_ge(evac2, NT + 18 * (NC - 1) + 2 * (t + 1))
                act.activation(ps[:, 0:2, :], acc[:, t, :].rearrange("p (a b) -> p a b", b=512), ACT.Square,
                               accum_out=stat[:, 0, t:t + 1]).then_inc(fin_rt, 1)
                act.wait_ge(fin_ss, t + 1)
                act.activation(stat[:, 2, t:t + 1], stat[:, 1, t:t + 1], ACT.Sqrt).then_inc(fin_rt, 1)

        @block.vector
        def _(dve):
            seq = [0]

            def link(ins):
                seq[0] += 1
                ins.then_inc(dve_seq, 1)
                dve.wait_ge(dve_seq, seq[0])

            def sub_hi(out, full, hi):
                return dve.tensor_tensor(out, full, hi.bitcast(F32), ALU.subtract)

            def lo_split(s):
                if s >= S_FF:
                    return ff_lo(s - S_FF, None)
                n, w = raw_n(s), unit_width(s)
                dve.wait_ge(hi_ready, s)
                sub_hi(ring_lo[:, s % RS, 0:w], raw[:, n % RS, 0:w], ring_hi[:, s % RS, 0:w]).then_inc(lo_ready, 1)

            def ff_lo(j, i):
                n0, r = N_FF + j, (S_FF + j) % RS
                dve.wait_ge(hi_ready, lin(S_FF + j, 12, i))
                sub_hi(ring_lo[:, r, :], raw[:, n0 % RS, :], ring_hi[:, r, :]).then_inc(lo_ready, 1)

            def rows(col, n):
                return vT[:, col:col + n].unsqueeze(2).to_broadcast([P, n, 2])

            dve.wait_ge(vec_done, 1)
            dve.tensor_copy(vT[:, :], ps[:, 3, 0:NV]).then_inc(vec_done, 1)
            dve.wait_ge(s_wg, 16 * 9)
            dve.memset(ring_hi[:, 0, :].bitcast(F32), 0.0)
            link(dve.memset(ring_lo[:, 0, :].bitcast(F32), 0.0))
            spread = lambda ap: ap.rearrange("p (k g c) -> p k g c", k=KD, g=4)[:, :, :, 0:4]
            wg4 = wgate[:, :, :].rearrange("p k (g c) -> p k g c", c=4)
            link(dve.tensor_copy(spread(ring_hi[:, 0, :]), wg4))
            sub_hi(spread(ring_lo[:, 0, :]), wg4, spread(ring_hi[:, 0, :])).then_inc(lo_ready, 1)

            def first_coef():
                dve.wait_ge(ada_used, ADA0)
                link(dve.tensor_tensor(modT[:, 0:ADA0, :], ps[:, 7, 0:2 * ADA0].rearrange("p (a b) -> p a b", b=2),
                                       rows(V_BADA, ADA0), ALU.add))
                dve.scalar_tensor_tensor(out=coefA1[:, :, :], in0=modT[:, 8:16, :], scalar=1.0, in1=rows(V_GPM, KD),
                                         op0=ALU.add, op1=ALU.mult).then_inc(coef1, 1)

            for b in range(NB):
                tiles = slice(b * TB, (b + 1) * TB)
                if b == NB - 1:
                    first_coef()
                dve.wait_ge(ss_done, TB * (b + 1))
                dve.tensor_scalar(stat[:, 1, tiles], stat[:, 0, tiles], 1.0 / DM, EPS, ALU.mult, ALU.add).then_inc(rt_done, 1)
                dve.wait_ge(rt_done, 2 * b + 2)
                link(dve.reciprocal(stat[:, 3, tiles], stat[:, 2, tiles]))
                for t in range(b * TB, (b + 1) * TB):
                    dve.tensor_scalar(X0[:, t, :], X0[:, t, :], stat[:, 3, t:t + 1], None, ALU.mult).then_inc(x_scaled, 1)
            def norm_split(evac, q0, n0, tile, b):
                for k in range(KD):
                    w = n0 + b * KD + k
                    dve.wait_ge(evac, q0 + b * KD + k + 1)
                    tok = slice(b * BW, (b + 1) * BW)
                    link(dve.tensor_copy(H_hi[:, k, tok], tile[:, w % 4, :]))
                    sub_hi(H_lo[:, k, tok], tile[:, w % 4, :], H_hi[:, k, tok]).then_inc(tl_done, 1)

            for b in range(NB):
                norm_split(xt_free, 0, 0, tsc, b)
            dve.wait_ge(s_cst, 32)
            dve.tensor_copy(idbf[:, :], ident[:, :])
            dve.tensor_copy(maskbf[:, :, :], mask32[:, :].rearrange("p (a b) -> p a b", b=P))
            dve.tensor_copy(sel[:, :, :], stage[1][:, 0:8 * P].rearrange("p (a b) -> p a b", b=P))

            def gates():
                dve.memset(Gt[3][0:GR, :], 0.0)
                dve.wait_ge(tl_done, 24)
                link(dve.memset(Gt[4][0:GR, :], 0.0))
                dve.memset(GS[:, :].bitcast(F32), 0.0)
                dve.memset(YS[:, :].bitcast(F32), 0.0)
                dve.wait_ge(g_lf, 1)
                li, lf, bb, mm_, gg, aa, yy = (Gt[r][0:GR, :] for r in (0, 1, 3, 4, 5, 6, 7))
                link(dve.scalar_tensor_tensor(out=lf, in0=lf, scalar=0.0, in1=Gt[2][0:GR, :], op0=ALU.min, op1=ALU.subtract))
                fwd, bwd = slice(0, 4), slice(32, 36)
                dve.tensor_tensor_scan(Gt[3][fwd, :], reset[fwd, :], Gt[1][fwd, :], 0.0, ALU.mult, ALU.add)
                dve.tensor_tensor_scan(Gt[3][bwd, :][:, ::-1], reset[bwd, :][:, ::-1], Gt[1][bwd, :][:, ::-1], 0.0,
                                       ALU.mult, ALU.add)
                for rw, dr in ((fwd, 1), (bwd, -1)):
                    for lo, hi, init in ((0, CTX, 0.0), (CTX, T, m0t[rw, :])):
                        a = [Gt[r][rw, lo:hi] if dr == 1 else Gt[r][rw, lo:hi][:, ::-1] for r in (4, 1, 0)]
                        ins = dve.tensor_tensor_scan(a[0], a[1], a[2], init, ALU.add, ALU.max)
                link(ins)
                m3 = Gt[4][0:GR, :].rearrange("p (t s) -> p t s", s=P)
                dve.tensor_copy(mprev[fwd, 1:2], m0t[fwd, :])
                dve.tensor_copy(mprev[bwd, NT - 1:NT], m0t[bwd, :])
                dve.tensor_copy(mprev[fwd, 2:NT], m3[fwd, 1:NT - 1, P - 1])
                dve.tensor_copy(mprev[bwd, 1:NT - 1], m3[bwd, 2:NT, 0])
                dve.tensor_tensor(aa, li, bb, ALU.subtract)
                link(dve.tensor_tensor(gg, bb, mm_, ALU.subtract))
                link(dve.tensor_tensor(yy.rearrange("p (t s) -> p t s", s=P), gg.rearrange("p (t s) -> p t s", s=P),
                                       mprev[0:GR, :].unsqueeze(2).to_broadcast([GR, NT, P]), ALU.add))
                dve.tensor_copy(GS[0:GR, :], gg)
                link(dve.tensor_copy(YS[0:GR, :], yy))
                sub_hi(GS[64:64 + GR, :], gg, GS[0:GR, :])
                sub_hi(YS[64:64 + GR, :], yy, YS[0:GR, :]).then_inc(g_ready, 1)

            def attention_weights(h, i):
                e = h * 9 + i
                tiles = (0, 0) if i == 0 else (i, NT - i)
                v = h % 2
                dve.wait_ge(attX, e + 1)
                dve.tensor_tensor(Pt[:, :, :].rearrange("p a b -> p (a b)"), ps[:, 4, 0:256],
                                  Wt[:, :, :].rearrange("p a b -> p (a b)"), ALU.mult)
                if i:
                    for d, cx in enumerate(tiles):
                        dve.tensor_tensor(qs[:, d, :], qT[v][:, cx * P:(cx + 1) * P], Et[:, d, :], ALU.mult)
                for d in range(2):
                    last = (1 - d) * (P - 1)
                    ins = dve.tensor_scalar(kw[:, d, :], ps[:, 4, 256 + d * P:256 + (d + 1) * P], Wt[:, d, last:last + 1], None,
                                            ALU.mult)
                ins.then_inc(attP, 1)

            def attention_outputs(h, i, d):
                e = h * 9 + i
                cx = 0 if i == 0 else (i, NT - i)[d]
                hd = hm[h % 2]
                last = (1 - d) * (P - 1)
                dve.wait_ge(attB, 2 * e + d + 1)
                if i == 0:
                    if h:
                        dve.wait_ge(c_out, 64 * h)
                    dve.tensor_copy(Cctx[:, d, :], ps[:, 7, 0:VW]).then_inc(attC, 1)
                else:
                    dve.scalar_tensor_tensor(out=Cst[:, d, :], in0=Cst[:, d, :], scalar=Et[:, d, last:last + 1],
                                             in1=ps[:, 7, 0:VW], op0=ALU.mult, op1=ALU.add).then_inc(attC, 1)
                den, rec = dsm[:, 2 * d:2 * d + 1], dsm[:, 2 * d + 1:2 * d + 2]
                link(dve.scalar_tensor_tensor(out=den, in0=ps[:, 5 + d, DV:VW], scalar=-1.0, in1=en_tok[:, cx, d, h:h + 1],
                                              op0=ALU.mult, op1=ALU.max))
                link(dve.tensor_tensor(den, ps[:, 5 + d, DV:VW], den, ALU.max))
                link(dve.reciprocal(rec, den))
                if (i == 0 and d == 0) or 1 <= i <= 4:
                    dve.tensor_scalar(hd[:, cx, :], ps[:, 5 + d, 0:DV], rec, None, ALU.mult).then_inc(attN, 1)
                else:
                    dve.scalar_tensor_tensor(out=hd[:, cx, :], in0=ps[:, 5 + d, 0:DV], scalar=rec, in1=hd[:, cx, :],
                                             op0=ALU.mult, op1=ALU.add).then_inc(attN, 1)

            lo_split(1)
            for m, (kind, idx) in enumerate(mains):
                seg = m - SEG
                lo_split(m + 2)
                if m == 0:
                    gates()
                if m == SEG - 4:
                    dve.wait_ge(g_tok, 1)
                    dve.wait_ge(s_out, 32)
                    dve.memset(vaug[0][:, :, DV:VW], 1.0)
                    dve.memset(vaug[1][:, :, DV:VW], 1.0).then_inc(ones_done, 1)
                if seg >= 0:
                    h, i = seg // 9, seg % 9
                    attention_weights(h, i)
                    attention_outputs(h, i, 0)
                    attention_outputs(h, i, 1)
                    if SEG_P <= m < SEG_P + 4:
                        g = m - SEG_P
                        dve.wait_ge(p_hi, g + 1)
                        sub_hi(pT_lo[:, g, :], pF[:, g, :], pT_hi[:, g, :]).then_inc(p_lo, 1)
                    if i == 8:
                        dve.wait_ge(hss, NT * (h + 1))
                        dve.tensor_scalar(hstat[:, 0, :], hstat[:, 0, :], 1.0 / DV, EPS, ALU.mult, ALU.add).then_inc(hrt, 1)
                        dve.wait_ge(hrt, 2 * h + 2)
                        link(dve.reciprocal(hstat[:, 0, :], hstat[:, 1, :]))
                        for t in range(NT):
                            ins = dve.tensor_scalar(hm[h % 2][:, t, :], hm[h % 2][:, t, :], hstat[:, 0, t:t + 1], None, ALU.mult)
                        ins.then_inc(hscaled, 1)

            dve.wait_ge(evac0, 3 * use_of[("main", NM - 1)] + 3)
            dve.scalar_tensor_tensor(out=coefA2[:, :, :], in0=modT[:, 32:40, :], scalar=1.0, in1=rows(V_GPF, KD),
                                     op0=ALU.add, op1=ALU.mult)
            dve.tensor_tensor(coefG1[:, :, :], modT[:, 16:24, :], rows(V_GQM, KD), ALU.mult)
            dve.tensor_tensor(coefG2[:, :, :], modT[:, 40:48, :], rows(V_GQF, KD), ALU.mult).then_inc(coef2, 1)
            for d in range(KD):
                wb, wo, wh = 3 * d % LS, (3 * d + 1) % LS, (3 * d + 2) % LS
                dve.wait_ge(ld_in[wh], 16 * ((3 * d + 2) // LS + 1))
                dve.wait_ge(sgm, 2 * d + 2)
                dve.scalar_tensor_tensor(out=ld[:, wh, :], in0=ld[:, wh, :], scalar=vT[:, V_GH + d:V_GH + d + 1],
                                         in1=ld[:, wo, :], op0=ALU.mult, op1=ALU.mult).then_inc(hmx, 1)
                lo_split(S_BR + d + 2)
                if d == 4:
                    dve.wait_ge(evac0, Q_P1)
                if d == 6:
                    for i in range(2):
                        dve.wait_ge(stored[i], 16 * ((len(stage_no) + 1 - i) // 2))
                for b in range(NB):
                    tok = slice(b * BW, (b + 1) * BW)
                    dve.wait_ge(done1, 3 * d + b + 1)
                    dve.tensor_tensor(mixF[:, d, tok], ps[:, 3 + b, 0:BW], ld[:, wb, tok], ALU.mult).then_inc(evac1, 1)
                dve.wait_ge(hmhi, d + 1)
                sub_hi(H_lo[:, d, :], ld[:, wh, :], H_hi[:, d, :]).then_inc(ld_used, 1)
            for d in range(KD):
                lo_split(S_YA + d + 2)
                wa = (3 * KD + d) % LS
                dve.wait_ge(sgm, 2 * KD + d + 1)
                for b in range(NB):
                    tok = slice(b * BW, (b + 1) * BW)
                    q = 3 * (U_YA + d) + b + 1
                    dve.wait_ge(done0, q)
                    dve.tensor_tensor(ld[:, wa, tok], ps[:, b, 0:BW], ld[:, wa, tok], ALU.mult).then_inc(evac0, 1)
                    dve.wait_ge(evac0, q)
                    ins = dve.tensor_tensor(mixF[:, d, tok], ld[:, wa, tok], mixF[:, d, tok], ALU.add)
                ins.then_inc(ld_used, 1)
            for b in range(NB):
                for k in range(KD):
                    tok = slice(b * BW, (b + 1) * BW)
                    dve.wait_ge(mixhi, b * KD + k + 1)
                    sub_hi(H_lo[:, k, tok], mixF[:, k, tok], H_hi[:, k, tok]).then_inc(mix_ready, 1)
            for d in range(KD):
                lo_split(S_OUT + d + 2)

            def scale_tile(t):
                dve.wait_ge(x1_stored[t % 2], 16 * (t // 2 + 1))
                dve.tensor_scalar(X1[:, t, :], X1[:, t, :], stat[:, 3, t:t + 1], None, ALU.mult).then_inc(x_scaled, 1)

            dve.wait_ge(gtb_done, 2)
            for t in range(NT):
                p = 4 + 2 * (t % 2)
                cond = 0 if t == 0 else 1
                dve.wait_ge(ss2, 2 * t + 1)
                dve.tensor_scalar(stat[:, 1, t:t + 1], stat[:, 0, t:t + 1], 1.0 / DM, EPS, ALU.mult, ALU.add).then_inc(vv2, 1)
                dve.wait_ge(rt2, 2 * t + 1)
                link(dve.reciprocal(stat[:, 0, t:t + 1], stat[:, 2, t:t + 1]))
                dve.scalar_tensor_tensor(out=X1[:, t, :], in0=ps[:, p:p + 2, :].rearrange("p a b -> p (a b)"),
                                         scalar=stat[:, 0, t:t + 1], in1=gtb1[:, cond, :], op0=ALU.mult,
                                         op1=ALU.mult).then_inc(evac2, 1)
                dve.wait_ge(evac2, t + 1)
                dve.wait_ge(x_in[t % 2], 16 * (t // 2 + 1))
                dve.tensor_tensor(X1[:, t, :], X1[:, t, :], xld[:, t % 2, :], ALU.add).then_inc(x1_ready, 1)
                dve.wait_ge(ss2, 2 * t + 2)
                dve.tensor_scalar(hstat[:, 0, t:t + 1], stat[:, 3, t:t + 1], 1.0 / DM, EPS, ALU.mult, ALU.add).then_inc(vv2, 1)
                dve.wait_ge(rt2, 2 * t + 2)
                link(dve.reciprocal(stat[:, 3, t:t + 1], hstat[:, 1, t:t + 1]))
                if t >= 2:
                    scale_tile(t - 2)
                if t == NT - 1:
                    scale_tile(t - 1)
                    scale_tile(t)
                if t in NORM_AFTER:
                    norm_split(evac0, Q_N2, 3 * KD, tsc2, NORM_AFTER.index(t))

            def ff_up_dve(f, e, slot, splits, i, before_last=None):
                n = [12 * f]

                def step(ins):
                    n[0] += 1
                    ins.then_inc(dve_ff, 1)

                def settle():
                    dve.wait_ge(dve_ff, lin(n[0], 48, i))

                for half in range(2):
                    for j in splits[half]:
                        ff_lo(j, i)
                    tile = cv if half else cg
                    for b in range(NB):
                        dve.wait_ge(conv_a, lin(6 * f + 3 * half + b + 1, 24, i))

                        def tap(lo, nr, ln, shift):
                            out = tile[:, b * BW + lo:b * BW + lo + nr * ln].rearrange("p (r c) -> p r c", c=ln)
                            src = ps[:, b + 3 * half, lo:lo + nr * ln].rearrange("p (r c) -> p r c", c=ln)
                            if shift < 0:
                                out, src, w = out[:, :, 1:ln], src[:, :, 0:ln - 1], V_W0
                            else:
                                out, src, w = out[:, :, 0:ln - 1], src[:, :, 1:ln], V_W2
                            return dve.scalar_tensor_tensor(out=out, in0=src, scalar=vcol(w + NF * half + f, i), in1=out,
                                                            op0=ALU.mult, op1=ALU.add)

                        parts = row_parts(b)
                        for pt in parts:
                            step(tap(*pt, -1))
                        settle()
                        tok = slice(b * BW, (b + 1) * BW)
                        if half == 0:
                            for pt in parts:
                                ins = tap(*pt, 1)
                            ins.then_inc(conv_g, 1)
                        else:
                            for pt in parts:
                                step(tap(*pt, 1))
                            settle()
                            dve.wait_ge(gel, lin(3 * f + b + 1, 12, i))
                            dve.tensor_tensor(cv[:, tok], cg[:, tok], cv[:, tok], ALU.mult).then_inc(conv_v, 1)
                            if before_last and b == NB - 1:
                                before_last()
                            dve.wait_ge(fhi, lin(3 * f + b + 1, 12, i))
                            sub_hi(fT_lo[:, slot, e, tok], cv[:, tok], fT_hi[:, slot, e, tok]).then_inc(f_ready, 1)
                assert n[0] == 12 * (f + 1)

            def add_halves(ch, t, i):
                for hb in range(2):
                    dve.wait_ge(done2, lin(NT + 18 * ch + 2 * t + hb + 1, 36, i))
                    cols = slice(hb * 512, (hb + 1) * 512)
                    dve.tensor_tensor(acc[:, t, cols], ps[:, 6 + hb, :], acc[:, t, cols], ALU.add).then_inc(evac2, 1)

            ff_up_dve(0, 0, 0, [[2], [3]], None)
            ff_up_dve(1, 1, 0, [[4], []], None)
            dve.wait_ge(acc_zero, 1)
            with dve.Fori(0, (NC - 1) // 2) as i:
                for cc in range(2):
                    j = 4 + 6 * cc
                    ff_up_dve(2 + 2 * cc, 0, 1 - cc, [[j + 1, j + 2], [j + 3]], i)
                    ff_up_dve(3 + 2 * cc, 1, 1 - cc, [[j + 4], [j + 5]], i, lambda: add_halves(cc, 0, i))
                    for t in range(1, NT):
                        add_halves(cc, t, i)
                        if t == 2:
                            ff_lo(j + 6, i)
            ff_lo(5 + 6 * (NC - 1), None)

            def finish(t):
                dve.wait_ge(fin_rt, 2 * t + 1)
                dve.tensor_scalar(stat[:, 1, t:t + 1], stat[:, 0, t:t + 1], 1.0 / DM, EPS, ALU.mult, ALU.add).then_inc(fin_ss, 1)
                dve.wait_ge(fin_rt, 2 * t + 2)
                link(dve.reciprocal(stat[:, 3, t:t + 1], stat[:, 2, t:t + 1]))
                dve.scalar_tensor_tensor(out=acc[:, t, :], in0=acc[:, t, :], scalar=stat[:, 3, t:t + 1],
                                         in1=gtb2[:, 0 if t == 0 else 1, :], op0=ALU.mult, op1=ALU.mult).then_inc(fin_m, 1)

            dve.wait_ge(gtb_done, 4)
            for t in range(NT):
                add_halves(NC - 1, t, None)
                if t:
                    finish(t - 1)
            finish(NT - 1)


_INS = ['x_prompt', 'x_sample', 'state_C', 'state_n', 'state_m', 'c', 'c_ctx', 'w_ada', 'b_ada', 'g_pre_mix',
        'g_post_mix', 'g_pre_ffn', 'g_post_ffn', 'w_in', 'b_gates', 'g_head', 'w_pool', 'pool_scale', 'w_br_a',
        'w_br_b', 'w_out', 'w_up', 'conv_w', 'conv_b', 'w_down']
_OUTS = [(1, 128, 1024), (1, 1024, 1024), (1, 1, 2, 4, 128, 256), (1, 1, 2, 4, 128), (1, 1, 2, 4)]


def kernel(**inputs):
    import concourse.bacc as _bacc
    from concourse.bass_utils import run_bass_kernel_spmd as _run

    nc = _bacc.Bacc("TRN2", target_bir_lowering=False, num_devices=1)
    arrays, args = {}, []
    for name in _INS:
        a = np.ascontiguousarray(inputs[name])
        arrays[f"in_{name}_dram"] = a
        args.append(nc.dram_tensor(f"in_{name}_dram", a.shape, mybir.dt.from_np(a.dtype), kind="ExternalInput").ap())
    arrays["in_consts_dram"] = shape_constants()
    args.append(nc.dram_tensor("in_consts_dram", (P, H_COLS), F32, kind="ExternalInput").ap())
    for i, shape in enumerate(_OUTS):
        args.append(nc.dram_tensor(f"out_{i}_dram", shape, F32, kind="ExternalOutput").ap())
    build(nc, *args)
    r = _run(nc, [arrays], core_ids=[0])
    return tuple(r.results[0][f"out_{i}_dram"] for i in range(len(_OUTS)))
```

```python
import numpy as np

import concourse.bass as bass
from concourse import mybir

F32 = mybir.dt.float32
F32R = mybir.dt.float32r
BF16 = mybir.dt.bfloat16
ALU = mybir.AluOpType
ACT = mybir.ActivationFunctionType

P = 128
DM = 1024
KD = DM // P
CTX = 128
LAT = 1024
T = CTX + LAT
NT = T // P
NB = 3
BW = T // NB
TB = BW // P
NH = 4
DK = 128
DV = 256
VW = DV + 1
DFF = 2816
NF = DFF // P
NC = NF // 2
ROW = 64
WINDOWS = (2, 4, 8, 16)
EPS = 1e-6
QSCALE = DK ** -0.5
NEG = -1e30

CQ, CK, CV, CO = 0, 512, 1024, 2048
CG, CU, CGA, CGB = 3072, 3088, 3600, 4624
GR = 36

V_BADA, V_GPM, V_GQM, V_GPF, V_GQF, V_GH, V_PS, V_C = 0, 48, 56, 64, 72, 80, 88, 92
V_W0, V_W1, V_W2, V_CB = 108, 152, 196, 240
NV = 284

H_ID, H_SEL, H_MASK, H_POOL = 0, 128, 128 + 8 * 128, 128 + 10 * 128
H_COLS = H_POOL + 8 * 128


def shape_constants():
    out = np.zeros((P, H_COLS), np.float32)
    out[:, H_ID:H_ID + P] = np.eye(P)
    for d in range(2):
        for h in range(NH):
            r = 32 * d + h
            for row in (r, 64 + r):
                out[row, H_SEL + (d * NH + h) * P:H_SEL + (d * NH + h + 1) * P] = 1.0
    s, t = np.arange(P)[:, None], np.arange(P)[None, :]
    out[:, H_MASK:H_MASK + P] = np.where(s <= t, 0.0, NEG)
    out[:, H_MASK + P:H_MASK + 2 * P] = np.where(s >= t, 0.0, NEG)
    for g, win in enumerate(WINDOWS):
        for kind, cols in enumerate((CTX, ROW)):
            m = np.zeros((P, P), np.float32)
            for tok in range(P):
                row, c = tok // cols, tok % cols
                lo, hi = max(c - win // 2, 0), min(c + win // 2, cols)
                m[row * cols + lo:row * cols + hi, tok] = np.float32(1.0) / np.float32(hi - lo)
                m[tok, tok] -= 1.0
            at = H_POOL + (2 * g + kind) * P
            out[:, at:at + P] = m
    return out


def plan():
    rest = [("o", j) for j in range(8)] + [("ga", j) for j in range(8)] + [("gb", j) for j in range(8)]
    mains = [("gates", 0)] + [("u", g) for g in range(4)]
    mains += [("v", 0), ("v", 1), ("q", 0), ("k", 0)]
    seg_start = len(mains)
    for h in range(NH):
        seg = []
        if h + 1 < NH:
            seg += [("v", 2 * h + 2), ("v", 2 * h + 3), ("q", h + 1), ("k", h + 1)]
            seg += rest[:5]
            rest = rest[5:]
        else:
            seg += rest
        mains += seg
    return mains, seg_start


def build(nc, x_prompt, x_sample, state_C, state_n, state_m, c, c_ctx, w_ada, b_ada, g_pre_mix, g_post_mix,
          g_pre_ffn, g_post_ffn, w_in, b_gates, g_head, w_pool, pool_scale, w_br_a, w_br_b, w_out, w_up,
          conv_w, conv_b, w_down, consts, y_prompt, y_sample, new_C, new_n, new_m):
    mains, SEG = plan()
    NM = len(mains)
    POOL_SPLIT = {SEG + NT * (NH - 1) + 5 + n: groups for n, groups in enumerate(((0,), (1,), (2, 3)))}
    NORM_AT = {SEG + NT * (h + 1) + 1: h for h in range(NH - 1)}
    NORM_AT[NM - 1] = NH - 1
    RS = 3
    LS = 5
    ADA0 = 16
    AG = ADA0 * P // 512

    S_BR = NM
    S_YA = S_BR + 8
    S_OUT = S_YA + 8
    S_FF = S_OUT + 8
    n_units = S_FF + 4 + 6 * (NC - 1) + 2
    ADA_AT = {}
    for s in range(2, NM):
        if s - 2 not in NORM_AT and ADA0 + len(ADA_AT) < 48:
            ADA_AT[s] = ADA0 + len(ADA_AT)
    raw_items = []
    for s in range(1, NM):
        raw_items.append(("unit", s))
        if s in ADA_AT:
            raw_items.append(("ada", ADA_AT[s]))
    for s in range(S_BR, S_FF):
        raw_items.append(("unit", s))
    raw_of = {it: n for n, it in enumerate(raw_items)}
    N_FF = len(raw_items)

    def raw_n(s):
        return raw_of[("unit", s)] if s < S_FF else N_FF + s - S_FF

    def pool_steps(m):
        return [(mains[m - 2 + n][1], 1 - n) for n in range(2) if m - 2 + n >= 0 and mains[m - 2 + n][0] == "u"]

    TURN_AT = {SEG + NT * (h + 1) + (5 if h < NH - 2 else 3) + j: (h, j) for h in range(NH - 1) for j in range(2)}
    HG = 2 * (NH - 1)

    loads = []
    for d in range(KD):
        loads += [("gb", d)] + ([("o", d)] if d >= HG else []) + [("hm", d)]
    loads += [("ga", d) for d in range(KD)]
    load_of = {it: w for w, it in enumerate(loads)}
    sigmoids = [it for it in loads if it[0] != "hm"]

    uses = []
    use_of = {}
    for m, (kind, idx) in enumerate(mains):
        if m in TURN_AT:
            h, j = TURN_AT[m]
            use_of[("hm", 2 * h + j)] = len(uses)
            uses.append("hm")
        use_of[("main", m)] = len(uses)
        uses.append(kind)
        for group, step in pool_steps(m):
            use_of[("pool", group, step)] = len(uses)
            uses.append("pool")
        if m and mains[m - 1][0] == "v":
            use_of[("turn", mains[m - 1][1])] = len(uses)
            uses.append("turn")
    for j in range(2):
        use_of[("hm", 2 * (NH - 1) + j)] = len(uses)
        uses.append("hm")
    Q_P1 = 3 * len(uses)
    U_YA = len(uses)
    Q_FF = 3 * (U_YA + 8)
    WO = 5

    def unit_done_q(s):
        return 3 * use_of[("main", s)] + 3

    base = [(nc.sbuf_base + 63) // 64 * 64]

    def place(name, shape, dt=F32, at=None):
        size = int(np.prod(shape[1:])) * (2 if dt == BF16 else 4)
        off = base[0] if at is None else at
        if at is None:
            base[0] += (size + 31) // 32 * 32
        return nc.alloc_sbuf_tensor_at(name, shape, dt, offset=off)

    ident = place("ident", [P, P])
    vT = place("vT", [P, NV])
    modT = place("modT", [P, 48, 2])
    condT = place("condT", [P, 2, KD])
    coefA1 = place("coefA1", [P, KD, 2])
    coefA2 = place("coefA2", [P, KD, 2])
    coefG1 = place("coefG1", [P, KD, 2])
    coefG2 = place("coefG2", [P, KD, 2])
    stat = place("stat", [P, 4, NT])
    hstat = place("hstat", [P, 2, NT])
    taps = place("taps", [P, 2, 6])
    den_rec = place("den_rec", [P, 8])
    HH0 = base[0]
    H_hi = place("H_hi", [P, KD, T], F32R)
    H_lo = place("H_lo", [P, KD, T], F32R)
    ring_hi = place("ring_hi", [P, RS, 1024], F32R)
    ring_lo = place("ring_lo", [P, RS, 1024], F32R)
    raw = place("raw", [P, RS, 1024])
    R = base[0]
    qT, kT, vaug, hm = [None, None], [None, None], [None, None], [None, None]
    for i in range(2):
        base_of_head1 = base[0]
        qT[i] = place(f"qT{i}", [P, T])
        kT[i] = place(f"kT{i}", [P, T])
        vaug[i] = place(f"vaug{i}", [P, NT, VW])
        if i == 0:
            SC0 = base[0]
            work = [place(f"work{j}", [P, T]) for j in range(2)]
        HM1 = base[0]
        hm[i] = place(f"hm{i}", [P, NT, DV])
    stage = [place(f"stage{i}", [P, T]) for i in range(2)]
    base_of_gates = base[0]
    GS = place("GS", [P, T], F32R)
    YS = place("YS", [P, T], F32R)
    a_tok = place("a_tok", [P, NT, 2, NH])
    en_tok = place("en_tok", [P, NT, 2, NH])
    ST0 = base[0]
    Cst = place("Cst", [P, 2, VW])
    Cctx = place("Cctx", [P, 2, VW])
    AT0 = base[0]
    Wt = place("Wt", [P, 2, P])
    Et = place("Et", [P, 2, P])
    Pt = place("Pt", [P, 2, P])
    k_weighted = place("k_weighted", [P, 2, P])
    qs = place("qs", [P, 2, P])
    sel = place("sel", [P, 8, P], F32R)
    ada_part = place("ada_part", [P, 2, P])
    ones = place("ones", [P, 1])
    idbf = place("idbf", [P, P], BF16)
    maskbf = place("maskbf", [P, 2, P], BF16)
    assert base[0] <= nc.sbuf_usable_end, (base[0], nc.sbuf_usable_end)
    adaw = place("adaw", [P, AG, KD, 512], at=HH0)
    ada_row = place("ada_row", [2, AG, 512], at=base_of_head1 + 16 * BW)
    X0 = place("X0", [P, NT, DM], at=R)
    Gt = [place(f"Gt{r}", [P, T], at=(R if r < 4 else base_of_head1) + (r % 4) * 4 * T) for r in range(8)]
    vecs = place("vecs", [P, 3, P], at=AT0 + 2048)
    tsc = place("tsc", [P, 4, BW], at=base_of_head1)
    reset = place("reset", [P, T], at=ST0)
    wgate = place("wgate", [P, KD, 16], at=ST0 + 4 * T)
    gbias = place("gbias", [P, 2], at=ST0 + 4 * T + 512)
    m0t = place("m0t", [P, 1], at=ST0 + 4 * T + 544)
    mprev = place("mprev", [P, NT], at=ST0 + 4 * T + 576)
    poolM = place("poolM", [P, 8, P], at=HM1)
    mixed = [place(f"mixed{i}", [P, T], at=SC0 + (8 + 4 * i) * T) for i in range(2)]
    mask32 = place("mask32", [P, 2 * P], at=HM1 + 6144)
    wpool = place("wpool", [P, 4, P], at=HM1 + 4096)
    pT_hi = place("pT_hi", [P, 4, T], F32R, at=R)
    pF = place("pF", [P, 4, T], at=SC0)
    pT_lo = place("pT_lo", [P, 4, T], F32R, at=SC0)
    mixF = place("mixF", [P, KD, T], at=SC0 + 16 * T)
    LD0 = base_of_gates
    tiles = place("tiles", [P, LS, T], at=LD0)
    assert SC0 + 16 * T == base_of_head1 and SC0 + 48 * T <= LD0 and LD0 + 4 * LS * T <= nc.sbuf_usable_end
    wo_hi = place("wo_hi", [P, WO - 1, 1024], F32R, at=R)
    wo_lo = place("wo_lo", [P, WO - 1, 1024], F32R, at=R + 16384)
    wo4_hi = place("wo4_hi", [P, 1024], F32R, at=R + 32768)
    wo4_lo = place("wo4_lo", [P, 1024], F32R, at=LD0 + 16 * T)
    X1 = place("X1", [P, NT, DM], at=SC0 + 16 * T)
    gtb1 = place("gtb1", [P, 2, DM], at=LD0)
    xld = place("xld", [P, 2, DM], at=LD0 + 8192)
    tsc2 = place("tsc2", [P, 2, BW], at=LD0 + 16 * T + 4096)
    acc = place("acc", [P, NT, DM], at=R)
    FF0 = R + 4 * NT * DM
    fT_hi = place("fT_hi", [P, 2, 2, T], F32R, at=FF0)
    fT_lo = place("fT_lo", [P, 2, 2, T], F32R, at=FF0 + 16 * T)
    conv_g = place("conv_g", [P, T], at=FF0 + 32 * T)
    conv_v = place("conv_v", [P, T], at=FF0 + 36 * T)
    x1ld = place("x1ld", [P, 2, DM], at=FF0 + 32 * T)
    gtb2 = place("gtb2", [P, 2, DM], at=FF0 + 40 * T)
    assert FF0 + 40 * T + 8192 <= nc.sbuf_usable_end

    ps = nc.alloc_psum_tensor("ps", [P, 8, 512], F32)

    def split_of(s):
        if S_OUT <= s < S_OUT + WO - 1:
            return wo_hi[:, s - S_OUT, :], wo_lo[:, s - S_OUT, :]
        if s == S_OUT + WO - 1:
            return wo4_hi[:, :], wo4_lo[:, :]
        r = (s + 1 if S_OUT <= s < S_FF else s) % RS
        return ring_hi[:, r, :], ring_lo[:, r, :]

    Z = {k: nc.dram_tensor("z_" + k, (n, P, T), F32, kind="Internal").ap()
         for k, n in (("o", 8), ("ga", 8), ("gb", 8), ("hm", 8), ("pool", 4))}
    x1_dram = nc.dram_tensor("z_x1", (NT, P, DM), F32, kind="Internal").ap()

    S = nc.alloc_semaphore
    ident_in, consts_in, vectors_in, small_in = S("ident_in"), S("consts_in"), S("vectors_in"), S("small_in")
    x_block_in = [S(f"x_block_in{b}") for b in range(NB)]
    ada_in = [S(f"ada_in{j}") for j in range(2 * AG)]
    landed = [S(f"landed{i}") for i in range(RS)]
    ada_mac, ada_summed = S("ada_mac"), S("ada_summed")
    hi_ready, lo_ready, ada_used, ring_read = S("hi_ready"), S("lo_ready"), S("ada_used"), S("ring_read")
    done0, evac0 = S("done0"), S("evac0")
    done1, evac1 = S("done1"), S("evac1")
    done2, evac2 = S("done2"), S("evac2")
    xt_done, xt_free = S("xt_done"), S("xt_free")
    act_seq, dve_seq, pool_seq = S("act_seq"), S("dve_seq"), S("pool_seq")
    vec_done, cond_done, coef1 = S("vec_done"), S("cond_done"), S("coef1")
    row_done, row_read = S("row_done"), S("row_read")
    x_squares, x_roots, x_scaled, h_split_done = S("x_squares"), S("x_roots"), S("x_scaled"), S("h_split_done")
    log_f_ready, gate_rows_ready = S("log_f_ready"), S("gate_rows_ready")
    gate_cols_done, gate_cols_ready, ones_done = S("gate_cols_done"), S("gate_cols_ready"), S("ones_done")
    att_scores, att_exps, att_weights = S("att_scores"), S("att_exps"), S("att_weights")
    att_values, att_outputs, att_state = S("att_values"), S("att_outputs"), S("att_state")
    state_in, new_state_stored, new_m_stored = S("state_in"), S("new_state_stored"), S("new_m_stored")
    head_squares, head_roots, hscaled = S("head_squares"), S("head_roots"), S("hscaled")
    stored, head_stored = [S("stored0"), S("stored1")], [S("head_stored0"), S("head_stored1")]
    pooled_in, pooled_hi_done, pooled_lo_done = S("pooled_in"), S("pooled_hi_done"), S("pooled_lo_done")
    tile_in = [S(f"tile_in{i}") for i in range(LS)]
    tile_used = S("tile_used")
    o_in, o_sigmoid, head_staged = [S("o_in0"), S("o_in1")], S("o_sigmoid"), S("head_staged")
    sigmoids_done, head_gated, head_hi_done = S("sigmoids_done"), S("head_gated"), S("head_hi_done")
    mix_sum, mix_hi_done, mix_ready = S("mix_sum"), S("mix_hi_done"), S("mix_ready")
    coef2, gate_bcast_done, gate_bcast_copied = S("coef2"), S("gate_bcast_done"), S("gate_bcast_copied")
    x_in = [S("x_in0"), S("x_in1")]
    x1_ready, x1_stored = S("x1_ready"), [S("x1_stored0"), S("x1_stored1")]
    norm_squares, norm_roots, norm_means = S("norm_squares"), S("norm_roots"), S("norm_means")
    acc_zero, taps_done, conv_middle, dve_conv = S("acc_zero"), S("taps_done"), S("conv_middle"), S("dve_conv")
    conv_gate_done, gelu_done, conv_value_done = S("conv_gate_done"), S("gelu_done"), S("conv_value_done")
    feature_hi_done, features_ready = S("feature_hi_done"), S("features_ready")
    final_means, final_roots, final_gated, final_done = S("final_means"), S("final_roots"), S("final_gated"), S("final_done")
    x1_in = [S("x1_in0"), S("x1_in1")]
    y_stored = [S("y_stored0"), S("y_stored1")]

    def tile_cols(w, kt, c0):
        return w.rearrange("(k p) c -> p k c", p=P)[:, 0:kt, c0:c0 + P]

    cols_of = {"q": CQ, "k": CK, "v": CV, "o": CO, "u": CU, "ga": CGA, "gb": CGB}

    def unit_source(s):
        if s < NM:
            kind, idx = mains[s]
            return tile_cols(w_in[0], KD, cols_of[kind] + idx * P), KD
        if s < S_YA:
            return tile_cols(w_br_b[0], 4, (s - S_BR) * P), 4
        if s < S_OUT:
            return tile_cols(w_br_a[0], KD, (s - S_YA) * P), KD
        return w_out[0][(s - S_OUT) * P:(s - S_OUT + 1) * P, :], None

    def unit_width(s):
        return 512 if S_BR <= s < S_YA else 1024

    w_up_t = w_up[0].rearrange("(k p) f -> p k f", p=P)

    def lin(at, step, i):
        return at if i is None else i * step + at

    def row_parts(b):
        return [(0, 1, CTX), (CTX, (BW - CTX) // ROW, ROW)] if b == 0 else [(0, BW // ROW, ROW)]

    def put_out(eng, t):
        eng.wait_ge(final_done, t + 1)
        dst = y_prompt[0] if t == 0 else y_sample[0, (t - 1) * P:t * P, :]
        eng.dma_start(dst, acc[:, t, :]).then_inc(y_stored[t % 2], 16)

    def stage_order():
        out = []
        for m, (kind, idx) in enumerate(mains):
            if m in TURN_AT:
                h, j = TURN_AT[m]
                out += [("hm", 2 * h + j)]
            if kind in ("o", "ga", "gb"):
                out.append((kind, idx))
            out += [("pool", group) for group, step in pool_steps(m) if step == 1]
        return out + [("hm", 2 * NH - 2), ("hm", 2 * NH - 1)]

    stage_no = {it: w for w, it in enumerate(stage_order())}
    store_of, stores = {}, {}
    for it, w in stage_no.items():
        sem = head_stored[w % 2] if it[0] == "hm" and it[1] < HG else stored[w % 2]
        stores[id(sem)] = stores.get(id(sem), 0) + 16
        store_of[it] = (sem, stores[id(sem)])
    staged = list(stage_no)

    ROW_BANK = (0, 1, 2, 6)
    NORM_AFTER = (2, 5, 8)

    def out_bank(t):
        return 2 if t % 2 else 4


    SPLIT_AT = [[S_YA + d + 2] for d in range(5)]
    SPLIT_AT += [[S_OUT - 1, S_OUT, S_OUT + 1], [S_OUT + 2, S_OUT + 3], [S_OUT + 4, S_OUT + 5, S_OUT + 6]]

    def gate_rows(pe, coef, cond, n):
        pe.wait_ge(coef2, 1)
        if n:
            pe.wait_ge(gate_bcast_copied, n)
        for k in range(KD):
            mm = pe.matmul(ps[:, 6 + k // 4, (k % 4) * P:(k % 4 + 1) * P],
                           coef[:, k, cond:cond + 1].to_broadcast([P, P]), ident[:, :], start=True, stop=True)
        mm.then_inc(gate_bcast_done, 1)

    def vcol(col, i):
        return vT[:, col:col + 1] if i is None else vT[:, bass.ds(i * 4 + col, 1)]

    def evac_main(act, q0, dst, scale, after_first):
        for b in range(NB):
            act.wait_ge(done0, q0 + b + 1)
            act.activation(dst[:, b * BW:(b + 1) * BW], ps[:, b, 0:BW], ACT.Copy, scale=scale).then_inc(evac0, 1)
            if b == 0:
                after_first()

    def free_slot(eng, s):
        if s < RS:
            return
        if s - RS < S_BR:
            eng.wait_ge(done0, unit_done_q(s - RS))
        elif s - RS < S_YA:
            eng.wait_ge(done1, 3 * (s - RS - S_BR + 1))
        elif s < S_OUT:
            eng.wait_ge(done0, 3 * (U_YA + s - RS - S_YA + 1))
        elif s < S_OUT + WO:
            eng.wait_ge(done1, 3 * KD)
        elif s < S_FF:
            eng.wait_ge(done0, 3 * (U_YA + s - S_OUT + 1))
        else:
            eng.wait_ge(ring_read, 1)

    with nc.Block() as block:
        @block.sync
        def _(sp):
            sp.dma_start(ident[:, :], consts[:, H_ID:H_ID + P]).then_inc(ident_in, 16)

            def ada_load(g):
                for kh in range(2):
                    ks = slice(kh * KD // 2, (kh + 1) * KD // 2)
                    src = w_ada[0].rearrange("(k p) c -> p k c", p=P)[:, ks, g * 512:(g + 1) * 512]
                    sp.dma_start(adaw[:, g, ks, :], src).then_inc(ada_in[2 * g + kh], 16)

            def x_load(b):
                if b == 0:
                    sp.dma_start(X0[:, 0, :], x_prompt[0]).then_inc(x_block_in[0], 16)
                t0 = max(b * TB, 1)
                rows = x_sample[0, (t0 - 1) * P:((b + 1) * TB - 1) * P, :]
                sp.dma_start(X0[:, t0:(b + 1) * TB, :], rows.rearrange("(t p) d -> p t d", p=P)).then_inc(x_block_in[b], 16)

            x_load(0)
            ada_load(0)
            vecA = [b_ada[0], g_pre_mix[0], g_post_mix[0], g_pre_ffn[0], g_post_ffn[0],
                    g_head[0].rearrange("h v -> (h v)"), pool_scale[0], c_ctx, c[0]]
            at = 0
            for v in vecA:
                n = v.shape[0] // P
                sp.dma_start(vecs[at:at + n, 0, :], v.rearrange("(r p) -> r p", p=P)).then_inc(vectors_in, 16)
                at += n
            for j, o, v in ((1, 0, conv_w[0, 0]), (1, 44, conv_w[0, 1]), (2, 0, conv_w[0, 2]), (2, 44, conv_b[0])):
                sp.dma_start(vecs[o:o + 44, j, :], v.rearrange("(r p) -> r p", p=P)).then_inc(vectors_in, 16)
            for g in range(1, AG):
                if g == AG - 1:
                    x_load(1)
                    x_load(2)
                ada_load(g)
            sp.dma_start(stage[1][:, 0:8 * P], consts[:, H_SEL:H_SEL + 8 * P]).then_inc(consts_in, 16)
            sp.dma_start(mask32[:, :], consts[:, H_MASK:H_MASK + 2 * P]).then_inc(consts_in, 16)

            for n, it in enumerate(raw_items):
                if n >= RS:
                    prev = raw_items[n - RS]
                    if prev[0] == "ada":
                        sp.wait_ge(ada_summed, prev[1] - ADA0 + 1)
                    else:
                        sp.wait_ge(lo_ready, prev[1] + 1)
                if it[0] == "ada":
                    src, kt = tile_cols(w_ada[0], KD, it[1] * P), KD
                else:
                    src, kt = unit_source(it[1])
                dst = raw[:, n % RS, :] if kt is None else raw[:, n % RS, 0:kt * P].rearrange("p (k c) -> p k c", c=P)
                sp.dma_start(dst, src).then_inc(landed[n % RS], 16)

            def ff_load(j, i, src, by_tile):
                n0 = N_FF + j
                sp.wait_ge(lo_ready, lin(S_FF + j - RS + 1, 12, i))
                dst = raw[:, n0 % RS, :]
                if by_tile:
                    dst = dst.rearrange("p (k c) -> p k c", c=P)
                sp.dma_start(dst, src).then_inc(landed[n0 % RS], 16)

            def up_src(f, i, half):
                if i is None:
                    return w_up_t[:, :, f * P + half * DFF:(f + 1) * P + half * DFF]
                return w_up_t[:, :, bass.ds(i * (4 * P) + (f * P + half * DFF), P)]

            def down_src(f, i):
                if i is None:
                    return w_down[0][f * P:(f + 1) * P, :]
                return w_down[0][bass.ds(i * (4 * P) + f * P, P), :]

            for j in range(4):
                ff_load(j, None, up_src(j // 2, None, j % 2), True)
            with sp.Fori(0, (NC - 1) // 2) as i:
                for cc in range(2):
                    for j in range(4):
                        ff_load(4 + 6 * cc + j, i, up_src(2 + 2 * cc + j // 2, i, j % 2), True)
                    for j in range(2):
                        ff_load(8 + 6 * cc + j, i, down_src(2 * cc + j, i), False)
            for j in range(2):
                ff_load(4 + 6 * (NC - 1) + j, None, down_src(NF - 2 + j, None), False)
            sp.wait_ge(features_ready, NB * NF)
            for t in range(NT):
                if t >= 2:
                    put_out(sp, t - 2)
                sp.dma_start(x1ld[:, t % 2, :], x1_dram[t]).then_inc(x1_in[t % 2], 16)
            put_out(sp, NT - 2)
            put_out(sp, NT - 1)
            for d in range(2):
                sp.wait_ge(y_stored[d], 16 * ((NT + 1 - d) // 2))
            sp.wait_ge(new_state_stored, 16 * 4 * NH)
            sp.wait_ge(new_m_stored, 32)

        @block.gpsimd
        def _(pool):
            rr = reset[:, :].rearrange("p (t s) -> p t s", s=P)
            fills = ((reset[:, :], 1.0), (rr[0:4, :, 0:1], 0.0), (rr[32:36, :, P - 1:P], 0.0), (gbias[:, :], 0.0),
                     (m0t[:, :], 0.0), (mprev[:, :], 0.0), (ones[:, :], 1.0))
            for n, (out, value) in enumerate(fills):
                pool.memset(out, value).then_inc(pool_seq, 1)
                pool.wait_ge(pool_seq, n + 1)
            bg = b_gates[0].rearrange("(r c) -> r c", c=1)
            for d in range(2):
                pool.dma_start(gbias[32 * d:32 * d + 4, 0:1], bg[4 * d:4 * d + 4, :]).then_inc(small_in, 16)
                pool.dma_start(gbias[32 * d:32 * d + 4, 1:2], bg[8 + 4 * d:12 + 4 * d, :]).then_inc(small_in, 16)
                pool.dma_start(m0t[32 * d:32 * d + 4, :], state_m[0, 0, d].rearrange("(r c) -> r c", c=1)).then_inc(small_in, 16)
            pool.dma_start(wgate[:, :, :], w_in[0].rearrange("(k p) c -> p k c", p=P)[:, :, CG:CG + 16]).then_inc(small_in, 16)
            pool.dma_start(poolM[:, :, :], consts[:, H_POOL:H_POOL + 8 * P].rearrange("p (m c) -> p m c", c=P)).then_inc(small_in, 16)
            pool.dma_start(wpool[:, :, :], w_pool[0].rearrange("g c d -> c g d")).then_inc(small_in, 16)
            for n, out in enumerate((GS, YS)):
                pool.memset(out[:, :].bitcast(F32), 0.0).then_inc(pool_seq, 1)
                pool.wait_ge(pool_seq, len(fills) + n + 1)
            pool.wait_ge(gate_rows_ready, 1)
            nm = new_m[0, 0]
            pool.dma_start(nm[0].rearrange("(r c) -> r c", c=1), Gt[4][0:4, CTX - 1:CTX]).then_inc(new_m_stored, 16)
            pool.dma_start(nm[1].rearrange("(r c) -> r c", c=1), Gt[4][32:36, 0:1]).then_inc(new_m_stored, 16)
            for h in range(NH):
                if h:
                    pool.wait_ge(att_outputs, 18 * h)
                for d in range(2):
                    pool.dma_start(Cst[:, d, 0:DV], state_C[0, 0, d, h]).then_inc(state_in, 16)
                    pool.dma_start(Cst[:, d, DV:VW], state_n[0, 0, d, h].rearrange("(r c) -> r c", c=1)).then_inc(state_in, 16)
                pool.wait_ge(att_state, 18 * h + 2)
                for d in range(2):
                    pool.dma_start(new_C[0, 0, d, h], Cctx[:, d, 0:DV]).then_inc(new_state_stored, 16)
                    pool.dma_start(new_n[0, 0, d, h].rearrange("(r c) -> r c", c=1), Cctx[:, d, DV:VW]).then_inc(new_state_stored, 16)

                if h:
                    pool.wait_ge(evac0, 3 * use_of[("turn", min(2 * h + 3, 2 * NH - 1))] + 3)
                    for j in range(2):
                        pool.wait_ge(*store_of[("o", 2 * h - 2 + j)])
                        if h > 1:
                            pool.wait_ge(head_staged, 2 * (h - 1))
                        pool.dma_start(work[j][:, :], Z["o"][2 * h - 2 + j]).then_inc(o_in[j], 16)
                    for j in range(2):
                        n = stage_no[("hm", 2 * h - 2 + j)]
                        pool.wait_ge(head_staged, 2 * h - 1 + j)
                        pool.dma_start(Z["hm"][2 * h - 2 + j], stage[n % 2][:, :]).then_inc(head_stored[n % 2], 16)
                if h == NH - 1:
                    pool.wait_ge(evac0, 3 * use_of[("hm", 2 * (NH - 2) + 1)] + 3)
                    for g in range(4):
                        pool.wait_ge(*store_of[("pool", g)])
                        pool.dma_start(pF[:, g, :], Z["pool"][g]).then_inc(pooled_in, 16)

            pool.wait_ge(att_scores, NT * NH)
            for w, (what, d) in enumerate(loads):
                if w == 2:
                    pool.wait_ge(att_outputs, 2 * NT * NH)
                    pool.wait_ge(att_state, 2 * NT * NH)
                    pool.wait_ge(new_state_stored, 16 * 4 * NH)
                pool.wait_ge(*store_of[(what, d)])
                if w >= LS:
                    last, e = loads[w - LS]
                    if last == "gb":
                        pool.wait_ge(evac1, NB * (e + 1))
                    elif last == "o":
                        pool.wait_ge(head_gated, e - HG + 1)
                    elif last == "hm":
                        pool.wait_ge(tile_used, e + 1)
                    else:
                        pool.wait_ge(tile_used, KD + e + 1)
                pool.dma_start(tiles[:, w % LS, :], Z[what][d]).then_inc(tile_in[w % LS], 16)
            pool.wait_ge(mix_sum, NB)
            for t in range(NT):
                if t >= 2:
                    pool.wait_ge(x1_stored[t % 2], 16 * (t // 2))
                    pool.wait_ge(x_scaled, NT + t - 1)
                src = x_prompt[0] if t == 0 else x_sample[0, (t - 1) * P:t * P, :]
                pool.dma_start(xld[:, t % 2, :], src).then_inc(x_in[t % 2], 16)
                if t >= 1:
                    pool.wait_ge(x1_ready, t)
                    pool.dma_start(x1_dram[t - 1], xld[:, (t - 1) % 2, :]).then_inc(x1_stored[(t - 1) % 2], 16)
            pool.wait_ge(x1_ready, NT)
            pool.dma_start(x1_dram[NT - 1], xld[:, (NT - 1) % 2, :]).then_inc(x1_stored[(NT - 1) % 2], 16)
            pool.wait_ge(done2, NT)
            pool.memset(acc[:, :, :], 0.0).then_inc(acc_zero, 1)
            for t in range(NT - 1):
                pool.wait_ge(final_gated, t + 1)
                pool.wait_ge(x1_in[t % 2], 16 * (t // 2 + 1))
                pool.tensor_tensor(acc[:, t, :], acc[:, t, :], x1ld[:, t % 2, :], ALU.add).then_inc(final_done, 1)

        @block.tensor
        def _(pe):
            def take0(q):
                if q >= 3:
                    pe.wait_ge(evac0, q - 2)

            def mm3(out, whi, wlo, xhi, xlo, first, last):
                pe.matmul(out, whi, xhi, start=first, stop=False)
                pe.matmul(out, whi, xlo, start=False, stop=False)
                return pe.matmul(out, wlo, xhi, start=False, stop=last)

            def block_product(out, s, b, kt, xhi, xlo, pieces=None):
                r = s % RS
                for k in range(kt):
                    w = slice(k * P, (k + 1) * P)
                    tok = slice(b * BW, (b + 1) * BW)
                    mm = mm3(out, ring_hi[:, r, w], ring_lo[:, r, w], xhi[:, k, tok], xlo[:, k, tok], k == 0, k == kt - 1)
                return mm

            pe.wait_ge(ident_in, 16)
            pe.wait_ge(vectors_in, 16 * 13)
            pe.transpose(ps[:, 3, 0:108], vecs[0:108, 0, :], ident[0:108, 0:108])
            pe.transpose(ps[:, 3, 108:196], vecs[0:88, 1, :], ident[0:88, 0:88])
            pe.transpose(ps[:, 3, 196:284], vecs[0:88, 2, :], ident[0:88, 0:88]).then_inc(vec_done, 1)

            def ada_sum(a):
                pe.wait_ge(ada_summed, a - ADA0 + 1)
                for cond in range(2):
                    mm = pe.matmul(ps[:, 0, 400 + cond:401 + cond], ada_part[:, cond, :], ones[:, :], start=True, stop=True)
                mm.then_inc(ada_used, 1)

            def norm_turn(Xt, out, b, k):
                for j in range(TB):
                    mm = pe.transpose(out[:, j * P:(j + 1) * P], Xt[:, b * TB + j, k * P:(k + 1) * P], ident[:, :])
                return mm

            def first_norm(b, k):
                w = b * KD + k
                if w >= 4:
                    pe.wait_ge(xt_free, w - 3)
                norm_turn(X0, ps[:, 3 + w % 4, :], b, k).then_inc(xt_done, 1)

            pe.wait_ge(cond_done, 1)
            for g in range(AG):
                for k in range(KD):
                    if k % (KD // 2) == 0:
                        pe.wait_ge(ada_in[2 * g + k // (KD // 2)], 16)
                    mm = pe.matmul(ps[0:2, ROW_BANK[g], :], condT[:, :, k], adaw[:, g, k, :], start=(k == 0), stop=(k == KD - 1))
                mm.then_inc(row_done, 1)
            for a in range(ADA0):
                pe.wait_ge(row_read, a // 4 + 1)
                mm = pe.transpose(ps[:, 7, 2 * a:2 * a + 2], ada_row[:, a // 4, (a % 4) * P:(a % 4 + 1) * P], ident[0:2, 0:2])
            mm.then_inc(ada_used, ADA0)
            pe.wait_ge(x_scaled, TB)
            for k in range(KD):
                first_norm(0, k)
            pe.wait_ge(lo_ready, 1)
            for b in range(NB):
                if b + 1 < NB:
                    pe.wait_ge(x_scaled, TB * (b + 2))
                for k in range(KD):
                    if b + 1 < NB:
                        first_norm(b + 1, k)
                    pe.wait_ge(h_split_done, b * KD + k + 1)
                    w = slice(k * P, (k + 1) * P)
                    tok = slice(b * BW, (b + 1) * BW)
                    mm = mm3(ps[:, b, 0:BW], ring_hi[:, 0, w], ring_lo[:, 0, w], H_hi[:, k, tok], H_lo[:, k, tok],
                             k == 0, k == KD - 1)
                mm.then_inc(done0, 1)

            def attention_scores(h, i):
                e = h * 9 + i
                cf, cb = (0, 0) if i == 0 else (i, NT - i)
                v = h % 2
                if i == 0:
                    mk = mains.index(("k", h))
                    pe.wait_ge(evac0, 3 * use_of[("main", mk)] + 3)
                    if h == 0:
                        pe.wait_ge(gate_cols_ready, 1)
                if e:
                    pe.wait_ge(att_weights, e)
                for d, cx in ((0, cf), (1, cb)):
                    tok = slice(cx * P, (cx + 1) * P)
                    j = d * NH + h
                    o = d * P
                    pe.matmul(ps[:, 3, o:o + P], idbf[:, :], maskbf[:, d, :], start=True, stop=False)
                    pe.matmul(ps[:, 3, o:o + P], sel[:, j, :], GS[:, tok], start=False, stop=True)
                    pe.matmul(ps[:, 3, 256 + o:256 + o + P], sel[:, j, :], YS[:, tok], start=True, stop=True)
                    pe.matmul(ps[:, 4, o:o + P], kT[v][:, tok], qT[v][:, tok], start=True, stop=True)
                    mm = pe.transpose(ps[:, 4, 256 + o:256 + o + P], kT[v][:, tok], ident[:, :])
                mm.then_inc(att_scores, 1)

            def attention_values(h, i, d):
                e = h * 9 + i
                cx = 0 if i == 0 else (i, NT - i)[d]
                v = h % 2
                pe.wait_ge(att_weights, e + 1)
                if i == 0 and d == 0:
                    pe.wait_ge(evac0, 3 * use_of[("turn", 2 * h + 1)] + 3)
                    if h == 0:
                        pe.wait_ge(ones_done, 1)
                if i == 1 and d == 0:
                    pe.wait_ge(state_in, 64 * (h + 1))
                if e or d:
                    pe.wait_ge(att_outputs, 2 * e + d)
                    pe.wait_ge(att_state, 2 * e + d)
                pe.matmul(ps[:, 5 + d, 0:VW], Pt[:, d, :], vaug[v][:, cx, :], start=True, stop=(i == 0))
                if i:
                    pe.matmul(ps[:, 5 + d, 0:VW], qs[:, d, :], Cst[:, d, :], start=False, stop=True)
                pe.matmul(ps[:, 7, 0:VW], k_weighted[:, d, :], vaug[v][:, cx, :], start=True, stop=True).then_inc(att_values, 1)

            def turn(one, q0):
                for b in range(NB):
                    take0(q0 + b)
                    for j in range(TB):
                        mm = one(ps[:, b, j * P:(j + 1) * P], b * TB + j)
                    mm.then_inc(done0, 1)

            def hm_turn(h, j):
                pe.wait_ge(hscaled, h + 1)
                turn(lambda o, t: pe.transpose(o, hm[h % 2][:, t, j * P:(j + 1) * P], ident[:, :]),
                     3 * use_of[("hm", 2 * h + j)])

            for m, (kind, idx) in enumerate(mains):
                seg = m - SEG
                if m in TURN_AT:
                    hm_turn(*TURN_AT[m])
                q0 = 3 * use_of[("main", m)]
                if m == 0:
                    continue
                take0(q0)
                if m in ADA_AT:
                    ada_sum(ADA_AT[m])
                pe.wait_ge(lo_ready, m + 1)
                for b in range(NB):
                    take0(q0 + b)
                    block_product(ps[:, b, 0:BW], m, b, KD, H_hi, H_lo).then_inc(done0, 1)
                    if seg >= 0:
                        if b == 0:
                            attention_scores(seg // 9, seg % 9)
                        else:
                            attention_values(seg // 9, seg % 9, b - 1)
                for group, step in pool_steps(m):
                    if step == 0:
                        if group == 0:
                            pe.wait_ge(small_in, 16 * 9)
                        pe.wait_ge(evac0, 3 * use_of[("main", m - 1)] + 3)
                        one = lambda o, t: pe.matmul(o, work[group % 2][:, t * P:(t + 1) * P], wpool[:, group, :],
                                                     start=True, stop=True)
                    else:
                        pe.wait_ge(evac0, 3 * use_of[("pool", group, 0)] + 3)
                        one = lambda o, t: pe.matmul(o, mixed[group % 2][:, t * P:(t + 1) * P],
                                                     poolM[:, 2 * group + (t > 0), :], start=True, stop=True)
                    turn(one, 3 * use_of[("pool", group, step)])
                if m and mains[m - 1][0] == "v":
                    vi = mains[m - 1][1]
                    pe.wait_ge(evac0, 3 * use_of[("main", m - 1)] + 3)
                    turn(lambda o, t: pe.transpose(o, work[vi % 2][:, t * P:(t + 1) * P], ident[:, :]),
                         3 * use_of[("turn", vi)])
                if m == 2:
                    pe.wait_ge(gate_rows_ready, 1)
                    for t in range(NT):
                        pe.transpose(ps[:, 3, t * GR:(t + 1) * GR], Gt[6][0:GR, t * P:(t + 1) * P], ident[0:GR, 0:GR])
                    for t in range(NT):
                        mm = pe.transpose(ps[:, 4, t * GR:(t + 1) * GR], Gt[4][0:GR, t * P:(t + 1) * P], ident[0:GR, 0:GR])
                    mm.then_inc(gate_cols_done, 1)
            for d in range(KD):
                s = S_BR + d
                if d == 0:
                    pe.wait_ge(pooled_lo_done, 4)
                    pe.wait_ge(att_weights, NT * NH)
                pe.wait_ge(lo_ready, s + 1)
                for b in range(NB):
                    if b == NB - 1 and d == 0:
                        pe.wait_ge(att_outputs, 2 * NT * NH)
                    if d:
                        pe.wait_ge(evac1, 3 * (d - 1) + b + 1)
                    block_product(ps[:, 3 + b, 0:BW], s, b, 4, pT_hi, pT_lo).then_inc(done1, 1)
                if d in (1, 2):
                    hm_turn(NH - 1, d - 1)
            for d in range(KD):
                s = S_YA + d
                pe.wait_ge(lo_ready, s + 1)
                for b in range(NB):
                    take0(3 * (U_YA + d) + b)
                    r = s % RS
                    for k in range(KD):
                        if d == 0 and b == 0:
                            pe.wait_ge(tile_used, k + 1)
                        w = slice(k * P, (k + 1) * P)
                        tok = slice(b * BW, (b + 1) * BW)
                        mm = mm3(ps[:, b, 0:BW], ring_hi[:, r, w], ring_lo[:, r, w], H_hi[:, k, tok], H_lo[:, k, tok],
                                 k == 0, k == KD - 1)
                    mm.then_inc(done0, 1)
            def out_product(t):
                bank = out_bank(t)
                if t == 1:
                    take0(Q_FF + 2)
                if t >= 2:
                    pe.wait_ge(evac2, t - 1)
                if t % TB == 0:
                    pe.wait_ge(mix_ready, KD * (t // TB + 1))
                tok = slice(t * P, (t + 1) * P)
                order = list(range(WO, KD)) + list(range(WO)) if t == NT - 1 else list(range(KD))
                for n, k in enumerate(order):
                    if t == 0:
                        pe.wait_ge(lo_ready, S_OUT + k + 1)
                    whi, wlo = split_of(S_OUT + k)
                    for x, w, first, last in ((H_hi, whi, True, False), (H_hi, wlo, False, False), (H_lo, whi, False, True)):
                        for hb in range(2):
                            mm = pe.matmul(ps[:, bank + hb, :], x[:, k, tok], w[:, hb * 512:(hb + 1) * 512],
                                           start=(n == 0 and first), stop=(n == KD - 1 and last))
                    if t == NT - 1 and k == KD - 1:
                        mm.then_inc(ring_read, 1)
                    if t - 2 in NORM_AFTER:
                        second_norm(NORM_AFTER.index(t - 2), n)
                mm.then_inc(done2, 1)

            def second_norm(b, k):
                if k == 0:
                    pe.wait_ge(x_scaled, NT + TB * (b + 1))
                w = b * KD + k
                if w >= 2:
                    pe.wait_ge(xt_free, NB * KD + w - 1)
                norm_turn(X1, ps[:, 6 + w % 2, :], b, k).then_inc(xt_done, 1)

            pe.wait_ge(evac1, 3 * KD)
            for t in range(NT):
                out_product(t)
                if t < 2:
                    gate_rows(pe, coefG1, t, t)
                if t == NORM_AFTER[0]:
                    pe.wait_ge(gate_bcast_copied, 2)

            def up_block(r, bank, done, freed, f, b, i):
                if f >= 1:
                    pe.wait_ge(freed, lin(3 * f + b - 2, 12, i))
                for k in range(KD):
                    w = slice(k * P, (k + 1) * P)
                    tok = slice(b * BW, (b + 1) * BW)
                    mm = mm3(ps[:, bank + b, 0:BW], ring_hi[:, r, w], ring_lo[:, r, w], H_hi[:, k, tok],
                             H_lo[:, k, tok], k == 0, k == KD - 1)
                mm.then_inc(done, 1)

            def up_unit(r, bank, done, freed, f, i):
                for b in range(NB):
                    up_block(r, bank, done, freed, f, b, i)

            def up_feature(j, f, i):
                pe.wait_ge(lo_ready, lin(S_FF + j + 1, 12, i))
                up_unit((S_FF + j) % RS, 0, done0, conv_gate_done, f, i)
                pe.wait_ge(lo_ready, lin(S_FF + j + 2, 12, i))
                up_unit((S_FF + j + 1) % RS, 3, done1, conv_value_done, f, i)

            def up_chunk(j0, f0, i):
                for e in range(2):
                    up_feature(j0 + 2 * e, f0 + e, i)

            def down_chunk(j0, ch, i):
                pe.wait_ge(lo_ready, lin(S_FF + j0 + 2, 12, i))
                pe.wait_ge(gate_bcast_copied, 4)
                pe.wait_ge(features_ready, lin(6 * (ch + 1), 12, i))
                slot = ch % 2
                for t in range(NT):
                    tok = slice(t * P, (t + 1) * P)
                    for hb in range(2):
                        pe.wait_ge(evac2, lin(NT + 18 * ch + 2 * t + hb - 1, 36, i))
                        cols = slice(hb * 512, (hb + 1) * 512)
                        out = ps[:, 6 + hb, :]
                        for k in range(2):
                            r = (S_FF + j0 + k) % RS
                            pe.matmul(out, fT_hi[:, slot, k, tok], ring_hi[:, r, cols], start=(k == 0), stop=False)
                            pe.matmul(out, fT_hi[:, slot, k, tok], ring_lo[:, r, cols], start=False, stop=False)
                            mm = pe.matmul(out, fT_lo[:, slot, k, tok], ring_hi[:, r, cols], start=False, stop=(k == 1))
                        mm.then_inc(done2, 1)

            def first_up(half, b, turns):
                bank, done = ((0, done0), (3, done1))[half]
                r = (S_FF + half) % RS
                if b == 0:
                    pe.wait_ge(lo_ready, S_FF + half + 1)
                    pe.wait_ge(evac2, NT) if half else pe.wait_ge(evac0, Q_FF)
                pe.wait_ge(h_split_done, KD * (NB + b + 1))
                for k in range(KD):
                    w = slice(k * P, (k + 1) * P)
                    tok = slice(b * BW, (b + 1) * BW)
                    mm = mm3(ps[:, bank + b, 0:BW], ring_hi[:, r, w], ring_lo[:, r, w], H_hi[:, k, tok],
                             H_lo[:, k, tok], k == 0, k == KD - 1)
                    if turns and k % 2:
                        second_norm(NB - 1, b * KD // 2 + k // 2)
                mm.then_inc(done, 1)

            for half, b in ((0, 0), (0, 1), (1, 0), (1, 1), (0, 2), (1, 2)):
                first_up(half, b, half == 1 and b < NB - 1)
            pe.wait_ge(xt_free, 2 * NB * KD)
            gate_rows(pe, coefG2, 0, 2)
            up_feature(2, 1, None)
            gate_rows(pe, coefG2, 1, 3)
            with pe.Fori(0, (NC - 1) // 2) as i:
                for cc in range(2):
                    up_chunk(4 + 6 * cc, 2 + 2 * cc, i)
                    down_chunk(8 + 6 * cc, cc, i)
            down_chunk(4 + 6 * (NC - 1), NC - 1, None)

        @block.scalar
        def _(act):
            seq = [0]

            def link(ins):
                seq[0] += 1
                ins.then_inc(act_seq, 1)
                act.wait_ge(act_seq, seq[0])

            def hi_split(s):
                if s >= S_FF:
                    return ff_hi(s - S_FF, None)
                n = raw_n(s)
                w = unit_width(s)
                act.wait_ge(landed[n % RS], 16 * (n // RS + 1))
                free_slot(act, s)
                act.activation(split_of(s)[0][:, 0:w], raw[:, n % RS, 0:w], ACT.Copy).then_inc(hi_ready, 1)

            def ff_hi(j, i):
                n0 = N_FF + j
                r = (S_FF + j) % RS
                act.wait_ge(landed[n0 % RS], lin(16 * (n0 // RS + 1), 16 * (12 // RS), i))
                if j < RS:
                    free_slot(act, S_FF + j)
                else:
                    p = j - RS
                    if p < 4:
                        if p % 2:
                            act.wait_ge(done1, lin(3 * KD + 3 * (p // 2 + 1), 12, i))
                        else:
                            act.wait_ge(done0, lin(Q_FF + 3 * (p // 2 + 1), 12, i))
                        if p >= 2 and i is not None:
                            act.wait_ge(done2, lin(NT, 36, i))
                    else:
                        ch, at = 1 + (p - 4) // 6, (p - 4) % 6
                        if at < 4:
                            f = 2 * ch + at // 2
                            act.wait_ge(done1 if at % 2 else done0, lin((3 * KD if at % 2 else Q_FF) + 3 * (f + 1), 12, i))
                        else:
                            act.wait_ge(done2, lin(NT + 18 * ch, 36, i))
                act.activation(ring_hi[:, r, :], raw[:, n0 % RS, :], ACT.Copy).then_inc(hi_ready, 1)

            act.wait_ge(vec_done, 2)
            act.activation(condT[:, :, :], vT[:, V_C:V_C + 16].rearrange("p (c k) -> p c k", c=2), ACT.Silu).then_inc(cond_done, 1)
            def x_stats(b):
                act.wait_ge(x_block_in[b], 32 if b == 0 else 16)
                tiles = slice(b * TB, (b + 1) * TB)
                for t in range(b * TB, (b + 1) * TB):
                    if t:
                        act.wait_ge(x_squares, t)
                    act.activation(stage[0][:, 0:DM], X0[:, t, :], ACT.Square, accum_out=stat[:, 0, t:t + 1]).then_inc(x_squares, 1)
                act.wait_ge(x_roots, 2 * b + 1)
                act.activation(stat[:, 2, tiles], stat[:, 1, tiles], ACT.Sqrt).then_inc(x_roots, 1)

            x_stats(0)
            for g in range(AG):
                if g == AG - 1:
                    x_stats(1)
                    x_stats(2)
                act.wait_ge(row_done, g + 1)
                act.activation(ada_row[:, g, :], ps[0:2, ROW_BANK[g], :], ACT.Copy).then_inc(row_read, 1)

            def norm_evac(src_of, ready, freed, coefA, sh, n0, tile, slots, b, ks=range(KD)):
                for k in ks:
                    w = n0 + b * KD + k
                    ready(b * KD + k)
                    if w - n0 >= slots:
                        act.wait_ge(h_split_done, w - slots + 1)
                    parts = [(0, 0, P), (1, P, BW)] if b == 0 else [(1, 0, BW)]
                    for cond, lo, hi in parts:
                        outs = [tile[:, w % slots, lo:hi]]
                        if b and k % 2:
                            outs.append(H_hi[:, k, b * BW + lo:b * BW + hi])
                        for out in outs:
                            ins = act.activation(out, src_of(b * KD + k)[:, lo:hi], ACT.Identity,
                                                 scale=coefA[:, k, cond:cond + 1], bias=modT[:, sh + k, cond:cond + 1])
                    ins.then_inc(freed, 1)

            act.wait_ge(coef1, 1)
            for b in range(NB):
                norm_evac(lambda w: ps[:, 3 + w % 4, :], lambda w: act.wait_ge(xt_done, w + 1), xt_free, coefA1, 0, 0, tsc, 4, b)


            def stage_slot(item):
                w = stage_no[item]
                if w >= 2:
                    act.wait_ge(*store_of[staged[w - 2]])
                return w % 2

            def put(item, q_end):
                w = stage_no[item]
                act.wait_ge(evac0, q_end)
                act.dma_start(Z[item[0]][item[1]], stage[w % 2][:, :]).then_inc(stored[w % 2], 16)

            def evac_copy(q0, dst, scale=None, func=ACT.Copy):
                for b in range(NB):
                    act.wait_ge(done0, q0 + b + 1)
                    out = dst(b)
                    src = ps[:, b, 0:BW]
                    if len(out.shape) == 3:
                        src = src.rearrange("p (t s) -> p t s", s=P)
                    kw_ = {} if scale is None else {"scale": scale}
                    act.activation(out, src, func, **kw_).then_inc(evac0, 1)

            def hm_evac(h, j):
                item = ("hm", 2 * h + j)
                st = stage_slot(item)
                q0 = 3 * use_of[item]
                evac_copy(q0, lambda b: stage[st][:, b * BW:(b + 1) * BW])
                if h == NH - 1:
                    put(item, q0 + 3)

            def sig(what, d):
                w = load_of[(what, d)]
                act.wait_ge(tile_in[w % LS], 16 * (w // LS + 1))
                act.activation(tiles[:, w % LS, :], tiles[:, w % LS, :], ACT.Sigmoid).then_inc(sigmoids_done, 1)

            def hm_norm(h):
                act.wait_ge(att_outputs, 18 * (h + 1))
                for t in range(NT):
                    if t:
                        act.wait_ge(head_squares, NT * h + t)
                    out = ps[:, 7, 0:DV] if h == NH - 1 else Wt[:, :, :].rearrange("p a b -> p (a b)")
                    act.activation(out, hm[h % 2][:, t, :], ACT.Square,
                                   accum_out=hstat[:, 0, t:t + 1]).then_inc(head_squares, 1)
                act.wait_ge(head_roots, 2 * h + 1)
                act.activation(hstat[:, 1, :], hstat[:, 0, :], ACT.Sqrt).then_inc(head_roots, 1)

            hi_split(1)
            for m, (kind, idx) in enumerate(mains):
                seg = m - SEG
                if m in TURN_AT:
                    h, j = TURN_AT[m]
                    hm_evac(h, j)
                    act.wait_ge(o_in[j], 16 * (h + 1))
                    act.activation(work[j][:, :], work[j][:, :], ACT.Sigmoid).then_inc(o_sigmoid, 1)
                hi_split(m + 2)
                q0 = 3 * use_of[("main", m)]
                if m in ADA_AT:
                    j = ADA_AT[m]
                    act.wait_ge(ada_used, j + 1)
                    act.wait_ge(done0, q0 + 1)
                    act.activation(modT[:, j, :], ps[:, 0, 400:402], ACT.Identity, bias=vT[:, V_BADA + j:V_BADA + j + 1])
                if kind == "gates":
                    act.wait_ge(small_in, 16 * 9)
                    for b in range(NB):
                        tok = slice(b * BW, (b + 1) * BW)
                        act.wait_ge(done0, q0 + b + 1)
                        act.activation(Gt[0][0:GR, tok], ps[0:GR, b, 0:BW], ACT.Identity, bias=gbias[0:GR, 0:1])
                        act.activation(Gt[1][0:GR, tok], ps[64:64 + GR, b, 0:BW], ACT.Identity, bias=gbias[0:GR, 1:2]).then_inc(evac0, 1)
                    act.wait_ge(evac0, q0 + 3)
                    link(act.activation(Gt[2][0:GR, :], Gt[1][0:GR, :], ACT.Abs))
                    link(act.activation(Gt[2][0:GR, :], Gt[2][0:GR, :], ACT.Exp, scale=-1.0))
                    act.activation(Gt[2][0:GR, :], Gt[2][0:GR, :], ACT.Ln, bias=1.0).then_inc(log_f_ready, 1)
                    continue
                if seg >= 0:
                    def exps():
                        h, i = seg // 9, seg % 9
                        e = h * 9 + i
                        cf, cb = (0, 0) if i == 0 else (i, NT - i)
                        act.wait_ge(att_scores, e + 1)
                        if e:
                            act.wait_ge(att_state, 2 * e)
                        for d, cx in ((0, cf), (1, cb)):
                            act.activation(Wt[:, d, :], ps[:, 3, d * P:(d + 1) * P], ACT.Exp, bias=a_tok[:, cx, d, h:h + 1])
                        act.activation(Et[:, :, :], ps[:, 3, 256:512].rearrange("p (a b) -> p a b", b=P), ACT.Exp).then_inc(att_exps, 1)
                else:
                    def exps():
                        pass
                if kind == "q":
                    evac_main(act, q0, qT[idx % 2], QSCALE, exps)
                elif kind == "k":
                    evac_main(act, q0, kT[idx % 2], 1.0, exps)
                elif kind in ("v", "u"):
                    evac_main(act, q0, work[idx % 2], 1.0, exps)
                else:
                    st = stage_slot((kind, idx))
                    evac_main(act, q0, stage[st], 1.0, exps)
                    put((kind, idx), q0 + 3)
                for group, step in pool_steps(m):
                    q1 = 3 * use_of[("pool", group, step)]
                    if step == 0:
                        evac_copy(q1, lambda b: mixed[group % 2][:, b * BW:(b + 1) * BW])
                    else:
                        st = stage_slot(("pool", group))
                        evac_copy(q1, lambda b: stage[st][:, b * BW:(b + 1) * BW], scale=vT[:, V_PS + group:V_PS + group + 1],
                                  func=ACT.Identity)
                        put(("pool", group), q1 + 3)
                if m and mains[m - 1][0] == "v":
                    vi = mains[m - 1][1]
                    q1 = 3 * use_of[("turn", vi)]
                    if vi == 0:
                        act.wait_ge(new_m_stored, 32)
                    evac_copy(q1, lambda b: vaug[(vi // 2) % 2][:, b * TB:(b + 1) * TB, (vi % 2) * P:(vi % 2 + 1) * P])
                if m == 2:
                    act.wait_ge(gate_cols_done, 1)
                    for src, dst, f, sc_ in ((3, a_tok, ACT.Copy, 1.0), (4, en_tok, ACT.Exp, -1.0)):
                        for d in range(2):
                            ins = act.activation(dst[:, :, d, :], ps[:, src, 0:NT * GR].rearrange("p (t r) -> p t r", r=GR)
                                                 [:, :, 32 * d:32 * d + NH], f, scale=sc_)
                    ins.then_inc(gate_cols_ready, 1)
                for g in POOL_SPLIT.get(m, ()):
                    act.wait_ge(pooled_in, 64)
                    act.activation(pT_hi[:, g, :], pF[:, g, :], ACT.Copy).then_inc(pooled_hi_done, 1)
                if m == NM - 1:
                    sig("gb", 0)
                if m in NORM_AT:
                    if m < NM - 1:
                        act.wait_ge(att_weights, seg + 1)
                    hm_norm(NORM_AT[m])

            for d in range(KD):
                hi_split(S_BR + d + 2)
                if d + 1 < KD:
                    sig("gb", d + 1)
                w = load_of[("hm", d)]
                if d < HG:
                    act.wait_ge(tile_in[w % LS], 16 * (w // LS + 1))
                else:
                    act.wait_ge(head_gated, d - HG + 1)
                act.activation(H_hi[:, d, :], tiles[:, w % LS, :], ACT.Copy).then_inc(head_hi_done, 1)
                if HG <= d + 1 < KD:
                    sig("o", d + 1)
                if d in (1, 2):
                    hm_evac(NH - 1, d - 1)
            for d in range(KD):
                for s in SPLIT_AT[d]:
                    hi_split(s)
                sig("ga", d)
            for b in range(NB):
                tok = slice(b * BW, (b + 1) * BW)
                act.wait_ge(mix_sum, b + 1)
                for k in range(KD):
                    act.activation(H_hi[:, k, tok], mixF[:, k, tok], ACT.Copy).then_inc(mix_hi_done, 1)
            hi_split(S_OUT + 7)

            def gate_copy(gtb, cond, n):
                act.wait_ge(gate_bcast_done, n + 1)
                act.activation(gtb[:, cond, :], ps[:, 6:8, :].rearrange("p a b -> p (a b)"), ACT.Copy).then_inc(gate_bcast_copied, 1)

            act.wait_ge(mix_ready, NB * KD)
            def second_evac(b, ks):
                norm_evac(lambda w: ps[:, 6 + w % 2, :], lambda w: act.wait_ge(xt_done, NB * KD + w + 1), xt_free,
                          coefA2, 24, 24, tsc2, 2, b, ks)

            for t in range(NT):
                if t < 2:
                    gate_copy(gtb1, t, t)
                if t == NT - 1:
                    hi_split(S_FF)
                    hi_split(S_FF + 1)
                pair = ps[:, out_bank(t):out_bank(t) + 2, :].rearrange("p a b -> p (a b)")
                act.wait_ge(done2, t + 1)
                act.activation(X1[:, t, :], pair, ACT.Square, accum_out=stat[:, 0, t:t + 1]).then_inc(norm_squares, 1)
                act.wait_ge(norm_means, 2 * t + 1)
                act.activation(stat[:, 2, t:t + 1], stat[:, 1, t:t + 1], ACT.Sqrt).then_inc(norm_roots, 1)
                if t - 1 in NORM_AFTER:
                    second_evac((t - 1) // TB, range(0, 3))
                act.wait_ge(x1_ready, t + 1)
                act.activation(X1[:, t, :], xld[:, t % 2, :], ACT.Square, accum_out=stat[:, 3, t:t + 1]).then_inc(norm_squares, 1)
                act.wait_ge(norm_means, 2 * t + 2)
                act.activation(hstat[:, 1, t:t + 1], hstat[:, 0, t:t + 1], ACT.Sqrt).then_inc(norm_roots, 1)
                if t - 1 in NORM_AFTER:
                    second_evac((t - 1) // TB, range(3, KD))
            second_evac(NB - 1, range(KD))

            def ff_up_act(f, e, slot, splits, i):
                first = V_W1 + f
                cols = slice(first, first + 5 * NF + 1, NF) if i is None else bass.ds(i * 4 + first, 6, NF)
                act.activation(taps[:, e, :], vT[:, cols], ACT.Copy).then_inc(taps_done, 1)
                act.wait_ge(taps_done, lin(f + 1, 4, i))
                for half in range(2):
                    for j in splits[half]:
                        ff_hi(j, i)
                    tile = conv_v if half else conv_g
                    for b in range(NB):
                        tok = slice(b * BW, (b + 1) * BW)
                        if half:
                            act.wait_ge(done1, lin(3 * KD + 3 * f + b + 1, 12, i))
                        else:
                            act.wait_ge(done0, lin(Q_FF + 3 * f + b + 1, 12, i))
                        if f:
                            act.wait_ge(features_ready, lin(3 * f + b - 2, 12, i))
                        act.activation(tile[:, tok], ps[:, b + 3 * half, 0:BW], ACT.Identity,
                                       scale=taps[:, e, half:half + 1], bias=taps[:, e, 4 + half:5 + half]).then_inc(conv_middle, 1)
                        if half:
                            act.wait_ge(conv_value_done, lin(3 * f + b + 1, 12, i))
                            act.activation(fT_hi[:, slot, e, tok], conv_v[:, tok], ACT.Copy).then_inc(feature_hi_done, 1)
                        else:
                            act.wait_ge(conv_gate_done, lin(3 * f + b + 1, 12, i))
                            act.activation(conv_g[:, tok], conv_g[:, tok], ACT.Gelu_apprx_tanh).then_inc(gelu_done, 1)

            act.wait_ge(x1_stored[0], 16 * ((NT + 1) // 2))
            act.wait_ge(x1_stored[1], 16 * (NT // 2))
            ff_up_act(0, 0, 0, [[2], [3]], None)
            gate_copy(gtb2, 0, 2)
            ff_up_act(1, 1, 0, [[4], []], None)
            gate_copy(gtb2, 1, 3)
            with act.Fori(0, (NC - 1) // 2) as i:
                for cc in range(2):
                    j = 4 + 6 * cc
                    ff_up_act(2 + 2 * cc, 0, 1 - cc, [[j + 1, j + 2], [j + 3]], i)
                    ff_up_act(3 + 2 * cc, 1, 1 - cc, [[j + 4], [j + 5]], i)
                    ff_hi(j + 6, i)
            ff_hi(5 + 6 * (NC - 1), None)
            for t in range(NT):
                act.wait_ge(evac2, NT + 18 * (NC - 1) + 2 * (t + 1))
                act.activation(ps[:, 0:2, :], acc[:, t, :].rearrange("p (a b) -> p a b", b=512), ACT.Square,
                               accum_out=stat[:, 0, t:t + 1]).then_inc(final_roots, 1)
                act.wait_ge(final_means, t + 1)
                act.activation(stat[:, 2, t:t + 1], stat[:, 1, t:t + 1], ACT.Sqrt).then_inc(final_roots, 1)

        @block.vector
        def _(dve):
            seq = [0]

            def link(ins):
                seq[0] += 1
                ins.then_inc(dve_seq, 1)
                dve.wait_ge(dve_seq, seq[0])

            def sub_hi(out, full, hi):
                return dve.tensor_tensor(out, full, hi.bitcast(F32), ALU.subtract)

            def lo_split(s):
                if s >= S_FF:
                    return ff_lo(s - S_FF, None)
                n, w = raw_n(s), unit_width(s)
                dve.wait_ge(hi_ready, s)
                if s == S_OUT + WO - 1:
                    dve.wait_ge(tile_used, KD + 1 + max(d for d in range(KD) if load_of[("ga", d)] % LS == LS - 1))
                hi, lo = split_of(s)
                sub_hi(lo[:, 0:w], raw[:, n % RS, 0:w], hi[:, 0:w]).then_inc(lo_ready, 1)

            def ff_lo(j, i):
                n0, r = N_FF + j, (S_FF + j) % RS
                dve.wait_ge(hi_ready, lin(S_FF + j, 12, i))
                sub_hi(ring_lo[:, r, :], raw[:, n0 % RS, :], ring_hi[:, r, :]).then_inc(lo_ready, 1)

            def rows(col, n):
                return vT[:, col:col + n].unsqueeze(2).to_broadcast([P, n, 2])

            dve.wait_ge(vec_done, 1)
            dve.tensor_copy(vT[:, :], ps[:, 3, 0:NV]).then_inc(vec_done, 1)
            dve.wait_ge(small_in, 16 * 9)
            dve.memset(ring_hi[:, 0, :].bitcast(F32), 0.0)
            link(dve.memset(ring_lo[:, 0, :].bitcast(F32), 0.0))
            spread = lambda ap: ap.rearrange("p (k g c) -> p k g c", k=KD, g=4)[:, :, :, 0:4]
            wg4 = wgate[:, :, :].rearrange("p k (g c) -> p k g c", c=4)
            link(dve.tensor_copy(spread(ring_hi[:, 0, :]), wg4))
            sub_hi(spread(ring_lo[:, 0, :]), wg4, spread(ring_hi[:, 0, :])).then_inc(lo_ready, 1)

            def first_coef():
                dve.wait_ge(ada_used, ADA0)
                link(dve.tensor_tensor(modT[:, 0:ADA0, :], ps[:, 7, 0:2 * ADA0].rearrange("p (a b) -> p a b", b=2),
                                       rows(V_BADA, ADA0), ALU.add))
                dve.scalar_tensor_tensor(out=coefA1[:, :, :], in0=modT[:, 8:16, :], scalar=1.0, in1=rows(V_GPM, KD),
                                         op0=ALU.add, op1=ALU.mult).then_inc(coef1, 1)

            def scale_x(b):
                tiles = slice(b * TB, (b + 1) * TB)
                dve.wait_ge(x_squares, TB * (b + 1))
                dve.tensor_scalar(stat[:, 1, tiles], stat[:, 0, tiles], 1.0 / DM, EPS, ALU.mult, ALU.add).then_inc(x_roots, 1)
                dve.wait_ge(x_roots, 2 * b + 2)
                link(dve.reciprocal(stat[:, 3, tiles], stat[:, 2, tiles]))
                for t in range(b * TB, (b + 1) * TB):
                    dve.tensor_scalar(X0[:, t, :], X0[:, t, :], stat[:, 3, t:t + 1], None, ALU.mult).then_inc(x_scaled, 1)

            for b in range(NB):
                scale_x(b)
            first_coef()

            def norm_split(n0, tile, slots, b, ks=range(KD)):
                for k in ks:
                    w = n0 + b * KD + k
                    dve.wait_ge(xt_free, w + 1)
                    tok = slice(b * BW, (b + 1) * BW)
                    if b == 0 or k % 2 == 0:
                        link(dve.tensor_copy(H_hi[:, k, tok], tile[:, w % slots, :]))
                    sub_hi(H_lo[:, k, tok], tile[:, w % slots, :], H_hi[:, k, tok]).then_inc(h_split_done, 1)

            for b in range(NB):
                norm_split(0, tsc, 4, b)
            dve.wait_ge(consts_in, 32)
            dve.tensor_copy(idbf[:, :], ident[:, :])
            dve.tensor_copy(maskbf[:, :, :], mask32[:, :].rearrange("p (a b) -> p a b", b=P))
            dve.tensor_copy(sel[:, :, :], stage[1][:, 0:8 * P].rearrange("p (a b) -> p a b", b=P))

            def gates():
                dve.memset(Gt[3][0:GR, :], 0.0)
                dve.wait_ge(h_split_done, 24)
                link(dve.memset(Gt[4][0:GR, :], 0.0))
                ada_products(ADA_AT[2])
                dve.wait_ge(log_f_ready, 1)
                li, lf, bb, mm_, gg, aa, yy = (Gt[r][0:GR, :] for r in (0, 1, 3, 4, 5, 6, 7))
                link(dve.scalar_tensor_tensor(out=lf, in0=lf, scalar=0.0, in1=Gt[2][0:GR, :], op0=ALU.min, op1=ALU.subtract))
                fwd, bwd = slice(0, 4), slice(32, 36)
                dve.tensor_tensor_scan(Gt[3][fwd, :], reset[fwd, :], Gt[1][fwd, :], 0.0, ALU.mult, ALU.add)
                dve.tensor_tensor_scan(Gt[3][bwd, :][:, ::-1], reset[bwd, :][:, ::-1], Gt[1][bwd, :][:, ::-1], 0.0,
                                       ALU.mult, ALU.add)
                for rw, dr in ((fwd, 1), (bwd, -1)):
                    for lo, hi, init in ((0, CTX, 0.0), (CTX, T, m0t[rw, :])):
                        a = [Gt[r][rw, lo:hi] if dr == 1 else Gt[r][rw, lo:hi][:, ::-1] for r in (4, 1, 0)]
                        ins = dve.tensor_tensor_scan(a[0], a[1], a[2], init, ALU.add, ALU.max)
                link(ins)
                lo_split(3)
                m3 = Gt[4][0:GR, :].rearrange("p (t s) -> p t s", s=P)
                dve.tensor_copy(mprev[fwd, 1:2], m0t[fwd, :])
                dve.tensor_copy(mprev[bwd, NT - 1:NT], m0t[bwd, :])
                dve.tensor_copy(mprev[fwd, 2:NT], m3[fwd, 1:NT - 1, P - 1])
                dve.tensor_copy(mprev[bwd, 1:NT - 1], m3[bwd, 2:NT, 0])
                dve.tensor_tensor(aa, li, bb, ALU.subtract)
                link(dve.tensor_tensor(gg, bb, mm_, ALU.subtract))
                link(dve.tensor_tensor(yy.rearrange("p (t s) -> p t s", s=P), gg.rearrange("p (t s) -> p t s", s=P),
                                       mprev[0:GR, :].unsqueeze(2).to_broadcast([GR, NT, P]), ALU.add))
                dve.wait_ge(pool_seq, 9)
                dve.tensor_copy(GS[0:GR, :], gg)
                link(dve.tensor_copy(YS[0:GR, :], yy))
                sub_hi(GS[64:64 + GR, :], gg, GS[0:GR, :])
                sub_hi(YS[64:64 + GR, :], yy, YS[0:GR, :]).then_inc(gate_rows_ready, 1)

            def attention_weights(h, i):
                e = h * 9 + i
                tiles = (0, 0) if i == 0 else (i, NT - i)
                v = h % 2
                dve.wait_ge(att_exps, e + 1)
                dve.tensor_tensor(Pt[:, :, :].rearrange("p a b -> p (a b)"), ps[:, 4, 0:256],
                                  Wt[:, :, :].rearrange("p a b -> p (a b)"), ALU.mult)
                if i:
                    for d, cx in enumerate(tiles):
                        dve.tensor_tensor(qs[:, d, :], qT[v][:, cx * P:(cx + 1) * P], Et[:, d, :], ALU.mult)
                for d in range(2):
                    last = (1 - d) * (P - 1)
                    ins = dve.tensor_scalar(k_weighted[:, d, :], ps[:, 4, 256 + d * P:256 + (d + 1) * P], Wt[:, d, last:last + 1], None,
                                            ALU.mult)
                ins.then_inc(att_weights, 1)

            def attention_outputs(h, i, d):
                e = h * 9 + i
                cx = 0 if i == 0 else (i, NT - i)[d]
                hd = hm[h % 2]
                last = (1 - d) * (P - 1)
                dve.wait_ge(att_values, 2 * e + d + 1)
                if i == 0:
                    if h:
                        dve.wait_ge(new_state_stored, 64 * h)
                    dve.tensor_copy(Cctx[:, d, :], ps[:, 7, 0:VW]).then_inc(att_state, 1)
                else:
                    dve.scalar_tensor_tensor(out=Cst[:, d, :], in0=Cst[:, d, :], scalar=Et[:, d, last:last + 1],
                                             in1=ps[:, 7, 0:VW], op0=ALU.mult, op1=ALU.add).then_inc(att_state, 1)
                den, rec = den_rec[:, 2 * d:2 * d + 1], den_rec[:, 2 * d + 1:2 * d + 2]
                link(dve.scalar_tensor_tensor(out=den, in0=ps[:, 5 + d, DV:VW], scalar=-1.0, in1=en_tok[:, cx, d, h:h + 1],
                                              op0=ALU.mult, op1=ALU.max))
                link(dve.tensor_tensor(den, ps[:, 5 + d, DV:VW], den, ALU.max))
                link(dve.reciprocal(rec, den))
                if (i == 0 and d == 0) or 1 <= i <= 4:
                    dve.tensor_scalar(hd[:, cx, :], ps[:, 5 + d, 0:DV], rec, None, ALU.mult).then_inc(att_outputs, 1)
                else:
                    dve.scalar_tensor_tensor(out=hd[:, cx, :], in0=ps[:, 5 + d, 0:DV], scalar=rec, in1=hd[:, cx, :],
                                             op0=ALU.mult, op1=ALU.add).then_inc(att_outputs, 1)

            def ada_products(a):
                n = raw_of[("ada", a)]
                dve.wait_ge(landed[n % RS], 16 * (n // RS + 1))
                dve.wait_ge(ada_used, a)
                for k in range(KD):
                    w = raw[:, n % RS, k * P:(k + 1) * P]
                    for cond in range(2):
                        done = (2 * KD - 1) * (a - ADA0) + 2 * k + cond
                        part = ada_part[:, cond, :]
                        if k == 0:
                            ins = dve.tensor_scalar(part, w, condT[:, cond, k:k + 1], None, ALU.mult)
                        else:
                            dve.wait_ge(ada_mac, done - 1)
                            ins = dve.scalar_tensor_tensor(out=part, in0=w, scalar=condT[:, cond, k:k + 1], in1=part,
                                                           op0=ALU.mult, op1=ALU.add)
                        if k == KD - 1 and cond:
                            ins.then_inc(ada_summed, 1)
                        else:
                            ins.then_inc(ada_mac, 1)

            def gate_branch_b(d):
                if d == 4:
                    dve.wait_ge(evac0, Q_P1)
                if d == 6:
                    for item in staged[-2:]:
                        dve.wait_ge(*store_of[item])
                wb = load_of[("gb", d)] % LS
                dve.wait_ge(sigmoids_done, sigmoids.index(("gb", d)) + 1)
                for b in range(NB):
                    tok = slice(b * BW, (b + 1) * BW)
                    dve.wait_ge(done1, 3 * d + b + 1)
                    dve.tensor_tensor(mixF[:, d, tok], ps[:, 3 + b, 0:BW], tiles[:, wb, tok], ALU.mult).then_inc(evac1, 1)

            lo_split(1)
            for m, (kind, idx) in enumerate(mains):
                seg = m - SEG
                if m == 0:
                    lo_split(2)
                    gates()
                elif m > 1:
                    if m + 1 in ADA_AT:
                        ada_products(ADA_AT[m + 1])
                    lo_split(m + 2)
                if m == SEG - 4:
                    dve.wait_ge(gate_cols_ready, 1)
                    dve.wait_ge(new_m_stored, 32)
                    dve.memset(vaug[0][:, :, DV:VW], 1.0)
                    dve.memset(vaug[1][:, :, DV:VW], 1.0).then_inc(ones_done, 1)
                if m in TURN_AT:
                    h, j = TURN_AT[m]
                    item = ("hm", 2 * h + j)
                    st = stage[stage_no[item] % 2]
                    dve.wait_ge(o_sigmoid, item[1] + 1)
                    dve.wait_ge(evac0, 3 * use_of[item] + 3)
                    dve.scalar_tensor_tensor(out=st[:, :], in0=st[:, :], scalar=vT[:, V_GH + item[1]:V_GH + item[1] + 1],
                                             in1=work[j][:, :], op0=ALU.mult, op1=ALU.mult).then_inc(head_staged, 1)
                if seg >= 0:
                    h, i = seg // 9, seg % 9
                    attention_weights(h, i)
                    attention_outputs(h, i, 0)
                    attention_outputs(h, i, 1)
                    for g in POOL_SPLIT.get(m, ()):
                        dve.wait_ge(pooled_hi_done, g + 1)
                        sub_hi(pT_lo[:, g, :], pF[:, g, :], pT_hi[:, g, :]).then_inc(pooled_lo_done, 1)
                    if m == NM - 1:
                        gate_branch_b(0)
                    if m in NORM_AT:
                        h = NORM_AT[m]
                        dve.wait_ge(head_squares, NT * (h + 1))
                        dve.tensor_scalar(hstat[:, 0, :], hstat[:, 0, :], 1.0 / DV, EPS, ALU.mult, ALU.add).then_inc(head_roots, 1)
                        dve.wait_ge(head_roots, 2 * h + 2)
                        link(dve.reciprocal(hstat[:, 0, :], hstat[:, 1, :]))
                        for t in range(NT):
                            ins = dve.tensor_scalar(hm[h % 2][:, t, :], hm[h % 2][:, t, :], hstat[:, 0, t:t + 1], None, ALU.mult)
                        ins.then_inc(hscaled, 1)

            dve.wait_ge(evac0, 3 * use_of[("main", NM - 1)] + 3)
            dve.scalar_tensor_tensor(out=coefA2[:, :, :], in0=modT[:, 32:40, :], scalar=1.0, in1=rows(V_GPF, KD),
                                     op0=ALU.add, op1=ALU.mult)
            dve.tensor_tensor(coefG1[:, :, :], modT[:, 16:24, :], rows(V_GQM, KD), ALU.mult)
            dve.tensor_tensor(coefG2[:, :, :], modT[:, 40:48, :], rows(V_GQF, KD), ALU.mult).then_inc(coef2, 1)
            for d in range(KD):
                wh = load_of[("hm", d)]
                if d >= HG:
                    wo = load_of[("o", d)]
                    dve.wait_ge(tile_in[wh % LS], 16 * (wh // LS + 1))
                    dve.wait_ge(sigmoids_done, sigmoids.index(("o", d)) + 1)
                    dve.scalar_tensor_tensor(out=tiles[:, wh % LS, :], in0=tiles[:, wh % LS, :],
                                             scalar=vT[:, V_GH + d:V_GH + d + 1], in1=tiles[:, wo % LS, :],
                                             op0=ALU.mult, op1=ALU.mult).then_inc(head_gated, 1)
                lo_split(S_BR + d + 2)
                if d + 1 < KD:
                    gate_branch_b(d + 1)
                dve.wait_ge(head_hi_done, d + 1)
                sub_hi(H_lo[:, d, :], tiles[:, wh % LS, :], H_hi[:, d, :]).then_inc(tile_used, 1)
            for d in range(KD):
                for s in SPLIT_AT[d]:
                    lo_split(s)
                wa = load_of[("ga", d)] % LS
                dve.wait_ge(sigmoids_done, sigmoids.index(("ga", d)) + 1)
                for b in range(NB):
                    tok = slice(b * BW, (b + 1) * BW)
                    q = 3 * (U_YA + d) + b + 1
                    dve.wait_ge(done0, q)
                    dve.tensor_tensor(tiles[:, wa, tok], ps[:, b, 0:BW], tiles[:, wa, tok], ALU.mult).then_inc(evac0, 1)
                    dve.wait_ge(evac0, q)
                    ins = dve.tensor_tensor(mixF[:, d, tok], tiles[:, wa, tok], mixF[:, d, tok], ALU.add)
                    if d == KD - 1:
                        ins.then_inc(mix_sum, 1)
                        for k in range(KD):
                            dve.wait_ge(mix_hi_done, b * KD + k + 1)
                            ins = sub_hi(H_lo[:, k, tok], mixF[:, k, tok], H_hi[:, k, tok])
                            ins.then_inc(mix_ready, 1)
                if d < KD - 1:
                    ins.then_inc(tile_used, 1)
            lo_split(S_OUT + 7)
            for t in range(NT):
                if t == NT - 1:
                    lo_split(S_FF)
                    lo_split(S_FF + 1)
                cond = 0 if t == 0 else 1
                pair = ps[:, out_bank(t):out_bank(t) + 2, :].rearrange("p a b -> p (a b)")
                if t < 2:
                    dve.wait_ge(gate_bcast_copied, t + 1)
                dve.wait_ge(norm_squares, 2 * t + 1)
                dve.tensor_scalar(stat[:, 1, t:t + 1], stat[:, 0, t:t + 1], 1.0 / DM, EPS, ALU.mult, ALU.add).then_inc(norm_means, 1)
                dve.wait_ge(norm_roots, 2 * t + 1)
                link(dve.reciprocal(stat[:, 0, t:t + 1], stat[:, 2, t:t + 1]))
                dve.scalar_tensor_tensor(out=X1[:, t, :], in0=pair, scalar=stat[:, 0, t:t + 1], in1=gtb1[:, cond, :],
                                         op0=ALU.mult, op1=ALU.mult).then_inc(evac2, 1)
                dve.wait_ge(evac2, t + 1)
                dve.wait_ge(x_in[t % 2], 16 * (t // 2 + 1))
                dve.tensor_tensor(xld[:, t % 2, :], X1[:, t, :], xld[:, t % 2, :], ALU.add).then_inc(x1_ready, 1)
                if t - 1 in NORM_AFTER:
                    norm_split(NB * KD, tsc2, 2, (t - 1) // TB, range(0, 3))
                dve.wait_ge(norm_squares, 2 * t + 2)
                dve.tensor_scalar(hstat[:, 0, t:t + 1], stat[:, 3, t:t + 1], 1.0 / DM, EPS, ALU.mult, ALU.add).then_inc(norm_means, 1)
                dve.wait_ge(norm_roots, 2 * t + 2)
                link(dve.reciprocal(stat[:, 3, t:t + 1], hstat[:, 1, t:t + 1]))
                dve.tensor_scalar(X1[:, t, :], xld[:, t % 2, :], stat[:, 3, t:t + 1], None, ALU.mult).then_inc(x_scaled, 1)
                if t - 1 in NORM_AFTER:
                    norm_split(NB * KD, tsc2, 2, (t - 1) // TB, range(3, KD))
            norm_split(NB * KD, tsc2, 2, NB - 1)

            def ff_up_dve(f, e, slot, splits, i, before_last=None):
                n = [12 * f]

                def step(ins):
                    n[0] += 1
                    ins.then_inc(dve_conv, 1)

                def settle():
                    dve.wait_ge(dve_conv, lin(n[0], 48, i))

                for half in range(2):
                    for j in splits[half]:
                        ff_lo(j, i)
                    tile = conv_v if half else conv_g
                    for b in range(NB):
                        dve.wait_ge(conv_middle, lin(6 * f + 3 * half + b + 1, 24, i))

                        def tap(lo, nr, ln, shift):
                            out = tile[:, b * BW + lo:b * BW + lo + nr * ln].rearrange("p (r c) -> p r c", c=ln)
                            src = ps[:, b + 3 * half, lo:lo + nr * ln].rearrange("p (r c) -> p r c", c=ln)
                            if shift < 0:
                                out, src, w = out[:, :, 1:ln], src[:, :, 0:ln - 1], V_W0
                            else:
                                out, src, w = out[:, :, 0:ln - 1], src[:, :, 1:ln], V_W2
                            return dve.scalar_tensor_tensor(out=out, in0=src, scalar=vcol(w + NF * half + f, i), in1=out,
                                                            op0=ALU.mult, op1=ALU.add)

                        parts = row_parts(b)
                        for pt in parts:
                            step(tap(*pt, -1))
                        settle()
                        tok = slice(b * BW, (b + 1) * BW)
                        if half == 0:
                            for pt in parts:
                                ins = tap(*pt, 1)
                            ins.then_inc(conv_gate_done, 1)
                        else:
                            for pt in parts:
                                step(tap(*pt, 1))
                            settle()
                            dve.wait_ge(gelu_done, lin(3 * f + b + 1, 12, i))
                            dve.tensor_tensor(conv_v[:, tok], conv_g[:, tok], conv_v[:, tok], ALU.mult).then_inc(conv_value_done, 1)
                            if before_last and b == NB - 1:
                                before_last()
                            dve.wait_ge(feature_hi_done, lin(3 * f + b + 1, 12, i))
                            sub_hi(fT_lo[:, slot, e, tok], conv_v[:, tok], fT_hi[:, slot, e, tok]).then_inc(features_ready, 1)
                assert n[0] == 12 * (f + 1)

            def add_halves(ch, t, i):
                for hb in range(2):
                    dve.wait_ge(done2, lin(NT + 18 * ch + 2 * t + hb + 1, 36, i))
                    cols = slice(hb * 512, (hb + 1) * 512)
                    dve.tensor_tensor(acc[:, t, cols], ps[:, 6 + hb, :], acc[:, t, cols], ALU.add).then_inc(evac2, 1)

            ff_up_dve(0, 0, 0, [[2], [3]], None)
            ff_up_dve(1, 1, 0, [[4], []], None)
            dve.wait_ge(acc_zero, 1)
            with dve.Fori(0, (NC - 1) // 2) as i:
                for cc in range(2):
                    j = 4 + 6 * cc
                    ff_up_dve(2 + 2 * cc, 0, 1 - cc, [[j + 1, j + 2], [j + 3]], i)
                    ff_up_dve(3 + 2 * cc, 1, 1 - cc, [[j + 4], [j + 5]], i, lambda: add_halves(cc, 0, i))
                    for t in range(1, NT):
                        add_halves(cc, t, i)
                        if t == 2:
                            ff_lo(j + 6, i)
            ff_lo(5 + 6 * (NC - 1), None)

            def finish(t):
                dve.wait_ge(final_roots, 2 * t + 1)
                dve.tensor_scalar(stat[:, 1, t:t + 1], stat[:, 0, t:t + 1], 1.0 / DM, EPS, ALU.mult, ALU.add).then_inc(final_means, 1)
                dve.wait_ge(final_roots, 2 * t + 2)
                link(dve.reciprocal(stat[:, 3, t:t + 1], stat[:, 2, t:t + 1]))
                dve.scalar_tensor_tensor(out=acc[:, t, :], in0=acc[:, t, :], scalar=stat[:, 3, t:t + 1],
                                         in1=gtb2[:, 0 if t == 0 else 1, :], op0=ALU.mult, op1=ALU.mult).then_inc(final_gated, 1)
                if t == NT - 1:
                    dve.wait_ge(final_gated, NT)
                    dve.wait_ge(final_done, NT - 1)
                    dve.wait_ge(x1_in[t % 2], 16 * (t // 2 + 1))
                    dve.tensor_tensor(acc[:, t, :], acc[:, t, :], x1ld[:, t % 2, :], ALU.add).then_inc(final_done, 1)

            dve.wait_ge(gate_bcast_copied, 4)
            for t in range(NT):
                add_halves(NC - 1, t, None)
                if t:
                    finish(t - 1)
            finish(NT - 1)


_INS = ['x_prompt', 'x_sample', 'state_C', 'state_n', 'state_m', 'c', 'c_ctx', 'w_ada', 'b_ada', 'g_pre_mix',
        'g_post_mix', 'g_pre_ffn', 'g_post_ffn', 'w_in', 'b_gates', 'g_head', 'w_pool', 'pool_scale', 'w_br_a',
        'w_br_b', 'w_out', 'w_up', 'conv_w', 'conv_b', 'w_down']
_OUTS = [(1, 128, 1024), (1, 1024, 1024), (1, 1, 2, 4, 128, 256), (1, 1, 2, 4, 128), (1, 1, 2, 4)]


def kernel(**inputs):
    import concourse.bacc as _bacc
    from concourse.bass_utils import run_bass_kernel_spmd as _run

    nc = _bacc.Bacc("TRN2", target_bir_lowering=False, num_devices=1)
    arrays, args = {}, []
    for name in _INS:
        a = np.ascontiguousarray(inputs[name])
        arrays[f"in_{name}_dram"] = a
        args.append(nc.dram_tensor(f"in_{name}_dram", a.shape, mybir.dt.from_np(a.dtype), kind="ExternalInput").ap())
    arrays["in_consts_dram"] = shape_constants()
    args.append(nc.dram_tensor("in_consts_dram", (P, H_COLS), F32, kind="ExternalInput").ap())
    for i, shape in enumerate(_OUTS):
        args.append(nc.dram_tensor(f"out_{i}_dram", shape, F32, kind="ExternalOutput").ap())
    build(nc, *args)
    r = _run(nc, [arrays], core_ids=[0])
    return tuple(r.results[0][f"out_{i}_dram"] for i in range(len(_OUTS)))
```
